# Optimizing a Trainium2 kernel written in Bass

```python
import math
import jax, jax.numpy as jnp
from jax import lax
import numpy as np

D_MODEL = 1024
BATCH = 1
SEQ = 512
DEPTH = 1
DEC_BATCH = 8
DEC_SEQ = 1
PAST_LEN = 512
PAGE_SIZE = 128

HEAD_DIM = 64
HEADS_PER_GROUP = 4
DIL_GROUPS = ((128, 1), (512, 4), (2048, 16))
N_ATT_GROUPS = len(DIL_GROUPS)
ATT_WIDTH = N_ATT_GROUPS * HEADS_PER_GROUP * HEAD_DIM
ATT_OUT = HEADS_PER_GROUP * HEAD_DIM
QBLOCK = 128
POOL_WINDOWS = (2, 4, 8, 16)
N_POOL_GROUPS = len(POOL_WINDOWS)
POOL_WIDTH = D_MODEL // 2
POOL_GROUP = POOL_WIDTH // N_POOL_GROUPS
POOL_BUF = max(POOL_WINDOWS) - 1
SSM_WIDTH = D_MODEL // 2
SSM_GROUP_CH = 16
SSM_GROUPS = SSM_WIDTH // SSM_GROUP_CH
SSM_STATE = 64
N_BRANCH = 3
IN_COLS = 3 * ATT_WIDTH + POOL_WIDTH + SSM_WIDTH + N_BRANCH * D_MODEL
SPLIT_POINTS = (ATT_WIDTH, 2 * ATT_WIDTH, 3 * ATT_WIDTH,
                3 * ATT_WIDTH + POOL_WIDTH, 3 * ATT_WIDTH + POOL_WIDTH + SSM_WIDTH)
D_FF = ((8 * D_MODEL + 3 * 256 - 1) // (3 * 256)) * 256
ALPHA = (2 * DEPTH) ** 0.25
BETA = (8 * DEPTH) ** -0.25
LN_EPS = 1e-5

kernel_name = 'hybrid_dilated_pool_s5_decoder_step'

F32 = jnp.float32

def layer_norm(x, g, b):
    xf = x.astype(F32)
    mu = jnp.mean(xf, axis=-1, keepdims=True)
    var = jnp.mean(jnp.square(xf - mu), axis=-1, keepdims=True)
    return ((xf - mu) * lax.rsqrt(var + LN_EPS) * g.astype(F32) + b.astype(F32)).astype(x.dtype)

def alibi_slopes():
    n = N_ATT_GROUPS * HEADS_PER_GROUP
    s = 2.0 ** (-8.0 * jnp.arange(1, n + 1, dtype=F32) / n)
    return s.reshape(N_ATT_GROUPS, HEADS_PER_GROUP)

def dilated_attn_prompt(q, k, v, dilation, n_back, slopes):
    B, L, H, E = q.shape
    lsub = L // dilation
    qb = min(QBLOCK, lsub)
    nblk = -(-lsub // qb)
    lpad = nblk * qb
    nk = qb + n_back

    def residues(t):
        return t.reshape(B, lsub, dilation, H, E).transpose(0, 2, 1, 3, 4)

    qs = jnp.pad(residues(q), ((0, 0), (0, 0), (0, lpad - lsub), (0, 0), (0, 0)))
    qs = qs.reshape(B, dilation, nblk, qb, H, E)
    pad_kv = ((0, 0), (0, 0), (n_back, lpad - lsub), (0, 0), (0, 0))
    ks = jnp.pad(residues(k), pad_kv)
    vs = jnp.pad(residues(v), pad_kv)
    kidx = jnp.arange(nblk)[:, None] * qb + jnp.arange(nk)[None, :]
    kb = ks[:, :, kidx]
    vb = vs[:, :, kidx]
    s = jnp.einsum('bdnqhe,bdnkhe->bdnhqk', qs.astype(F32), kb.astype(F32)) * (E ** -0.5)
    jd = jnp.arange(qb)[:, None] - jnp.arange(nk)[None, :] + n_back
    key_row = kidx - n_back
    valid = (jd >= 0) & (jd <= n_back) & (key_row[:, None, :] >= 0)
    bias = -slopes.astype(F32)[:, None, None] * (jd * dilation).astype(F32)
    s = jnp.where(valid[:, None], s + bias, -jnp.inf)
    lse = jax.nn.logsumexp(s, axis=-1)
    p = jnp.exp(s - lse[..., None])
    o = jnp.einsum('bdnhqk,bdnkhe->bdnqhe', p, vb.astype(F32))
    o = o.reshape(B, dilation, lpad, H, E)[:, :, :lsub]
    o = o.transpose(0, 2, 1, 3, 4).reshape(B, L, H, E)
    lse = lse.transpose(0, 1, 2, 4, 3).reshape(B, dilation, lpad, H)[:, :, :lsub]
    lse = lse.transpose(0, 2, 1, 3).reshape(B, L, H)
    return o, lse

def dilated_attn_decode(q, k_all, v_all, dilation, n_back, slopes):
    S = q.shape[1]
    lb = k_all.shape[1] - S
    j = jnp.arange(n_back + 1)
    idx = lb + jnp.arange(S)[:, None] - j[None, :] * dilation
    valid = idx >= 0
    idxc = jnp.maximum(idx, 0)
    kg = k_all[:, idxc].astype(F32)
    vg = v_all[:, idxc].astype(F32)
    s = jnp.einsum('bshe,bsjhe->bhsj', q.astype(F32), kg) * (q.shape[-1] ** -0.5)
    s = s - slopes.astype(F32)[None, :, None, None] * (j * dilation).astype(F32)[None, None, None, :]
    s = jnp.where(valid[None, None], s, -jnp.inf)
    lse = jax.nn.logsumexp(s, axis=-1)
    p = jnp.exp(s - lse[..., None])
    o = jnp.einsum('bhsj,bsjhe->bshe', p, vg)
    return o, lse.transpose(0, 2, 1)

def combine_groups(outs, lses):
    o = jnp.stack(outs, axis=0)
    w = jax.nn.softmax(jnp.stack(lses, axis=0), axis=0)
    o = jnp.sum(w[..., None] * o, axis=0)
    B, L = o.shape[:2]
    return o.reshape(B, L, ATT_OUT)

def pool_mix(u, buf, pos0, w_pool, scale):
    B, L, C = u.shape
    nb = buf.shape[1]
    uf = u.astype(F32)
    ext = jnp.concatenate([buf.astype(F32), uf], axis=1)
    cs = jnp.concatenate([jnp.zeros((B, 1, C), F32), jnp.cumsum(ext, axis=1)], axis=1)
    end = nb + 1 + jnp.arange(L)
    n_real = pos0 + 1 + jnp.arange(L)
    means = []
    for g, w in enumerate(POOL_WINDOWS):
        csg = cs[:, :, g * POOL_GROUP:(g + 1) * POOL_GROUP]
        tot = csg[:, end] - csg[:, end - w]
        cnt = jnp.minimum(n_real, w).astype(F32)
        means.append(tot / cnt[None, :, None])
    diff = (jnp.concatenate(means, axis=-1) - uf).reshape(B, L, N_POOL_GROUPS, POOL_GROUP)
    y = jnp.einsum('blgc,gce->blge', diff, w_pool.astype(F32)).reshape(B, L, POOL_WIDTH)
    return y * scale.astype(F32)

def s5_mix(u, h0_re, h0_im, lam_re, lam_im, b_re, b_im, c_re, c_im, d_skip, log_step, w_glu):
    B, L, _ = u.shape
    lam = lax.complex(lam_re.astype(F32), lam_im.astype(F32))
    step = jnp.exp(log_step.astype(F32))[:, None]
    lam_bar = jnp.exp(lam * step)
    bmat = lax.complex(b_re.astype(F32), b_im.astype(F32))
    b_bar = ((lam_bar - 1.0) / lam)[..., None] * bmat
    uf = u.astype(F32)
    ug = uf.reshape(B, L, SSM_GROUPS, SSM_GROUP_CH)
    bu = jnp.einsum('gph,blgh->blgp', b_bar, ug.astype(jnp.complex64))
    a = jnp.broadcast_to(lam_bar, bu.shape)

    def combine(e1, e2):
        a1, b1 = e1
        a2, b2 = e2
        return a1 * a2, a2 * b1 + b2

    a_cum, b_cum = lax.associative_scan(combine, (a, bu), axis=1)
    h0 = lax.complex(h0_re.astype(F32), h0_im.astype(F32))
    h = a_cum * h0[:, None] + b_cum
    cmat = lax.complex(c_re.astype(F32), c_im.astype(F32))
    y = jnp.real(jnp.einsum('ghp,blgp->blgh', cmat, h)).reshape(B, L, SSM_WIDTH)
    y = jax.nn.gelu(y + d_skip.astype(F32) * uf)
    y = y * jax.nn.sigmoid(y @ w_glu.astype(F32))
    h_last = h[:, -1]
    return y, jnp.real(h_last), jnp.imag(h_last)

def trunk_layer(x, pos0, kv_cache, pool_buf, h0_re, h0_im, p):
    B, L, _ = x.shape
    proj = x @ p['w_in']
    q, k, v, u_pool, u_ssm, g_logits = jnp.split(proj, SPLIT_POINTS, axis=-1)
    hshape = (B, L, N_ATT_GROUPS, HEADS_PER_GROUP, HEAD_DIM)
    q, k, v = q.reshape(hshape), k.reshape(hshape), v.reshape(hshape)
    slopes = alibi_slopes()
    outs, lses, new_state = [], [], []
    for g, (window, dil) in enumerate(DIL_GROUPS):
        n_back = window // dil
        qg, kg, vg = q[:, :, g], k[:, :, g], v[:, :, g]
        if kv_cache is None:
            o, lse = dilated_attn_prompt(qg, kg, vg, dil, n_back, slopes[g])
            keep = min(window, L)
            new_state += [kg[:, L - keep:], vg[:, L - keep:]]
        else:
            k_all = jnp.concatenate([kv_cache[2 * g].astype(kg.dtype), kg], axis=1)
            v_all = jnp.concatenate([kv_cache[2 * g + 1].astype(vg.dtype), vg], axis=1)
            o, lse = dilated_attn_decode(qg, k_all, v_all, dil, n_back, slopes[g])
            new_state += [kg, vg]
        outs.append(o)
        lses.append(lse)
    y_att = combine_groups(outs, lses)

    y_pool = pool_mix(u_pool, pool_buf, pos0, p['pool_w'], p['pool_scale'])
    new_state.append(u_pool[:, L - min(POOL_BUF, L):] if kv_cache is None else u_pool)

    y_ssm, h_re, h_im = s5_mix(u_ssm, h0_re, h0_im, p['ssm_lambda_re'], p['ssm_lambda_im'],
                               p['ssm_b_re'], p['ssm_b_im'], p['ssm_c_re'], p['ssm_c_im'],
                               p['ssm_d'], p['ssm_log_step'], p['ssm_w_glu'])
    new_state += [h_re, h_im]

    gates = jax.nn.sigmoid(g_logits.astype(F32)).reshape(B, L, N_BRANCH, D_MODEL)
    merged = (gates[:, :, 0] * (y_att @ p['w_br_att'].astype(F32))
              + gates[:, :, 1] * (y_pool @ p['w_br_pool'].astype(F32))
              + gates[:, :, 2] * (y_ssm @ p['w_br_ssm'].astype(F32)))
    mix = (merged @ p['w_out'].astype(F32)).astype(x.dtype)
    x = layer_norm(ALPHA * x + mix, p['ln1_g'], p['ln1_b'])
    f = (jax.nn.silu(x @ p['ffn_w_gate']) * (x @ p['ffn_w_up'])) @ p['ffn_w_down']
    x = layer_norm(ALPHA * x + f, p['ln2_g'], p['ln2_b'])
    return x, new_state

def setup_inputs(seed: int = 0) -> dict:
    key = jax.random.key(seed)
    ks = iter(jax.random.split(key, 40))

    def nrm(shape, scale):
        return scale * jax.random.normal(next(ks), shape, F32)

    hd = (HEADS_PER_GROUP, HEAD_DIM)
    lb128, lb512, lb2048 = (min(w, PAST_LEN) for w, _ in DIL_GROUPS)
    lam_im0 = math.pi * jnp.arange(SSM_STATE, dtype=F32)
    inp = {}
    inp['x_prompt'] = nrm((BATCH, SEQ, D_MODEL), 1.0)
    inp['x_sample'] = nrm((DEC_BATCH, DEC_SEQ, D_MODEL), 1.0)
    inp['cache_k_w128'] = nrm((DEPTH, DEC_BATCH, lb128) + hd, 1.0)
    inp['cache_v_w128'] = nrm((DEPTH, DEC_BATCH, lb128) + hd, 1.0)
    inp['cache_k_w512'] = nrm((DEPTH, DEC_BATCH, lb512) + hd, 1.0)
    inp['cache_v_w512'] = nrm((DEPTH, DEC_BATCH, lb512) + hd, 1.0)
    inp['cache_k_w2048'] = nrm((DEPTH, DEC_BATCH, lb2048) + hd, 1.0)
    inp['cache_v_w2048'] = nrm((DEPTH, DEC_BATCH, lb2048) + hd, 1.0)
    inp['state_pool'] = nrm((DEPTH, DEC_BATCH, POOL_BUF, POOL_WIDTH), 1.0)
    inp['state_ssm_re'] = nrm((DEPTH, DEC_BATCH, SSM_GROUPS, SSM_STATE), 0.5)
    inp['state_ssm_im'] = nrm((DEPTH, DEC_BATCH, SSM_GROUPS, SSM_STATE), 0.5)
    inp['w_in'] = nrm((DEPTH, D_MODEL, IN_COLS), D_MODEL ** -0.5)
    inp['pool_w'] = nrm((DEPTH, N_POOL_GROUPS, POOL_GROUP, POOL_GROUP), POOL_GROUP ** -0.5)
    inp['pool_scale'] = 1.0 + nrm((DEPTH, POOL_WIDTH), 0.02)
    inp['ssm_lambda_re'] = -0.5 + nrm((DEPTH, SSM_GROUPS, SSM_STATE), 0.01)
    inp['ssm_lambda_im'] = lam_im0 + nrm((DEPTH, SSM_GROUPS, SSM_STATE), 0.01)
    inp['ssm_b_re'] = nrm((DEPTH, SSM_GROUPS, SSM_STATE, SSM_GROUP_CH), (2 * SSM_GROUP_CH) ** -0.5)
    inp['ssm_b_im'] = nrm((DEPTH, SSM_GROUPS, SSM_STATE, SSM_GROUP_CH), (2 * SSM_GROUP_CH) ** -0.5)
    inp['ssm_c_re'] = nrm((DEPTH, SSM_GROUPS, SSM_GROUP_CH, SSM_STATE), (2 * SSM_STATE) ** -0.5)
    inp['ssm_c_im'] = nrm((DEPTH, SSM_GROUPS, SSM_GROUP_CH, SSM_STATE), (2 * SSM_STATE) ** -0.5)
    inp['ssm_d'] = nrm((DEPTH, SSM_WIDTH), 1.0)
    inp['ssm_log_step'] = jax.random.uniform(next(ks), (DEPTH, SSM_GROUPS), F32,
                                             math.log(0.001), math.log(0.1))
    inp['ssm_w_glu'] = nrm((DEPTH, SSM_WIDTH, SSM_WIDTH), SSM_WIDTH ** -0.5)
    inp['w_br_att'] = nrm((DEPTH, ATT_OUT, D_MODEL), ATT_OUT ** -0.5)
    inp['w_br_pool'] = nrm((DEPTH, POOL_WIDTH, D_MODEL), POOL_WIDTH ** -0.5)
    inp['w_br_ssm'] = nrm((DEPTH, SSM_WIDTH, D_MODEL), SSM_WIDTH ** -0.5)
    inp['w_out'] = nrm((DEPTH, D_MODEL, D_MODEL), BETA * D_MODEL ** -0.5)
    inp['ln1_g'] = 1.0 + nrm((DEPTH, D_MODEL), 0.02)
    inp['ln1_b'] = nrm((DEPTH, D_MODEL), 0.02)
    inp['ffn_w_gate'] = nrm((DEPTH, D_MODEL, D_FF), D_MODEL ** -0.5)
    inp['ffn_w_up'] = nrm((DEPTH, D_MODEL, D_FF), D_MODEL ** -0.5)
    inp['ffn_w_down'] = nrm((DEPTH, D_FF, D_MODEL), BETA * D_FF ** -0.5)
    inp['ln2_g'] = 1.0 + nrm((DEPTH, D_MODEL), 0.02)
    inp['ln2_b'] = nrm((DEPTH, D_MODEL), 0.02)
    return inp

def reference(x_prompt, x_sample, cache_k_w128, cache_v_w128, cache_k_w512, cache_v_w512,
              cache_k_w2048, cache_v_w2048, state_pool, state_ssm_re, state_ssm_im,
              w_in, pool_w, pool_scale, ssm_lambda_re, ssm_lambda_im, ssm_b_re, ssm_b_im,
              ssm_c_re, ssm_c_im, ssm_d, ssm_log_step, ssm_w_glu, w_br_att, w_br_pool,
              w_br_ssm, w_out, ln1_g, ln1_b, ffn_w_gate, ffn_w_up, ffn_w_down, ln2_g, ln2_b):
    yp, ys = x_prompt, x_sample
    st_p = [[] for _ in range(9)]
    st_s = [[] for _ in range(9)]
    zero_pool = jnp.zeros((x_prompt.shape[0], POOL_BUF, POOL_WIDTH), x_prompt.dtype)
    zero_h = jnp.zeros((x_prompt.shape[0], SSM_GROUPS, SSM_STATE), F32)
    for l in range(DEPTH):
        p = dict(w_in=w_in[l], pool_w=pool_w[l], pool_scale=pool_scale[l],
                 ssm_lambda_re=ssm_lambda_re[l], ssm_lambda_im=ssm_lambda_im[l],
                 ssm_b_re=ssm_b_re[l], ssm_b_im=ssm_b_im[l], ssm_c_re=ssm_c_re[l],
                 ssm_c_im=ssm_c_im[l], ssm_d=ssm_d[l], ssm_log_step=ssm_log_step[l],
                 ssm_w_glu=ssm_w_glu[l], w_br_att=w_br_att[l], w_br_pool=w_br_pool[l],
                 w_br_ssm=w_br_ssm[l], w_out=w_out[l], ln1_g=ln1_g[l], ln1_b=ln1_b[l],
                 ffn_w_gate=ffn_w_gate[l], ffn_w_up=ffn_w_up[l], ffn_w_down=ffn_w_down[l],
                 ln2_g=ln2_g[l], ln2_b=ln2_b[l])
        yp, new_p = trunk_layer(yp, 0, None, zero_pool, zero_h, zero_h, p)
        kv = [cache_k_w128[l], cache_v_w128[l], cache_k_w512[l], cache_v_w512[l],
              cache_k_w2048[l], cache_v_w2048[l]]
        ys, new_s = trunk_layer(ys, PAST_LEN, kv, state_pool[l], state_ssm_re[l],
                                state_ssm_im[l], p)
        for i in range(9):
            st_p[i].append(new_p[i])
            st_s[i].append(new_s[i])
    (k128_p, v128_p, k512_p, v512_p, k2048_p, v2048_p,
     pool_p, ssm_re_p, ssm_im_p) = [jnp.stack(s, axis=0) for s in st_p]
    (k128_s, v128_s, k512_s, v512_s, k2048_s, v2048_s,
     pool_s, ssm_re_s, ssm_im_s) = [jnp.stack(s, axis=0) for s in st_s]
    return (yp, ys,
            k128_p, v128_p, k512_p, v512_p, k2048_p, v2048_p, pool_p, ssm_re_p, ssm_im_p,
            k128_s, v128_s, k512_s, v512_s, k2048_s, v2048_s, pool_s, ssm_re_s, ssm_im_s)


_drawn_inputs = setup_inputs


def setup_inputs(seed=0):
    import zlib

    import numpy as np

    out = dict(_drawn_inputs(seed))
    spreads = {}
    factors = {'pool_scale': 8.0,
     'ssm_lambda_re': 17.485,
     'ln1_g': 2.99,
     'ln2_g': 7.444,
     'ln2_b': 7.722,
     'cache_k_w128': 4.248,
     'cache_v_w128': 2.87,
     'cache_k_w512': 3.977,
     'cache_v_w512': 3.064,
     'cache_k_w2048': 2.748,
     'ssm_c_re': 3.15,
     'ssm_c_im': 3.042,
     'ssm_w_glu': 3.279,
     'ln1_b': 6.581}
    for name, (base, spread) in spreads.items():
        noise = np.random.default_rng([zlib.crc32(name.encode()), seed]).standard_normal(out[name].shape)
        drawn = base * np.exp(spread * noise) if base else spread * noise
        out[name] = __import__('jax').numpy.asarray(drawn.astype(out[name].dtype))
    for name, factor in factors.items():
        out[name] = (out[name] * factor).astype(out[name].dtype)
    return out
```

```python
import math
from contextlib import ExitStack

import numpy as np

import concourse.bass as bass
from concourse import mybir

F32 = mybir.dt.float32
F32R = mybir.dt.float32r
I32 = mybir.dt.int32
ALU = mybir.AluOpType
ACT = mybir.ActivationFunctionType
AX = mybir.AxisListType

P = 128
D = 1024
SEQ, DEC = 512, 8
T = SEQ + DEC
HALF = T // 2
KD = D // P
FF = 2816
KF = FF // P
ATT = 768
N_GROUPS, HEADS, E = 3, 4, 64
WINDOWS = (128, 512, 2048)
DILATION = (1, 4, 16)
PAST = 512
BACK = 128
POOL_W = (2, 4, 8, 16)
PBUF = 15
COL_K, COL_V, COL_POOL, COL_SSM, COL_GATE = 768, 1536, 2304, 2816, 3328
NT = SEQ // P
CH = 8
NC = SEQ // CH
ALPHA = 2.0 ** 0.25
EPS = 1e-5
BIG = 1e30
ROUND = 1.5 * 2.0 ** 23
SLOPE = [[2.0 ** (-8.0 * (4 * g + h + 1) / 12) for h in range(HEADS)] for g in range(N_GROUPS)]

PAN_SSM, PAN_POOL, PAN_POOLBR, PAN_QKV = 0, 4, 8, 24
PAN_GLU, PAN_SSMBR, PAN_ATTBR, PAN_OUT = 42, 46, 62, 78
PAN_FF, PAN_DOWN, PAN_END = 86, 130, 162
DOWN_K = (6, 6, 5, 5)
RAW, RING = 2, 4
SP_LAG = 8
LOOK = 3


def panel_blocks(p):
    if PAN_POOLBR <= p < PAN_QKV or PAN_SSMBR <= p < PAN_ATTBR:
        return 8 if p % 2 == 0 else 4
    if PAN_GLU <= p < PAN_SSMBR:
        return 4
    if PAN_ATTBR <= p < PAN_OUT:
        return 8 if p % 2 == 0 else 2
    if p >= PAN_DOWN:
        return DOWN_K[(p - PAN_DOWN) % 4]
    return 8


def qkv_panel(p):
    n = p - PAN_QKV
    return (n % 9) // 3, n % 3, n // 9


AFTER = {
    1: ["turn_params", "params", ("powers", 0)], 5: [("ssm_prep", 0)], 6: [("powers", 1)],
    7: [("ssm_in", 0), "pool_diff", "pool_mix"],
    8: [("ssm_prep", 1)], 9: [("ssm_out", 0), ("powers", 2)], 11: [("ssm_in", 1)], 12: [("ssm_prep", 2)],
    13: [("ssm_out", 1), ("powers", 3), ("gelu", 0)], 15: [("ssm_in", 2)], 16: [("ssm_prep", 3)],
    17: [("ssm_out", 2), ("gelu", 1)], 19: [("ssm_in", 3)], 21: [("ssm_out", 3), ("gelu", 2)],
    22: [("gelu", 3), "gelu_split"],
    32: [("to_tokens", 0)],
    41: [("to_tokens", 1), "decode_q", "decode_k", "decode_v", "decode_scores", "decode_softmax", "decode_out", "bias"],
}
ATT_STEPS = [(h, i) for h in range(HEADS) for i in reversed(range(NT))]
for n in range(len(ATT_STEPS) + 1):
    at = PAN_GLU + n
    todo = AFTER.setdefault(at, [])
    if n < len(ATT_STEPS):
        todo.append(("scores", n))
    if n >= 1:
        todo.append(("probs", n - 1))


def build(nc, ins, outs):
    (x_prompt, x_sample, ck128, cv128, ck512, cv512, ck2048, cv2048, state_pool, ssm_re, ssm_im, w_in, pool_w,
     pool_scale, lam_re, lam_im, b_re, b_im, c_re, c_im, ssm_d, log_step, w_glu, w_br_att, w_br_pool,
     w_br_ssm, w_out, ln1_g, ln1_b, w_gate, w_up, w_down, ln2_g, ln2_b) = ins
    (y_p, y_s, k128_p, v128_p, k512_p, v512_p, k2048_p, v2048_p, pool_p, ssmre_p, ssmim_p,
     k128_s, v128_s, k512_s, v512_s, k2048_s, v2048_s, pool_s, ssmre_s, ssmim_s) = outs
    cache_k, cache_v = (ck128, ck512, ck2048), (cv128, cv512, cv2048)
    kp, vp = (k128_p, k512_p, k2048_p), (v128_p, v512_p, v2048_p)
    ks, vs = (k128_s, k512_s, k2048_s), (v128_s, v512_s, v2048_s)

    ctx = ExitStack()
    with ctx:
        ctx.enter_context(nc.allow_non_contiguous_dma(reason="per-feature vectors: one element per partition"))
        place = [((nc.sbuf_base + 31) // 32) * 32]

        def at(name, shape, dt, offset=None):
            size = 4 * int(np.prod(shape[1:]))
            where = place[0] if offset is None else offset
            if offset is None:
                place[0] += (size + 31) // 32 * 32
            return nc.alloc_sbuf_tensor_at(name, shape, dt, offset=where)

        def region(size):
            where = place[0]
            place[0] += (size + 31) // 32 * 32
            return where

        raw = at("raw", [P, RAW, 1024], F32)
        w_hi = at("w_hi", [P, RING, 1024], F32R)
        w_lo = at("w_lo", [P, RING, 1024], F32R)
        x_hi = at("x_hi", [P, KD, T], F32R)
        x_lo = at("x_lo", [P, KD, T], F32R)
        r_z = region(4 * KD * T)
        z = at("z", [P, KD, T], F32, r_z)
        tg = at("tg", [P, 2, T], F32)
        tw = at("tw", [P, 2, T], F32)
        ident = at("ident", [P, P], F32)
        ones = at("ones", [P, P], F32)
        vecs = at("vecs", [P, 48], F32)
        rcnt = at("rcnt", [P, 4, 16], F32)
        wsel = at("wsel", [P, 4, DEC], F32)
        hmask = at("hmask", [32, 4, E], F32)
        sc32 = at("sc32", [32, 3 * P], F32)
        dist32 = at("dist32", [32, 3 * P], F32)
        small = at("small", [P, 64], F32)
        pt32 = at("pt32", [P, 3, 32], F32)
        diag32 = at("diag32", [32, 3, 32], F32)
        s32 = at("s32", [P, 3, 32], F32)
        stage_dec = at("stage_dec", [32, 512], F32)
        ln1g, ln1b, ln2g, ln2b = (vecs[:, 8 * n:8 * n + 8] for n in range(4))
        pscale, dskip = vecs[:, 32:36], vecs[:, 36:40]

        dexp = at("dexp", [P, 3, 2, 3, 32], F32)
        hfin = at("hfin", [P, 2, 36], F32)
        rotk = at("rotk", [P, 6, 2, 16], F32)
        oldsum = at("oldsum", [P, 4, DEC], F32)
        wide = at("wide", [P, 2, SEQ + 16], F32, r_z + 4 * (KD * T - 2 * (SEQ + 16)))
        ein1 = at("ein1", [P, 2, 4, NC], F32)
        dec01 = at("dec01", [P, 4, NC], F32)
        r1, r2, r3 = region(36 * 1024), region(18432), region(16640)
        r_u, r_y, r4 = region(8320), region(8320), region(22784)
        assert place[0] <= nc.sbuf_usable_end, place[0]
        xtok = at("xtok", [P, NT, D], F32, r2)
        xstok = at("xstok", [DEC, D], F32, r3)
        bp = [at(f"bp{n}", [P, CH, 4, 32], F32, r1 + 4096 * n) for n in range(2)]
        bt = [at(f"bt{n}", [P, CH, P], F32, r1 + 8192 + 4096 * n) for n in range(2)]
        cp = [[at(f"cp{m}{n}", [P, CH + 1, 4, 32], F32, (r1 + 16384, r3)[m] + 4608 * n) for n in range(2)] for m in range(2)]
        kbd = [at(f"kbd{m}", [P, CH, P], F32, (r1 + 25600, r3 + 9216)[m]) for m in range(2)]
        t1 = at("t1", [P, 512], F32, r1 + 29696)
        t2 = at("t2", [P, 512], F32, r1 + 31744)
        spool = at("spool", [120, 512], F32, r1 + 33792)
        poolw = at("poolw", [P, 4, P], F32, r3 + 13312)
        upool = at("upool", [P, 4, 16 + T], F32, r4)
        ein = [at("ein0", [P, 2, 4, NC], F32, r4 + 8704), ein1]
        dec0 = [at("dec00", [P, 4, NC], F32, r4 + 10752), dec01]
        vsb = at("vsb", [P, 4, 2 * 72], F32, r4 + 11776)
        wrot = at("wrot", [P, 2, 4, NC], F32, r4 + 14080)
        grot = at("grot", [P, 2, 4, NC], F32, r4 + 16128)
        hst = at("hst", [P, 2, 4, 73], F32, r4 + 18176)
        st_out = at("st_out", [36, 2, P], F32, r4 + 20512)
        bbar = at("bbar", [P, 2, 16, 16], F32, r_y)
        cc = at("cc", [P, 2, 16, 16], F32, r_y + 2048)
        h0 = at("h0", [P, 2, DEC, 16], F32, r_y + 4096)
        par = at("par", [P, 34, 16], F32, r_y + 5120)
        braw = at("braw", [P, 2, 16, 16], F32, r1 + 16384)
        craw = at("craw", [P, 2, 4, 2, E], F32, r1 + 18432)
        h0raw = at("h0raw", [P, 2, P], F32, r1 + 22528)
        lrow = at("lrow", [16, 3, P], F32, r1 + 23552)
        srow = at("srow", [16, 2], F32, r1 + 25088)
        u_ssm = at("u_ssm", [P, 4, T], F32, r_u)
        yp_hi = at("yp_hi", [P, 4, T], F32R, r2)
        yp_lo = at("yp_lo", [P, 4, T], F32R, r2 + 8320)
        ys_hi = at("ys_hi", [P, 4, T], F32R, r3)
        ys_lo = at("ys_lo", [P, 4, T], F32R, r3 + 8320)
        q_t = at("q_t", [P, 2, 3, T], F32, r1)
        k_t = at("k_t", [P, 2, 3, T], F32, r1 + 12480)
        v_t = at("v_t", [P, 3, T], F32, r1 + 24960)
        reps = [at("qrep", [32, 3, 256], F32, r1 + 31232), at("krep", [32, 3, 256], F32, r4 + 16384),
                at("vrep", [32, 3, 256], F32, r4 + 19456)]
        v_tok = at("v_tok", [P, NT, 3, 256], F32, r2)
        k_tok = at("k_tok", [P, NT, 3, P], F32, r2 + 12288)
        ya_hi = at("ya_hi", [P, 2, T], F32R, r_y)
        ya_lo = at("ya_lo", [P, 2, T], F32R, r_y + 4160)
        cbuf = [at(f"cbuf{n}", [P, DEC, 256], F32, r4 + 8192 * n) for n in range(2)]
        td = at("td", [P, 3, 512], F32, r4 + 14336)
        sc = at("sc", [P, 2, 1280], F32, r4)
        ptr = at("ptr", [P, 2, 512], F32, r4 + 10240)
        tdi = at("tdi", [P, 512], I32, r4 + 20480)
        m_hi = at("m_hi", [P, KD, T], F32R, r1)
        m_lo = at("m_lo", [P, KD, T], F32R, r1 + 16640)
        assert r1 + 33280 <= r2
        f_hi = at("f_hi", [P, KF, T], F32R, r1)
        f_lo = at("f_lo", [P, KF, T], F32R, r1 + 45760)
        ytok = [at(f"ytok{n}", [P, D], F32, r1 + 4096 * n) for n in range(2)]
        assert r1 + 91520 <= r4 + 22784

        ps = ctx.enter_context(nc.psum_tensor("ps", [P, 8, 512], F32))

        def pair(n):
            return ps[:, 2 * n:2 * n + 2, 0:HALF]

        def rows(a):
            return a.rearrange("p (h t) -> p h t", h=2)

        sems = {}

        def sem(name):
            if name not in sems:
                sems[name] = ctx.enter_context(nc.semaphore(name))
            return sems[name]

        raw_full = [sem(f"raw_full{n}") for n in range(RAW)]
        hi_done, lo_done = sem("hi_done"), sem("lo_done")
        panel_done = sem("panel_done")
        drained = [sem(f"drained{n}") for n in range(4)]
        x_in, par_in, vec_in = sem("x_in"), sem("par_in"), sem("vec_in")
        consts = sem("consts")

        def w_view(w):
            return w[0].rearrange("(k p) n -> p k n", p=P)

        v_in, v_out, v_glu = w_view(w_in), w_view(w_out), w_view(w_glu)
        v_bra, v_brp, v_brs = w_view(w_br_att), w_view(w_br_pool), w_view(w_br_ssm)
        v_gate, v_up, v_down = w_view(w_gate), w_view(w_up), w_view(w_down)

        def panel_source(p):
            if p < PAN_POOL:
                return v_in[:, :, COL_SSM + P * p:COL_SSM + P * (p + 1)]
            if p < PAN_POOLBR:
                c = COL_POOL + P * (p - PAN_POOL)
                return v_in[:, :, c:c + P]
            if p < PAN_QKV:
                c = (p - PAN_POOLBR) // 2 * P
                return v_brp[:, :, c:c + P] if p % 2 else v_in[:, :, COL_GATE + D + c:COL_GATE + D + c + P]
            if p < PAN_GLU:
                kind, g, hc = qkv_panel(p)
                c = (0, COL_K, COL_V)[kind] + 256 * g + P * hc
                return v_in[:, :, c:c + P]
            if p < PAN_SSMBR:
                return v_glu[:, :, P * (p - PAN_GLU):P * (p - PAN_GLU + 1)]
            c = (p - PAN_SSMBR) // 2 * P
            return v_brs[:, :, c:c + P] if p % 2 else v_in[:, :, COL_GATE + 2 * D + c:COL_GATE + 2 * D + c + P]

        block = ctx.enter_context(nc.Block())

        @block.sync
        def _(sp):
            def load(p, slot, src, blocks, wait):
                if wait is not None:
                    sp.wait_ge(lo_done, wait)
                dst = raw[:, slot, 0:blocks * P].rearrange("p (k n) -> p k n", k=blocks)
                sp.dma_start(dst, src).then_inc(raw_full[slot], 16)

            sent = {}

            def store(dst, src, name):
                sent[name] = sent.get(name, 0) + 16
                sp.dma_start(dst, src).then_inc(sem(name), 16)

            for p in range(RAW):
                load(p, p, panel_source(p), panel_blocks(p), None)
            loads = [
                (lrow[:, 0, :], lam_re[0].rearrange("(a g) p -> a (g p)", g=2)),
                (lrow[:, 1, :], lam_im[0].rearrange("(a g) p -> a (g p)", g=2)),
                (srow[:, :], log_step[0].rearrange("(a g) -> a g", g=2)),
            ]
            for n, (b, c, h) in enumerate(((b_re, c_re, ssm_re), (b_im, c_im, ssm_im))):
                loads.append((braw[:, n, :, :], b[0].rearrange("(a g) p h -> (g p) a h", g=2)))
                for m in range(2):
                    loads.append((craw[:, n, :, m, :], c[0].rearrange("(t g) h p -> (g h) t p", t=4)))
                loads.append((h0raw[:, n, :], h[0].rearrange("b (a g) p -> (b a) (g p)", g=2)))
            for dst, src in loads:
                sp.dma_start(dst, src).then_inc(par_in, 16)
            assert len(loads) == N_PAR
            loads = [(spool[:, :], state_pool[0].rearrange("b r c -> (b r) c")),
                     (poolw[:, :, :], pool_w[0].rearrange("g c e -> c g e")),
                     (dskip, ssm_d[0].rearrange("(k p) -> p k", p=P)),
                     (pscale, pool_scale[0].rearrange("(k p) -> p k", p=P))]
            for n, vec in enumerate((ln1_g, ln1_b, ln2_g, ln2_b)):
                loads.append((vecs[:, 8 * n:8 * n + 8], vec[0].rearrange("(k p) -> p k", p=P)))
            for dst, src in loads:
                sp.dma_start(dst, src).then_inc(vec_in, 16)
            assert len(loads) == N_VEC

            def cache_load(n):
                g, cache = n % 3, (cache_k, cache_v)[n // 3]
                keys, step = (P, DILATION[g]) if g < 2 else (PAST // DILATION[2], DILATION[2])
                src = cache[g][0].rearrange("b (r s) h e -> r s b (h e)", s=step)[:, 0]
                sp.dma_start(cbuf[n % 2][0:keys, :, :], src).then_inc(sem(f"cache_in{n}"), 16)

            for p in range(RAW, PAN_ATTBR):
                load(p, p % RAW, panel_source(p), panel_blocks(p), p - RAW + 1)
                for step in AFTER.get(p - SP_LAG, []):
                    if step[0] == "ssm_out":
                        ct = step[1]
                        sp.wait_ge(sem("state_staged"), ct + 1)
                        for n, (prompt, sample) in enumerate(((ssmre_p, ssmre_s), (ssmim_p, ssmim_s))):
                            store(prompt[0, 0].rearrange("(a g) p -> a (g p)", g=2)[4 * ct:4 * ct + 4], st_out[0:4, n, :],
                                  f"state_sent{ct}")
                            store(sample[0].rearrange("b (a g) p -> b a (g p)", g=2)[:, 4 * ct:4 * ct + 4],
                                  st_out[4:36, n, :], f"state_sent{ct}")
                    if step == "pool_mix":
                        sp.wait_ge(sem("pool_staged"), 1)
                        store(pool_p[0, 0], stage_dec[0:PBUF, :], "pool_sent")
                        store(pool_s[0].rearrange("b s c -> (b s) c"), stage_dec[PBUF:PBUF + DEC, :], "pool_sent")
                    if step[0] == "to_tokens":
                        hc = step[1]
                        for name, tile, dram in (("v_tokens", v_tok, vp), ("k_tokens", k_tok, kp)):
                            for i in range(NT):
                                sp.wait_ge(sem(name), NT * hc + i + 1)
                                for g in range(N_GROUPS):
                                    if g or i == NT - 1:
                                        dst = dram[g][0, 0].rearrange("t h e -> t (h e)")
                                        t0 = 0 if g == 0 else P * i
                                        c = slice(P * hc, P * hc + P)
                                        store(dst[t0:t0 + P, c], tile[:, i, g, c] if tile is v_tok else tile[:, i, g, :],
                                              f"{name}_sent{hc}")
                if p == PAN_GLU - 2:
                    sp.wait_ge(sem("gelu_split_done"), 4)
                    sp.wait_ge(sem("pool_split"), 4)
                    cache_load(0)
                    cache_load(1)
                if p == PAN_GLU + 3:
                    sp.wait_ge(sem("reps_done"), 3)
                    for g in range(N_GROUPS):
                        store(ks[g][0].rearrange("b s h e -> b (s h e)"), reps[1][0:32:4, g, :], "reps_sent")
                        store(vs[g][0].rearrange("b s h e -> b (s h e)"), reps[2][0:32:4, g, :], "reps_sent")
                    for n in range(2, 6):
                        if n < 5:
                            sp.wait_ge(sem("cache_scored"), n - 1)
                        else:
                            sp.wait_ge(sem("cache_summed"), n - 4)
                        cache_load(n)

            first = PAN_ATTBR // 2
            with sp.Fori(first, PAN_OUT // 2) as t:
                for j, (view, c0) in enumerate(((v_in, COL_GATE), (v_bra, 0))):
                    load(None, j, view[:, :, bass.ds(t * P + (c0 - first * P), P)], (8, 2)[j], t * 2 + (j - RAW + 1))
            with sp.Fori(0, KD // 2) as i:
                for j in range(2):
                    load(None, j, v_out[:, :, bass.ds(i * (2 * P) + P * j, P)], 8, i * 2 + (PAN_OUT + j - RAW + 1))
            with sp.Fori(0, KF) as i:
                for j, view in enumerate((v_gate, v_up)):
                    load(None, j, view[:, :, bass.ds(i * P, P)], 8, i * 2 + (PAN_FF + j - RAW + 1))
            with sp.Fori(0, KD) as i:
                k0 = 0
                for j, blocks in enumerate(DOWN_K):
                    load(None, j % 2, v_down[:, k0:k0 + blocks, bass.ds(i * P, P)], blocks, i * 4 + (PAN_DOWN + j - RAW + 1))
                    k0 += blocks
            for i in range(NT + 1):
                sp.wait_ge(sem("y_staged"), i + 1)
                if i < NT:
                    store(y_p[0, P * i:P * i + P, :], ytok[i % 2][:, :], f"y_sent{i}")
                else:
                    store(y_s.rearrange("b s d -> (b s) d"), ytok[i % 2][0:DEC, :], f"y_sent{i}")
            for name, value in sent.items():
                sp.wait_ge(sem(name), value)

        @block.gpsimd
        def _(pool):
            count = [0]

            def link(ins):
                count[0] += 1
                ins.then_inc(sem("pool_seq"), 1)
                pool.wait_ge(sem("pool_seq"), count[0])

            def lo(slot, raw_slot, blocks, n):
                pool.wait_ge(hi_done, n + 1)
                nc.gpsimd.tensor_tensor(w_lo[:, slot, 0:blocks * P], raw[:, raw_slot, 0:blocks * P],
                                        w_hi[:, slot, 0:blocks * P].bitcast(F32), ALU.subtract).then_inc(lo_done, 1)

            nc.gpsimd.memset(ones[:, :], 1.0).then_inc(consts, 1)
            pool.wait_ge(consts, 1)
            nc.gpsimd.affine_select(out=ident[:, :], in_=ones[:, :], compare_op=ALU.is_equal, fill=0.0, base=0,
                                    pattern=[[-1, P]], channel_multiplier=1).then_inc(consts, 1)
            for p in range(2):
                lo(p % RING, p % RAW, panel_blocks(p), p)
            for g, w in enumerate(POOL_W):
                link(nc.gpsimd.affine_select(out=wsel[:, g, :], in_=ones[:, 0:DEC], compare_op=ALU.is_ge, fill=0.0,
                                             base=-(PBUF - w + 1), pattern=[[-PBUF, DEC]], channel_multiplier=1))
                link(nc.gpsimd.affine_select(out=wsel[:, g, :], in_=wsel[:, g, :], compare_op=ALU.is_ge, fill=0.0,
                                             base=PBUF - 1, pattern=[[PBUF, DEC]], channel_multiplier=-1))
            link(nc.gpsimd.iota(rcnt[:, 0, :], pattern=[[1, 16]], base=1, channel_multiplier=0,
                                allow_small_or_imprecise_dtypes=True))
            link(nc.gpsimd.iota(dist32[:, 0:128], pattern=[[-1, P]], base=P, channel_multiplier=0,
                                allow_small_or_imprecise_dtypes=True))
            link(nc.gpsimd.iota(dist32[:, 128:256], pattern=[[-4, P]], base=4 * P, channel_multiplier=0,
                                allow_small_or_imprecise_dtypes=True))
            nc.gpsimd.iota(dist32[:, 256:288], pattern=[[-16, 32]], base=512, channel_multiplier=0,
                           allow_small_or_imprecise_dtypes=True).then_inc(consts, 1)

            def bias_tables():
                pool.wait_ge(sem("decode_done"), 1)
                pool.wait_ge(sem("reps_sent"), 16 * 2 * N_GROUPS)
                link(nc.gpsimd.iota(tdi[:, :], pattern=[[-1, 512]], base=384, channel_multiplier=1))
                link(nc.gpsimd.iota(td[:, 1, :], pattern=[[-1, 512]], base=384, channel_multiplier=1,
                                    allow_small_or_imprecise_dtypes=True))
                link(nc.gpsimd.affine_select(out=td[:, 1, :], in_=td[:, 1, :], compare_op=ALU.is_ge, fill=BIG,
                                             base=384, pattern=[[-1, 512]], channel_multiplier=1))
                nc.gpsimd.affine_select(out=td[:, 0, :], in_=td[:, 1, :], compare_op=ALU.is_ge, fill=BIG,
                                        base=BACK - 384, pattern=[[1, 512]], channel_multiplier=-1
                                        ).then_inc(sem("td_base"), 1)

            for p in range(2, PAN_ATTBR):
                lo(p % RING, p % RAW, panel_blocks(p), p)
                for step in AFTER.get(p - 4, []):
                    if step == "bias":
                        bias_tables()
            with pool.Fori(0, KD // 2) as i:
                for j in range(4):
                    lo((PAN_ATTBR + j) % RING, j % RAW, (8, 2)[j % 2], i * 4 + (PAN_ATTBR + j))
            with pool.Fori(0, (KD + 2 * KF) // 4) as i:
                for j in range(4):
                    lo((PAN_OUT + j) % RING, j % RAW, 8, i * 4 + (PAN_OUT + j))
            with pool.Fori(0, KD) as i:
                for j in range(4):
                    lo((PAN_DOWN + j) % RING, j % RAW, DOWN_K[j], i * 4 + (PAN_DOWN + j))

        @block.tensor
        def _(pe):
            mm = nc.tensor.matmul

            def tr(out, in_):
                n = in_.partition_size()
                return nc.tensor.transpose(out, in_, ident[0:n, 0:n])

            def multiply(slot, blocks, hi, lo, out_pair, k0=0, first=True, last=True):
                for k in range(blocks):
                    wh, wl = (w[:, slot, P * k:P * k + P] for w in (w_hi, w_lo))
                    for m, (w, x) in enumerate(((wh, hi), (wh, lo), (wl, hi))):
                        for h in range(2):
                            ins = mm(ps[:, 2 * out_pair + h, 0:HALF], w, x[:, k0 + k, HALF * h:HALF * (h + 1)],
                                     start=(first and k == 0 and m == 0), stop=(last and k == blocks - 1 and m == 2))
                return ins

            def panel(p, hi, lo, wait=True):
                pe.wait_ge(lo_done, p + 1)
                if p >= 2:
                    pe.wait_ge(drained[p % 2], p // 2)
                multiply(p % RING, panel_blocks(p), hi, lo, p % 2).then_inc(panel_done, 1)

            pe.wait_ge(consts, 2)
            for c in range(KD):
                if c == 0:
                    pe.wait_ge(x_in, 16 * (NT + 1))
                if c >= 4:
                    pe.wait_ge(sem("x_split"), c - 3)
                for i in range(NT):
                    ins = tr(ps[:, 4 + c % 4, P * i:P * i + P], xtok[:, i, P * c:P * c + P])
                ins.then_inc(sem("x_turned"), 1)
            for c in range(KD):
                ins = tr(ps[:, 0, DEC * c:DEC * c + DEC], xstok[0:DEC, P * c:P * c + P])
            ins.then_inc(sem("x_turned"), 1)
            def turn_params():
                pe.wait_ge(par_in, 16 * N_PAR)
                pe.wait_ge(sem("steps_spread"), 1)
                for n in range(3):
                    ins = tr(ps[:, 4, 16 * n:16 * n + 16], lrow[:, n, :])
                ins.then_inc(sem("lam_turned"), 1)
                for n in range(2):
                    for ct in range(4):
                        ins = tr(ps[:, 5 + n, P * ct:P * ct + P], craw[:, n, ct, :, :].rearrange("p g e -> p (g e)"))
                ins.then_inc(sem("c_turned"), 1)
                for n in range(2):
                    ins = tr(ps[:, 7, P * n:P * n + P], h0raw[:, n, :])
                ins.then_inc(sem("h0_turned"), 1)

            def ssm_prep(ct):
                m = ct % 2
                pe.wait_ge(sem("powers_done"), ct + 1)
                if ct == 0:
                    pe.wait_ge(sem("par_read"), 3)
                else:
                    pe.wait_ge(sem("v_copied"), ct)
                if ct == 1:
                    pe.wait_ge(sem("pool_scaled"), 4)
                for n in range(2):
                    for k in range(CH):
                        bank = 4 + 2 * n + k // 4
                        ins = tr(ps[:, bank, P * (k % 4):P * (k % 4) + P],
                                 bp[n][:, k, :, :].rearrange("p q c -> p (q c)"))
                ins.then_inc(sem("bt_turned"), 1)
                pe.wait_ge(sem("bt_copied"), ct + 1)
                for q in range(4):
                    for n in range(2):
                        ins = mm(ps[32 * q:32 * q + 32, 4, 0:256], bp[n][:, 0, q, :], cp[m][n][:, 0:CH, q, :],
                                 start=n == 0, stop=n == 1)
                ins.then_inc(sem("k_formed"), 1)

            def ssm_in(ct):
                pe.wait_ge(sem("k_copied"), ct + 1)
                if ct == 0:
                    pe.wait_ge(drained[1], 2)
                    pe.wait_ge(drained[0], 2)
                else:
                    pe.wait_ge(sem("y_read"), ct)
                    pe.wait_ge(sem("state_staged"), ct)
                for q in range(4):
                    r = slice(32 * q, 32 * q + 32)
                    for n in range(2):
                        for s in range(CH):
                            mm(ps[:, 4 + q, 72 * n:72 * n + NC], bt[n][r, CH - 1 - s, :],
                               u_ssm[r, ct, NC * s:NC * s + NC], start=s == 0, stop=s == CH - 1)
                        ins = mm(ps[:, 4 + q, 72 * n + NC:72 * n + 72], bt[n][r, 0, :], u_ssm[r, ct, SEQ:T],
                                 start=True, stop=True)
                ins.then_inc(sem("v_formed"), 1)

            def ssm_out(ct):
                m = ct % 2
                pe.wait_ge(sem("h_done"), ct + 1)
                if ct < 3:
                    pe.wait_ge(sem("k_copied"), ct + 2)
                for j in range(CH):
                    mm(ps[:, 4, NC * j:512], kbd[m][:, j, :], u_ssm[:, ct, 0:NC * (CH - j)],
                       start=j == 0, stop=False, skip_group_check=True)
                for q in range(4):
                    r = slice(32 * q, 32 * q + 32)
                    for t in range(CH):
                        for n in range(2):
                            mm(ps[r, 4, NC * t:NC * t + NC], cp[m][n][:, t + 1, q, :], hst[:, n, q, 0:NC],
                               start=False, stop=n == 1, skip_group_check=True)
                for q in range(4):
                    for n in range(2):
                        ins = mm(ps[32 * q:32 * q + 32, 5, 0:DEC], cp[m][n][:, 0, q, :], hst[:, n, q, 65:73],
                                 start=n == 0, stop=n == 1)
                ins.then_inc(sem("y_formed"), 1)
                for n in range(2):
                    ins = tr(ps[0:36, 6, P * n:P * n + P], hfin[:, n, :])
                ins.then_inc(sem("state_turned"), 1)

            def pool_mix():
                pe.wait_ge(consts, 3)
                pe.wait_ge(vec_in, 16 * N_VEC)
                pe.wait_ge(sem("v_copied"), 1)
                pe.wait_ge(drained[0], PAN_POOLBR // 2)
                pe.wait_ge(drained[1], PAN_POOLBR // 2)
                for g in range(4):
                    ins = mm(ps[:, 4, DEC * g:DEC * g + DEC], spool[0:120, P * g:P * g + P], wsel[0:120, g, :],
                             start=True, stop=True)
                ins.then_inc(sem("psum_old"), 1)
                for g in range(4):
                    ins = tr(ps[0:PBUF + DEC, 5, P * g:P * g + P], upool[:, g, 16 + SEQ - PBUF:16 + T])
                ins.then_inc(sem("pool_turned"), 1)
                for g in range(4):
                    pe.wait_ge(sem("diff_done"), g + 1)
                    if g == 0:
                        pe.wait_ge(sem("psum_old_read"), 1)
                        pe.wait_ge(sem("pool_staged"), 1)
                    if g >= 2:
                        pe.wait_ge(sem("pool_scaled"), g - 1)
                    for h in range(2):
                        ins = mm(ps[:, 4 + 2 * (g % 2) + h, 0:HALF], poolw[:, g, :],
                                 upool[:, g, 16 + HALF * h:16 + HALF * (h + 1)], start=True, stop=True)
                    ins.then_inc(sem("pool_mixed"), 1)

            def to_tokens(hc):
                pe.wait_ge(drained[(PAN_QKV + 9 * hc + 8) % 2], (PAN_QKV + 9 * hc + 8) // 2 + 1)
                pe.wait_ge(drained[(PAN_QKV + 9 * hc + 7) % 2], (PAN_QKV + 9 * hc + 7) // 2 + 1)
                for i in range(NT):
                    if hc == 0:
                        pe.wait_ge(sem("y_read"), 4)
                        pe.wait_ge(sem("state_staged"), 4)
                        pe.wait_ge(sem("pool_split"), 4)
                    else:
                        pe.wait_ge(sem("k_tokens"), NT)
                    for g in range(N_GROUPS):
                        ins = tr(ps[:, 4 + i, P * g:P * g + P], v_t[:, g, P * i:P * i + P])
                    ins.then_inc(sem("v_turned"), 1)
                for i in range(NT):
                    pe.wait_ge(sem("v_tokens"), NT * hc + i + 1)
                    for g in range(N_GROUPS):
                        if g or i == NT - 1:
                            ins = tr(ps[:, 4 + i, P * g:P * g + P], k_t[:, hc, g, P * i:P * i + P])
                    ins.then_inc(sem("k_turned"), 1)

            def decode_rep(n):
                if n == 0:
                    pe.wait_ge(sem("k_tokens"), 2 * NT)
                    pe.wait_ge(sem("decode_kept"), 6)
                if n == 2:
                    pe.wait_ge(sem("reps_done"), 1)
                b = 4 + 2 * (n % 2)
                for g in range(N_GROUPS):
                    for hc in range(2):
                        c = 256 * g + P * hc
                        ins = tr(ps[0:32, b + c // 512, c % 512:c % 512 + P], dexp[:, n, hc, g, :])
                ins.then_inc(sem("rep_turned"), 1)

            def decode_scores():
                for g in range(N_GROUPS):
                    for b2 in range(4):
                        n = 4 * g + b2
                        if n == 0:
                            pe.wait_ge(sem("reps_done"), 3)
                        if n >= 4:
                            pe.wait_ge(sem("qk_read"), n - 3)
                        for b in range(2):
                            ins = mm(ps[:, 4 + n % 4, 256 * b:256 * b + 256],
                                     ident[0:32, 4 * (2 * b2 + b):4 * (2 * b2 + b) + 1].broadcast_to([32, P]),
                                     reps[0][:, g, :], start=True, stop=True)
                        ins.then_inc(sem("q_spread"), 1)
                pe.wait_ge(sem("qk_read"), 12)
                for g in range(N_GROUPS):
                    pe.wait_ge(sem("cache_scored"), g + 1)
                    keys = P if g < 2 else 32
                    ins = tr(ps[0:32, 4, P * g:P * g + keys], s32[0:keys, g, :])
                ins.then_inc(sem("s_turned"), 1)

            def decode_softmax():
                pe.wait_ge(sem("p_done"), 1)
                for g in range(N_GROUPS):
                    keys = P if g < 2 else 32
                    ins = tr(ps[0:keys, 5, 32 * g:32 * g + 32], sc32[:, P * g:P * g + keys])
                ins.then_inc(sem("p_turned"), 1)

            def decode_out():
                pe.wait_ge(sem("p_copied"), 1)
                pe.wait_ge(sem("diag_done"), 1)
                for hc in range(2):
                    for g in range(N_GROUPS):
                        ins = mm(ps[:, 6 + hc, 0:16], reps[2][:, g, P * hc:P * hc + P],
                                 diag32[:, g, :].rearrange("r (b h) -> r b h", h=4)[:, :, 2 * hc:2 * hc + 2],
                                 start=g == 0, stop=False, skip_group_check=True)
                for g in range(N_GROUPS):
                    keys = P if g < 2 else 32
                    pe.wait_ge(sem(f"cache_in{3 + g}"), 16)
                    for hc in range(2):
                        for b in range(DEC):
                            ins = mm(ps[:, 6 + hc, 2 * b:2 * b + 2], cbuf[(3 + g) % 2][0:keys, b, P * hc:P * hc + P],
                                     pt32[0:keys, g, 4 * b + 2 * hc:4 * b + 2 * hc + 2],
                                     start=False, stop=g == 2, skip_group_check=True)
                    ins.then_inc(sem("cache_summed"), 1)

            blocks_of = [(g, kt) for g in range(N_GROUPS) for kt in range(NT)]

            def keys_of(g, i):
                return [kt for kt in range(NT) if kt <= i and (g or kt >= i - 1)]

            tcount = [0]

            def scores(n):
                h, i = ATT_STEPS[n]
                r = slice(64 * (h % 2), 64 * (h % 2) + 64)
                for g in range(N_GROUPS):
                    keys = keys_of(g, i)
                    if n == 0:
                        pe.wait_ge(sem("decode_done"), 1)
                    if n > 0 or g == 2:
                        pe.wait_ge(sem("scored"), 3 * n + (0, -1, 1)[g])
                    mm(ps[:, 4 + g % 2, 0:P * len(keys)], q_t[r, h // 2, g, P * i:P * i + P],
                       k_t[r, h // 2, g, P * keys[0]:P * (i + 1)], start=True, stop=True
                       ).then_inc(sem("s_formed"), 1)

            def probs(n):
                h, i = ATT_STEPS[n]
                r = slice(64 * (h % 2), 64 * (h % 2) + 64)
                blocks = [(g, kt) for g in range(N_GROUPS) for kt in keys_of(g, i)]
                quads = [blocks[m:m + 4] for m in range(0, len(blocks), 4)]
                pe.wait_ge(sem("p_normed"), n + 1)
                for m in range(len(quads) + 1):
                    if m < len(quads):
                        if tcount[0] >= 1:
                            pe.wait_ge(sem("pt_copied"), tcount[0])
                        for j, _ in enumerate(quads[m]):
                            c = P * (4 * m + j)
                            ins = tr(ps[:, 7, P * j:P * j + P], sc[:, n % 2, c:c + P])
                        tcount[0] += 1
                        ins.then_inc(sem("pt_turned"), 1)
                    if m >= 1:
                        if m == len(quads):
                            pe.wait_ge(sem("pt_copied"), tcount[0])
                        if m == 1 and n >= 1:
                            pe.wait_ge(sem("o_split"), n)
                        t = tcount[0] - (1 if m == len(quads) else 2)
                        for j, (g, kt) in enumerate(quads[m - 1]):
                            b = 4 * (m - 1) + j
                            ins = mm(ps[r, 6, 0:P], v_tok[:, kt, g, 64 * h:64 * h + 64], ptr[:, t % 2, P * j:P * j + P],
                                     start=b == 0, stop=b == len(blocks) - 1)
                        if m < len(quads):
                            ins.then_inc(sem("pt_used"), 1)
                ins.then_inc(sem("pt_used"), 1)

            def run(step):
                name, arg = step if isinstance(step, tuple) else (step, None)
                todo = {"ssm_prep": ssm_prep, "ssm_in": ssm_in, "ssm_out": ssm_out, "to_tokens": to_tokens,
                        "scores": scores, "probs": probs}
                if name in todo:
                    todo[name](arg)
                elif name == "turn_params":
                    turn_params()
                elif name == "pool_mix":
                    pool_mix()
                elif name in ("decode_q", "decode_k", "decode_v"):
                    decode_rep(("decode_q", "decode_k", "decode_v").index(name))
                elif name == "decode_scores":
                    decode_scores()
                elif name == "decode_softmax":
                    decode_softmax()
                elif name == "decode_out":
                    decode_out()

            pe.wait_ge(sem("x_split"), KD + 1)
            for p in range(PAN_ATTBR):
                if p == PAN_POOLBR + 1:
                    pe.wait_ge(sem("pool_split"), 4)
                if p == PAN_GLU:
                    pe.wait_ge(sem("gelu_split_done"), 4)
                if p == PAN_SSMBR + 1:
                    pe.wait_ge(sem("ys_split"), 4)
                rows_of = (x_hi, x_lo)
                if PAN_POOLBR <= p < PAN_QKV and p % 2:
                    rows_of = (yp_hi, yp_lo)
                if PAN_GLU <= p < PAN_SSMBR or (p >= PAN_SSMBR and p % 2):
                    rows_of = (ys_hi, ys_lo)
                panel(p, *rows_of)
                for step in AFTER.get(p, []):
                    run(step)

            pe.wait_ge(sem("o_split"), len(ATT_STEPS))
            with pe.Fori(0, KD // 2) as i:
                for j in range(4):
                    pe.wait_ge(lo_done, i * 4 + (PAN_ATTBR + j + 1))
                    pe.wait_ge(drained[j % 2], i * 2 + (PAN_ATTBR + j) // 2)
                    hi, lo = ((x_hi, x_lo), (ya_hi, ya_lo))[j % 2]
                    multiply((PAN_ATTBR + j) % RING, (8, 2)[j % 2], hi, lo, j % 2).then_inc(panel_done, 1)
            pe.wait_ge(sem("m_split"), KD)
            with pe.Fori(0, KD // 4) as i:
                for j in range(4):
                    pe.wait_ge(lo_done, i * 4 + (PAN_OUT + j + 1))
                    pe.wait_ge(drained[j % 2], i * 2 + (PAN_OUT + j) // 2)
                    multiply((PAN_OUT + j) % RING, 8, m_hi, m_lo, j % 2).then_inc(panel_done, 1)

            def norm_sums(n):
                for c in range(KD):
                    pe.wait_ge(sem("z_done"), KD * n + c + 1)
                    for h in range(2):
                        ins = mm(ps[:, 4 + h, 0:HALF], ones[:, :], z[:, c, HALF * h:HALF * (h + 1)],
                                 start=c == 0, stop=c == KD - 1)
                ins.then_inc(sem("sum_done"), 1)
                for c in range(KD):
                    pe.wait_ge(sem("squared"), KD * n + c + 1)
                    for h in range(2):
                        ins = mm(ps[:, 6 + h, 0:HALF], ones[:, :], tg[:, c % 2, HALF * h:HALF * (h + 1)],
                                 start=c == 0, stop=c == KD - 1)
                    ins.then_inc(sem("square_summed"), 1)

            norm_sums(0)
            pe.wait_ge(sem("x1_split"), KD)
            with pe.Fori(0, KF // 2) as i:
                for j in range(4):
                    pe.wait_ge(lo_done, i * 4 + (PAN_FF + j + 1))
                    pe.wait_ge(drained[j], i * 1 + (PAN_FF // 2 if j < 2 else 0))
                    multiply((PAN_FF + j) % RING, 8, x_hi, x_lo, j).then_inc(panel_done, 1)
            pe.wait_ge(sem("f_split"), KF)
            with pe.Fori(0, KD // 2) as i:
                for o in range(2):
                    k0 = 0
                    for j, blocks in enumerate(DOWN_K):
                        pe.wait_ge(lo_done, i * 8 + (PAN_DOWN + 4 * o + j + 1))
                        if j == 0:
                            pe.wait_ge(drained[o], i * 1 + (PAN_FF // 2 + KF // 2))
                        multiply((PAN_DOWN + j) % RING, blocks, f_hi, f_lo, o, k0, j == 0, j == 3).then_inc(panel_done, 1)
                        k0 += blocks
            norm_sums(1)
            for i in range(NT + 1):
                n = P if i < NT else DEC
                if i >= 4:
                    pe.wait_ge(sem("y_staged"), i - 3)
                for c in range(KD):
                    pe.wait_ge(sem("y_done"), c + 1)
                    ins = tr(ps[0:n, 2 * (i % 4) + c // 4, P * (c % 4):P * (c % 4) + P], z[:, c, P * i:P * i + n])
                ins.then_inc(sem("y_turned"), 1)

        @block.scalar
        def _(act):
            A = nc.scalar.activation

            def hi(slot, raw_slot, blocks, n, turn, used=None):
                act.wait_ge(raw_full[raw_slot], turn)
                if used is not None:
                    act.wait_ge(panel_done, used)
                A(w_hi[:, slot, 0:blocks * P], raw[:, raw_slot, 0:blocks * P], ACT.Copy).then_inc(hi_done, 1)

            def hi_static(p):
                if p < PAN_END:
                    hi(p % RING, p % RAW, panel_blocks(p), p, 16 * (p // RAW + 1), p - RING + 1 if p >= RING else None)

            for i in range(NT):
                act.dma_start(xtok[:, i, :], x_prompt[0, P * i:P * i + P, :]).then_inc(x_in, 16)
            act.dma_start(xstok[:, :], x_sample.rearrange("b s d -> (b s) d")).then_inc(x_in, 16)
            for p in range(2):
                hi_static(p)
            for c in range(KD):
                act.wait_ge(sem("x_turned"), c + 1)
                A(x_hi[:, c, 0:SEQ], ps[:, 4 + c % 4, :], ACT.Copy).then_inc(sem("x_high"), 1)
            act.wait_ge(sem("x_turned"), KD + 1)
            A(x_hi[:, :, SEQ:T], ps[:, 0, 0:DEC * KD].rearrange("p (c b) -> p c b", b=DEC), ACT.Copy).then_inc(sem("x_high"), 1)
            hi_static(2)

            def params():
                act.wait_ge(sem("angle_done"), 1)
                A(par[:, 6, :], par[:, 4, :], ACT.Sin).then_inc(sem("sin_done"), 1)
                A(par[:, 7, :], par[:, 5, :], ACT.Sin).then_inc(sem("sin_done"), 1)

            def evacuate(p):
                if p >= PAN_ATTBR:
                    return
                act.wait_ge(panel_done, p + 1)
                b = 2 * (p % 2)
                if p < PAN_POOL:
                    u = u_ssm[:, p, 0:SEQ].rearrange("p (s c) -> p c s", s=CH)
                    A(u[:, 0:32, :], ps[:, b, 0:256].rearrange("p (c s) -> p c s", s=CH), ACT.Copy)
                    A(u[:, 32, 0:4], ps[:, b, 256:260], ACT.Copy)
                    A(u[:, 32, 4:8], ps[:, b + 1, 0:4], ACT.Copy)
                    A(u[:, 33:64, :], ps[:, b + 1, 4:252].rearrange("p (c s) -> p c s", s=CH), ACT.Copy)
                    A(u_ssm[:, p, SEQ:T], ps[:, b + 1, 252:260], ACT.Copy).then_inc(drained[p % 2], 1)
                elif p < PAN_POOLBR:
                    A(rows(upool[:, p - PAN_POOL, 16:16 + T]), pair(p % 2), ACT.Copy).then_inc(drained[p % 2], 1)
                elif p < PAN_QKV or p >= PAN_SSMBR:
                    if p % 2 == 0:
                        n = (p - PAN_POOLBR) // 2 if p < PAN_QKV else (p - PAN_SSMBR) // 2
                        first = p in (PAN_POOLBR, PAN_POOLBR + 2)
                        if p in (PAN_SSMBR, PAN_SSMBR + 2):
                            act.wait_ge(sem("glu_used"), 4)
                        elif not first:
                            act.wait_ge(drained[1], (p - 3) // 2 + 1)
                        A(rows(tg[:, n % 2, :]), pair(0), ACT.Tanh, scale=0.5).then_inc(drained[0], 1)
                elif p < PAN_GLU:
                    kind, g, hc = qkv_panel(p)
                    if p == PAN_QKV:
                        act.wait_ge(sem("gelu_split_done"), 4)
                    if kind == 2 and hc == 1 and g == 0:
                        act.wait_ge(sem("v_turned"), NT)
                        act.wait_ge(sem("decode_kept"), 3)
                    dst = (q_t[:, hc, g, :], k_t[:, hc, g, :], v_t[:, g, :])[kind]
                    A(rows(dst), pair(p % 2), ACT.Copy).then_inc(drained[p % 2], 1)
                else:
                    n = p - PAN_GLU
                    if n >= 2:
                        act.wait_ge(sem("glu_used"), n - 1)
                    else:
                        act.wait_ge(drained[1], PAN_QKV // 2)
                    A(rows(tg[:, n % 2, :]), pair(p % 2), ACT.Tanh, scale=0.5).then_inc(drained[p % 2], 1)

            def ssm_prep(ct):
                act.wait_ge(sem("bt_turned"), ct + 1)
                for n in range(2):
                    for half in range(2):
                        ins = A(bt[n][:, 4 * half:4 * half + 4, :], ps[:, 4 + 2 * n + half, :].rearrange("p (k c) -> p k c", k=4),
                                ACT.Copy)
                ins.then_inc(sem("bt_copied"), 1)

            def ssm_in(ct):
                act.wait_ge(sem("v_formed"), ct + 1)
                if ct >= 1:
                    act.wait_ge(sem("h_done"), ct)
                A(vsb[:, :, :], ps[:, 4:8, 0:144], ACT.Copy).then_inc(sem("v_copied"), 1)

            def ssm_out(ct):
                act.wait_ge(sem("state_turned"), ct + 1)
                if ct >= 1:
                    act.wait_ge(sem(f"state_sent{ct - 1}"), 64)
                A(st_out[:, :, :], ps[0:36, 6, 0:256].rearrange("p (n c) -> p n c", n=2), ACT.Copy).then_inc(sem("state_staged"), 1)

            def gelu(ct):
                act.wait_ge(sem("g_in"), ct + 1)
                A(t2_row, t1_row, ACT.Tanh, scale=math.sqrt(2 / math.pi)).then_inc(sem("g_tanh"), 1)

            def high_rows(dst, ct, scale):
                A(dst[:, ct, 0:SEQ].rearrange("p (c s) -> p c s", s=CH),
                  u_ssm[:, ct, 0:SEQ].rearrange("p (s c) -> p c s", s=CH), ACT.Copy, scale=scale)
                return A(dst[:, ct, SEQ:T], u_ssm[:, ct, SEQ:T], ACT.Copy, scale=scale)

            def gelu_split():
                act.wait_ge(sem("gelu_done"), 4)
                act.wait_ge(sem("y_formed"), 4)
                for ct in range(4):
                    high_rows(ys_hi, ct, 0.5).then_inc(sem("gelu_high"), 1)

            def pool_mix():
                act.wait_ge(sem("pool_turned"), 1)
                A(stage_dec[0:PBUF + DEC, :], ps[0:PBUF + DEC, 5, :], ACT.Copy).then_inc(sem("pool_staged"), 1)
                for g in range(4):
                    act.wait_ge(sem("pool_scaled"), g + 1)
                    A(yp_hi[:, g, :], tw[:, g % 2, :], ACT.Copy).then_inc(sem("pool_high"), 1)

            def to_tokens(hc):
                for i in range(NT):
                    act.wait_ge(sem("v_turned"), NT * hc + i + 1)
                    A(v_tok[:, i, :, P * hc:P * hc + P], ps[:, 4 + i, 0:384].rearrange("p (g c) -> p g c", g=3),
                      ACT.Copy).then_inc(sem("v_tokens"), 1)
                for i in range(NT):
                    act.wait_ge(sem("k_turned"), NT * hc + i + 1)
                    if hc == 1 and i == 0:
                        act.wait_ge(sem("k_tokens_sent0"), 16 * 9)
                    g0 = 0 if i == NT - 1 else 1
                    A(k_tok[:, i, g0:3, :], ps[:, 4 + i, P * g0:384].rearrange("p (g c) -> p g c", c=P),
                      ACT.Copy).then_inc(sem("k_tokens"), 1)

            def decode_rep(n):
                act.wait_ge(sem("rep_turned"), n + 1)
                b = 4 + 2 * (n % 2)
                A(reps[n][:, 0:2, :], ps[0:32, b, :].rearrange("p (g c) -> p g c", g=2), ACT.Copy)
                A(reps[n][:, 2, :], ps[0:32, b + 1, 0:256], ACT.Copy).then_inc(sem("reps_done"), 1)

            def decode_softmax():
                act.wait_ge(sem("s32_done"), 1)
                A(sc32[:, 0:291], sc32[:, 0:291], ACT.Exp, bias=small[0:32, 1:2], scale=0.125,
                  accum_out=small[0:32, 2:3]).then_inc(sem("e32_done"), 1)
                act.wait_ge(sem("p_turned"), 1)
                A(pt32[:, 0:2, :], ps[:, 5, 0:64].rearrange("p (g c) -> p g c", g=2), ACT.Copy)
                A(pt32[0:32, 2, :], ps[0:32, 5, 64:96], ACT.Copy).then_inc(sem("p_copied"), 1)

            def decode_out():
                act.wait_ge(sem("cache_summed"), 3)
                for h in range(2):
                    r = slice(64 * h, 64 * h + 64)
                    ins = A(ya_hi[r, :, SEQ:T], ps[r, 6:8, 0:16].rearrange("p c (b h) -> p c b h", h=2)[:, :, :, h], ACT.Copy)
                ins.then_inc(sem("od_high"), 1)

            def scores(n):
                h, i = ATT_STEPS[n]
                act.wait_ge(sem("max_done"), n + 1)
                cols = P * sum(len([1 for kt in range(i + 1) if g or kt >= i - 1]) for g in range(3))
                A(sc[:, n % 2, 0:cols], sc[:, n % 2, 0:cols], ACT.Exp, bias=small[:, 8 + n % 2:9 + n % 2], scale=0.125,
                  accum_out=small[:, 10 + n % 2:11 + n % 2]).then_inc(sem("exp_done"), 1)

            tcount = [0]

            def probs(n):
                h, i = ATT_STEPS[n]
                total = sum(len([1 for kt in range(i + 1) if g or kt >= i - 1]) for g in range(3))
                for m in range(0, total, 4):
                    k = min(4, total - m)
                    act.wait_ge(sem("pt_turned"), tcount[0] + 1)
                    if tcount[0] >= 2:
                        act.wait_ge(sem("pt_used"), tcount[0] - 1)
                    A(ptr[:, tcount[0] % 2, 0:P * k], ps[:, 7, 0:P * k], ACT.Copy).then_inc(sem("pt_copied"), 1)
                    tcount[0] += 1
                act.wait_ge(sem("pt_used"), tcount[0])
                r = slice(64 * (h % 2), 64 * (h % 2) + 64)
                A(ya_hi[r, h // 2, P * i:P * i + P], ps[r, 6, 0:P], ACT.Copy).then_inc(sem("o_high"), 1)

            t1_row = tw[:, 0, :]
            t2_row = tw[:, 1, :]

            def run(step):
                name, arg = step if isinstance(step, tuple) else (step, None)
                todo = {"ssm_prep": ssm_prep, "ssm_in": ssm_in, "ssm_out": ssm_out, "to_tokens": to_tokens,
                        "scores": scores, "probs": probs, "gelu": gelu}
                if name in todo:
                    todo[name](arg)
                elif name == "params":
                    params()
                elif name == "pool_mix":
                    pool_mix()
                elif name == "gelu_split":
                    gelu_split()
                elif name in ("decode_q", "decode_k", "decode_v"):
                    decode_rep(("decode_q", "decode_k", "decode_v").index(name))
                elif name == "decode_softmax":
                    decode_softmax()
                elif name == "decode_out":
                    decode_out()

            for p in range(PAN_ATTBR):
                hi_static(p + LOOK)
                evacuate(p)
                for step in AFTER.get(p, []):
                    run(step)
                if p == PAN_SSMBR - 1:
                    for ct in range(4):
                        act.wait_ge(sem("glu_used"), 4)
                        high_rows(ys_hi, ct, 0.25).then_inc(sem("ys_high"), 1)

            def att_turn(i, looks):
                for j in range(4):
                    if looks is None:
                        q = PAN_ATTBR + j + LOOK
                        hi(q % RING, q % RAW, (8, 2)[q % 2], None, i * 32 + 16 * (q // RAW + 1), i * 4 + (q - RING + 1))
                    else:
                        hi_static(looks + j + LOOK)
                    act.wait_ge(panel_done, i * 4 + (PAN_ATTBR + j + 1))
                    if j % 2 == 0:
                        act.wait_ge(drained[1], i * 2 + (PAN_ATTBR + j - 3) // 2 + 1)
                        A(rows(tg[:, j // 2, :]), pair(0), ACT.Tanh, scale=0.5).then_inc(drained[0], 1)
                    else:
                        act.wait_ge(sem("m_summed"), i * 2 + (j // 2 + 1))
                        A(m_hi[:, bass.ds(i * 2 + j // 2, 1), :], z[:, bass.ds(i * 2 + j // 2, 1), :],
                          ACT.Copy, scale=0.5).then_inc(sem("m_high"), 1)

            with act.Fori(0, KD // 2 - 1) as i:
                att_turn(i, None)
            att_turn(KD // 2 - 1, PAN_OUT - 4)
            with act.Fori(0, KD // 4) as i:
                for j in range(4):
                    q = PAN_OUT + j + LOOK
                    hi(q % RING, q % RAW, 8, None, i * 32 + 16 * (q // RAW + 1), i * 4 + (q - RING + 1))

            def norm(n):
                g_v, b_v = ((ln1g, ln1b), (ln2g, ln2b))[n]
                for c in range(KD):
                    act.wait_ge(sem("centred"), KD * n + c + 1)
                    if c >= 2:
                        act.wait_ge(sem("square_summed"), KD * n + c - 1)
                    A(tg[:, c % 2, :], z[:, c, :], ACT.Square).then_inc(sem("squared"), 1)
                act.wait_ge(sem("var_done"), n + 1)
                A(tw[:, 1, :], tw[:, 0, :], ACT.Sqrt).then_inc(sem("std_done"), 1)
                for c in range(KD):
                    act.wait_ge(sem("scaled"), KD * n + c + 1)
                    if n == 0:
                        A(x_hi[:, c, :], z[:, c, :], ACT.Identity, bias=b_v[:, c:c + 1],
                          scale=g_v[:, c:c + 1]).then_inc(sem("x1_high"), 1)

            norm(0)

            def ff_turn(i, looks):
                for j in range(4):
                    if looks is None:
                        q = PAN_FF + j + LOOK
                        hi(q % RING, q % RAW, 8, None, i * 32 + 16 * (q // RAW + 1), i * 4 + (q - RING + 1))
                    else:
                        hi_static(looks + j + LOOK)
                    act.wait_ge(panel_done, i * 4 + (PAN_FF + j + 1))
                    if j % 2 == 0:
                        A(rows(tg[:, j // 2, :]), pair(j), ACT.Tanh, scale=0.5).then_inc(sem("f_tanh"), 1)
                    else:
                        act.wait_ge(drained[j], i * 1 + ((PAN_FF // 2 if j == 1 else 0) + 1))
                        A(f_hi[:, bass.ds(i * 2 + j // 2, 1), :], tw[:, bass.ds(j // 2, 1), :], ACT.Copy,
                          scale=0.5).then_inc(sem("f_high"), 1)

            with act.Fori(0, KF // 2 - 1) as i:
                ff_turn(i, None)
            ff_turn(KF // 2 - 1, PAN_DOWN - 4)

            with act.Fori(0, KD - 1) as i:
                for j in range(4):
                    q = PAN_DOWN + j + LOOK
                    hi(q % RING, q % RAW, panel_blocks(q), None, i * 32 + 16 * (q // RAW + 1), i * 4 + (q - RING + 1))
            for j in range(4):
                hi_static(PAN_END - 4 + j + LOOK)
            norm(1)
            for i in range(NT + 1):
                n = P if i < NT else DEC
                act.wait_ge(sem("y_turned"), i + 1)
                if i >= 2:
                    act.wait_ge(sem(f"y_sent{i - 2}"), 16)
                A(ytok[i % 2][0:n, :].rearrange("p (h c) -> p h c", h=2), ps[0:n, 2 * (i % 4):2 * (i % 4) + 2, :],
                  ACT.Copy).then_inc(sem("y_staged"), 1)

        @block.vector
        def _(dve):
            V = nc.vector
            count = [0]
            told = {}

            def link(ins):
                count[0] += 1
                ins.then_inc(sem("dve_seq"), 1)
                dve.wait_ge(sem("dve_seq"), count[0])

            def tell(ins, name):
                told[name] = told.get(name, 0) + 1
                ins.then_inc(sem(name), 1)
                dve.wait_ge(sem(name), told[name])

            def cmul(out_r, out_i, a_r, a_i, s_r, s_i, conj, u, w):
                tt = V.tensor_tensor
                link(tt(u, a_r, s_r, ALU.mult))
                link(tt(w, a_i, s_i, ALU.mult))
                link(tt(out_r, u, w, ALU.add if conj else ALU.subtract))
                link(tt(u, a_i, s_r, ALU.mult))
                link(tt(w, a_r, s_i, ALU.mult))
                link(tt(out_i, u, w, ALU.subtract if conj else ALU.add))

            for c in range(KD):
                dve.wait_ge(sem("x_high"), c + 1)
                tell(V.tensor_tensor(x_lo[:, c, 0:SEQ], ps[:, 4 + c % 4, :], x_hi[:, c, 0:SEQ].bitcast(F32), ALU.subtract),
                     "x_split")
            dve.wait_ge(sem("x_high"), KD + 1)
            tell(V.tensor_tensor(x_lo[:, :, SEQ:T], ps[:, 0, 0:DEC * KD].rearrange("p (c b) -> p c b", b=DEC),
                                 x_hi[:, :, SEQ:T].bitcast(F32), ALU.subtract), "x_split")

            LR, LI, ST, MAG, RED, RHALF, SIN, SHALF = range(8)
            TMP, TMP2, TMP3, COS, LBR, LBI, CFR, CFI, L2R, L2I, L4R, L4I, L8R, L8I, PR, PI, A8, TH, KI = range(8, 27)

            def v(n):
                return par[:, n, :]

            dve.wait_ge(par_in, 16 * N_PAR)
            tell(V.tensor_copy(lrow[:, 2, :].rearrange("a (g p) -> a g p", g=2),
                               srow[:, :].unsqueeze(2).broadcast_to([16, 2, E])), "steps_spread")

            def turn_params():
                dve.wait_ge(sem("lam_turned"), 1)
                tell(V.tensor_copy(par[:, 0:3, :], ps[:, 4, 0:48].rearrange("p (n a) -> p n a", n=3)), "par_read")
                dve.wait_ge(sem("c_turned"), 1)
                for n in range(2):
                    src = ps[:, 5 + n, :].rearrange("p (a g h) -> p a g h", g=2, h=16)
                    for g in range(2):
                        r = slice(64 * g, 64 * g + 64)
                        ins = V.tensor_scalar(cc[r, n, :, :], src[r, :, g, :], (1.0, -1.0)[n], None, ALU.mult)
                        if n == 1 and g == 1:
                            tell(ins, "par_read")
                        else:
                            link(ins)
                dve.wait_ge(sem("h0_turned"), 1)
                tell(V.tensor_copy(h0[:, :, :, :], ps[:, 7, 0:256].rearrange("p (n b a) -> p n b a", n=2, b=DEC)), "par_read")

            def params():
                def ts(out, a, s1, s2, o1, o2):
                    link(V.tensor_scalar(v(out), v(a), s1, s2, o1, o2))

                def tt(out, a, b, op):
                    link(V.tensor_tensor(v(out), v(a), v(b), op))

                def stt(out, a, s, b, o1, o2):
                    link(V.scalar_tensor_tensor(v(out), v(a), s, v(b), o1, o2))

                def exp(out, a):
                    ts(a, a, -87.0, 88.0, ALU.max, ALU.min)
                    ts(TMP, a, math.log2(math.e), ROUND, ALU.mult, ALU.add)
                    ts(TMP, TMP, -ROUND, None, ALU.add, ALU.bypass)
                    stt(TMP2, TMP, -0.693359375, a, ALU.mult, ALU.add)
                    stt(TMP2, TMP, 2.12194440e-4, TMP2, ALU.mult, ALU.add)
                    ts(TMP3, TMP2, 1 / 5040.0, None, ALU.mult, ALU.bypass)
                    for f in (720.0, 120.0, 24.0, 6.0, 2.0, 1.0):
                        stt(TMP3, TMP3, 1 / f, TMP2, ALU.add, ALU.mult)
                    link(V.tensor_scalar(v(KI).bitcast(I32), v(TMP), 127.0, 2.0 ** 23, ALU.add, ALU.mult))
                    stt(out, TMP3, 1.0, KI, ALU.add, ALU.mult)

                exp(ST, ST)
                tt(MAG, LR, ST, ALU.mult)
                exp(MAG, MAG)
                tt(TH, LI, ST, ALU.mult)
                ts(TMP, TH, 1 / (2 * math.pi), ROUND, ALU.mult, ALU.add)
                ts(TMP, TMP, -ROUND, None, ALU.add, ALU.bypass)
                c1 = 6.28125
                c2 = float((np.float32(2 * math.pi - c1).view(np.uint32) & np.uint32(0xFFFFF000)).view(np.float32))
                c3 = 2 * math.pi - c1 - c2
                stt(RED, TMP, -c1, TH, ALU.mult, ALU.add)
                stt(RED, TMP, -c2, RED, ALU.mult, ALU.add)
                stt(RED, TMP, -c3, RED, ALU.mult, ALU.add)
                ts(RHALF, RED, 0.5, None, ALU.mult, ALU.bypass)
                tell(V.tensor_scalar(v(RED), v(RED), 3.1415925, -3.1415925, ALU.min, ALU.max), "angle_done")
                dve.wait_ge(sem("sin_done"), 2)
                tt(TMP, SHALF, SHALF, ALU.mult)
                ts(COS, TMP, -2.0, 1.0, ALU.mult, ALU.add)
                tt(LBR, MAG, COS, ALU.mult)
                tt(LBI, MAG, SIN, ALU.mult)
                ts(TMP3, LBR, -1.0, None, ALU.add, ALU.bypass)
                cmul(v(CFR), v(CFI), v(TMP3), v(LBI), v(LR), v(LI), True, v(TMP), v(TMP2))
                tt(TMP, LR, LR, ALU.mult)
                tt(TMP2, LI, LI, ALU.mult)
                tt(TMP, TMP, TMP2, ALU.add)
                link(V.reciprocal(v(TMP), v(TMP)))
                tt(CFR, CFR, TMP, ALU.mult)
                tt(CFI, CFI, TMP, ALU.mult)
                for a, b in ((LBR, L2R), (L2R, L4R), (L4R, L8R)):
                    cmul(v(b), v(b + 1), v(a), v(a + 1), v(a), v(a + 1), False, v(TMP), v(TMP2))
                for a, b in ((MAG, A8), (A8, A8), (A8, A8)):
                    tt(b, a, a, ALU.mult)
                link(V.tensor_copy(v(PR), v(COS)))
                link(V.tensor_copy(v(PI), v(SIN)))
                for _ in range(3):
                    unit_square()
                s = [1, 16, 16]
                a_r, a_i = (bbar[:, n, :, :] for n in range(2))
                cf = [v(n).unsqueeze(2).broadcast_to([P, 16, 16]) for n in (CFR, CFI)]
                w1 = t1[:, 0:256].rearrange("p (a h) -> p a h", a=16)
                w2 = t2[:, 0:256].rearrange("p (a h) -> p a h", a=16)
                cmul(a_r, a_i, braw[:, 0, :, :], braw[:, 1, :, :], cf[0], cf[1], False, w1, w2)
                for n in range(2):
                    link(V.memset(bp[n][:, 0, :, :], 0.0))
                link(V.memset(kbd[0][:, :, :], 0.0))
                link(V.memset(hst[:, :, :, 0:1], 0.0))

            def unit_square():
                def tt(out, a, b, op):
                    link(V.tensor_tensor(v(out), v(a), v(b), op))
                tt(TMP, PR, PR, ALU.mult)
                tt(TMP2, PI, PI, ALU.mult)
                tt(TMP3, PR, PI, ALU.mult)
                tt(PR, TMP, TMP2, ALU.subtract)
                link(V.tensor_scalar(v(PI), v(TMP3), 2.0, None, ALU.mult))
                tt(TMP, PR, PR, ALU.mult)
                tt(TMP2, PI, PI, ALU.mult)
                tt(TMP, TMP, TMP2, ALU.add)
                link(V.tensor_scalar(v(TMP), v(TMP), -0.5, 1.5, ALU.mult, ALU.add))
                tt(PR, PR, TMP, ALU.mult)
                tt(PI, PI, TMP, ALU.mult)

            def powers(ct):
                m = ct % 2
                aq = slice(4 * ct, 4 * ct + 4)
                if ct == 0:
                    for k in range(6):
                        link(V.tensor_copy(rotk[:, k, 0, :], v(PR)))
                        link(V.tensor_copy(rotk[:, k, 1, :], v(PI)))
                        if k < 5:
                            unit_square()
                else:
                    dve.wait_ge(sem("k_formed"), ct)
                    if ct == 1:
                        link(V.memset(kbd[1][:, :, :], 0.0))
                    if ct >= 2:
                        dve.wait_ge(sem("y_formed"), ct - 1)

                def lam(n, shape):
                    s = [par[:, L, aq] for L in (n, n + 1)]
                    if len(shape) == 3:
                        return [a.unsqueeze(2).broadcast_to(shape) for a in s]
                    return [a.unsqueeze(1).unsqueeze(3).broadcast_to(shape) for a in s]

                for n in range(2):
                    if ct == 0 or ct == 1:
                        link(V.memset(cp[m][n][:, 0, :, :], 0.0))
                    for g in range(2):
                        r = slice(64 * g, 64 * g + 64)
                        link(V.tensor_copy(bp[n][r, 0, :, 16 * g:16 * g + 16], bbar[r, n, aq, :]))
                        link(V.tensor_copy(cp[m][n][r, 0, :, 16 * g:16 * g + 16], cc[r, n, aq, :]))
                for (a_r, a_i), conj, top in (((bp[0], bp[1]), False, 8), (tuple(cp[m]), True, 9)):
                    for k, name in ((1, LBR), (2, L2R), (4, L4R), (8, L8R)):
                        if k >= top:
                            continue
                        c = min(k, top - k)
                        shape = [P, c, 4, 32]
                        w1, w2 = (x[:, 0:128 * c].rearrange("p (k q c) -> p k q c", k=c, q=4) for x in (t1, t2))
                        s_r, s_i = lam(name, shape)
                        args = [x[:, k:k + c, :, :] for x in (a_r, a_i)] + [x[:, 0:c, :, :] for x in (a_r, a_i)]
                        cmul(*args, s_r, s_i, conj, w1, w2)
                link(V.memset(ein[ct % 2][:, 0, :, 0:1], 1.0))
                link(V.memset(ein[ct % 2][:, 1, :, 0:1], 0.0))
                for k in range(6):
                    c = 1 << k
                    s_r, s_i = (rotk[:, k, n, aq].unsqueeze(2).broadcast_to([P, 4, c]) for n in range(2))
                    w1, w2 = (x[:, 0:4 * c].rearrange("p (q c) -> p q c", q=4) for x in (t1, t2))
                    cmul(ein[ct % 2][:, 0, :, c:2 * c], ein[ct % 2][:, 1, :, c:2 * c], ein[ct % 2][:, 0, :, 0:c], ein[ct % 2][:, 1, :, 0:c],
                         s_r, s_i, False, w1, w2)
                link(V.tensor_copy(dec0[ct % 2][:, :, :], v(A8)[:, aq].unsqueeze(2).broadcast_to([P, 4, NC])))
                tell(V.memset(dec0[ct % 2][:, :, 0:1], 0.0), "powers_done")

            def ssm_prep(ct):
                dve.wait_ge(sem("k_formed"), ct + 1)
                for q in range(4):
                    r = slice(32 * q, 32 * q + 32)
                    ins = V.tensor_copy(kbd[ct % 2][r, :, 32 * q:32 * q + 32],
                                        ps[r, 4, 0:256].rearrange("p (j c) -> p j c", j=CH))
                    if q < 3:
                        link(ins)
                    else:
                        tell(ins, "k_copied")

            def ssm_in(ct):
                aq = slice(4 * ct, 4 * ct + 4)
                dve.wait_ge(sem("v_copied"), ct + 1)
                if ct >= 1:
                    dve.wait_ge(sem("state_turned"), ct)
                w1, w2 = (x[:, 0:4 * NC].rearrange("p (q c) -> p q c", q=4) for x in (t1, t2))
                e_r, e_i = ein[ct % 2][:, 0, :, :], ein[ct % 2][:, 1, :, :]
                cmul(wrot[:, 0, :, :], wrot[:, 1, :, :], vsb[:, :, 0:NC], vsb[:, :, 72:72 + NC], e_r, e_i, True, w1, w2)
                d0 = dec0[ct % 2][:, :, :].rearrange("p q c -> p (q c)")
                for n in range(2):
                    link(V.tensor_tensor_scan(grot[:, n, :, :].rearrange("p q c -> p (q c)"), d0,
                                              wrot[:, n, :, :].rearrange("p q c -> p (q c)"), 0.0, ALU.mult, ALU.add))
                cmul(hst[:, 0, :, 1:65], hst[:, 1, :, 1:65], grot[:, 0, :, :], grot[:, 1, :, :], e_r, e_i, False, w1, w2)
                d1, d2 = (x[:, 0:32].rearrange("p (q b) -> p q b", q=4) for x in (t1, t2))
                hr, hi_ = (h0[:, n, :, aq].rearrange("p b q -> p q b") for n in range(2))
                lr, li = (par[:, L, aq].unsqueeze(2).broadcast_to([P, 4, DEC]) for L in (LBR, LBI))
                cmul(hst[:, 0, :, 65:73], hst[:, 1, :, 65:73], hr, hi_, lr, li, False, d1, d2)
                link(V.tensor_tensor(hst[:, 0, :, 65:73], hst[:, 0, :, 65:73], vsb[:, :, 64:72], ALU.add))
                link(V.tensor_tensor(hst[:, 1, :, 65:73], hst[:, 1, :, 65:73], vsb[:, :, 136:144], ALU.add))
                tell(V.tensor_copy(hfin[:, :, :].rearrange("p n (j q) -> p n q j", q=4), hst[:, :, :, 64:73]), "h_done")

            def ssm_out(ct):
                dve.wait_ge(sem("y_formed"), ct + 1)
                link(V.scalar_tensor_tensor(u_ssm[:, ct, 0:SEQ], u_ssm[:, ct, 0:SEQ], dskip[:, ct:ct + 1], ps[:, 4, :],
                                            ALU.mult, ALU.add))
                tell(V.scalar_tensor_tensor(u_ssm[:, ct, SEQ:T], u_ssm[:, ct, SEQ:T], dskip[:, ct:ct + 1],
                                            ps[:, 5, 0:DEC], ALU.mult, ALU.add), "y_read")

            def gelu(ct):
                u, a = u_ssm[:, ct, :], tw[:, 0, :]
                link(V.tensor_tensor(a, u, u, ALU.mult))
                link(V.tensor_scalar(a, a, 0.044715, 1.0, ALU.mult, ALU.add))
                tell(V.tensor_tensor(a, a, u, ALU.mult), "g_in")
                dve.wait_ge(sem("g_tanh"), ct + 1)
                tell(V.scalar_tensor_tensor(u, tw[:, 1, :], 1.0, u, ALU.add, ALU.mult), "gelu_done")

            def low_rows(dst, high, ct, scale, name):
                link(V.scalar_tensor_tensor(dst[:, ct, 0:SEQ].rearrange("p (c s) -> p c s", s=CH),
                                            u_ssm[:, ct, 0:SEQ].rearrange("p (s c) -> p c s", s=CH), scale,
                                            high[:, ct, 0:SEQ].bitcast(F32).rearrange("p (c s) -> p c s", s=CH),
                                            ALU.mult, ALU.subtract))
                tell(V.scalar_tensor_tensor(dst[:, ct, SEQ:T], u_ssm[:, ct, SEQ:T], scale,
                                            high[:, ct, SEQ:T].bitcast(F32), ALU.mult, ALU.subtract), name)

            def gelu_split():
                for ct in range(4):
                    dve.wait_ge(sem("gelu_high"), ct + 1)
                    low_rows(ys_lo, ys_hi, ct, 0.5, "gelu_split_done")

            def pool_diff():
                dve.wait_ge(consts, 3)
                dve.wait_ge(vec_in, 16 * N_VEC)
                for g in (3, 2, 1, 0):
                    link(V.tensor_scalar(rcnt[:, g, :], rcnt[:, 0, :], float(POOL_W[g]), None, ALU.min))
                link(V.reciprocal(rcnt[:, :, :], rcnt[:, :, :]))
                for g, w in enumerate(POOL_W):
                    if g == 0:
                        dve.wait_ge(drained[(PAN_POOL + 2) % 2], (PAN_POOL + 2) // 2 + 1)
                        dve.wait_ge(drained[(PAN_POOL + 3) % 2], (PAN_POOL + 3) // 2 + 1)
                        link(V.memset(upool[:, :, 0:16], 0.0))
                        dve.wait_ge(sem("psum_old"), 1)
                        tell(V.tensor_copy(oldsum[:, :, :], ps[:, 4, 0:32].rearrange("p (g b) -> p g b", g=4)), "psum_old_read")
                        dve.wait_ge(sem("pool_turned"), 1)
                    src = upool[:, g, 0:16 + SEQ]
                    n, size = 1, SEQ + 16
                    bufs = [wide[:, 0, :], wide[:, 1, :]]
                    cur, turn = src, 0
                    while n < w:
                        out = bufs[turn]
                        link(V.tensor_tensor(out[:, 2 * n - 1:size], cur[:, 2 * n - 1:size], cur[:, n - 1:size - n], ALU.add))
                        cur, turn, n = out, 1 - turn, 2 * n
                    tot = cur[:, 16:16 + SEQ]
                    link(V.tensor_tensor(small[:, 16:32], tot[:, 0:16], rcnt[:, g, :], ALU.mult))
                    link(V.tensor_tensor(oldsum[:, g, :], oldsum[:, g, :], upool[:, g, 16 + SEQ:16 + T], ALU.add))
                    link(V.scalar_tensor_tensor(upool[:, g, 16 + SEQ:16 + T], oldsum[:, g, :], 1.0 / w,
                                                upool[:, g, 16 + SEQ:16 + T], ALU.mult, ALU.subtract))
                    link(V.scalar_tensor_tensor(upool[:, g, 32:16 + SEQ], tot[:, 16:SEQ], 1.0 / w,
                                                upool[:, g, 32:16 + SEQ], ALU.mult, ALU.subtract))
                    tell(V.tensor_tensor(upool[:, g, 16:32], small[:, 16:32], upool[:, g, 16:32], ALU.subtract), "diff_done")

            def pool_mix():
                for g in range(4):
                    dve.wait_ge(sem("pool_mixed"), g + 1)
                    tell(V.tensor_scalar(rows(tw[:, g % 2, :]), pair(2 + g % 2), pscale[:, g:g + 1], None, ALU.mult),
                         "pool_scaled")
                    dve.wait_ge(sem("pool_high"), g + 1)
                    tell(V.tensor_tensor(yp_lo[:, g, :], tw[:, g % 2, :], yp_hi[:, g, :].bitcast(F32), ALU.subtract), "pool_split")

            def to_tokens(hc):
                dve.wait_ge(sem("v_turned"), NT * (hc + 1))
                for n, src in enumerate((q_t[:, hc, :, SEQ:T], k_t[:, hc, :, SEQ:T], v_t[:, :, SEQ:T])):
                    tell(V.tensor_copy(dexp[:, n, hc, :, :].rearrange("p g (b h) -> p g b h", h=4),
                                       src.unsqueeze(3).broadcast_to([P, 3, DEC, 4])), "decode_kept")

            def decode_v():
                rep = ident[0:32, 0:32].rearrange("p (b h) -> p h b", h=4)
                link(V.tensor_reduce(small[0:32, 4:8], rep, AX.X, ALU.add))
                link(V.tensor_copy(hmask[:, :, :], small[0:32, 4:8].unsqueeze(2).broadcast_to([32, 4, E])))
                for g in range(N_GROUPS):
                    for h in range(HEADS):
                        link(V.memset(small[0:32, 32 + 4 * g + h:33 + 4 * g + h], -8.0 * SLOPE[g][h]))
                for g in range(N_GROUPS):
                    link(V.tensor_tensor(small[0:32, 12:16], small[0:32, 4:8], small[0:32, 32 + 4 * g:36 + 4 * g], ALU.mult))
                    link(V.tensor_reduce(small[0:32, 44 + g:45 + g], small[0:32, 12:16], AX.X, ALU.add))

            def decode_scores():
                dve.wait_ge(sem("reps_done"), 3)
                for g in range(N_GROUPS):
                    w1 = tw[0:32, 0, 0:256]
                    link(V.tensor_tensor(w1, reps[0][:, g, :], reps[1][:, g, :], ALU.mult))
                    link(V.tensor_tensor(w1, w1, hmask[:, :, :].rearrange("p h e -> p (h e)"), ALU.mult))
                    link(V.tensor_reduce(sc32[:, 288 + g:289 + g], w1, AX.X, ALU.add))
                for g in range(N_GROUPS):
                    keys = P if g < 2 else 32
                    dve.wait_ge(sem(f"cache_in{g}"), 16)
                    buf = cbuf[g % 2]
                    for b2 in range(4):
                        n = 4 * g + b2
                        dve.wait_ge(sem("q_spread"), n + 1)
                        tell(V.tensor_tensor(buf[0:keys, 2 * b2:2 * b2 + 2, :], buf[0:keys, 2 * b2:2 * b2 + 2, :],
                                             ps[0:keys, 4 + n % 4, :].rearrange("p (b c) -> p b c", b=2), ALU.mult), "qk_read")
                    tell(V.tensor_reduce(s32[0:keys, g, :], buf[0:keys, :, :].rearrange("p b (h e) -> p (b h) e", h=4),
                                         AX.X, ALU.add), "cache_scored")
                dve.wait_ge(sem("s_turned"), 1)
                for g in range(N_GROUPS):
                    keys = P if g < 2 else 32
                    c = slice(P * g, P * g + keys)
                    link(V.scalar_tensor_tensor(sc32[:, c], dist32[:, c], small[0:32, 44 + g:45 + g], ps[0:32, 4, c],
                                                ALU.mult, ALU.add))

            def decode_softmax():
                link(V.reduce_max(small[0:32, 0:1], sc32[:, 0:291], AX.X))
                tell(V.tensor_scalar(small[0:32, 1:2], small[0:32, 0:1], -0.125, None, ALU.mult), "s32_done")
                dve.wait_ge(sem("e32_done"), 1)
                link(V.reciprocal(small[0:32, 3:4], small[0:32, 2:3]))
                tell(V.tensor_scalar(sc32[:, 0:291], sc32[:, 0:291], small[0:32, 3:4], None, ALU.mult), "p_done")
                for g in range(N_GROUPS):
                    ins = V.tensor_scalar(diag32[:, g, :], ident[0:32, 0:32], sc32[:, 288 + g:289 + g], None, ALU.mult)
                ins.then_inc(sem("diag_done"), 1)

            def decode_out():
                dve.wait_ge(sem("od_high"), 1)
                for h in range(2):
                    r = slice(64 * h, 64 * h + 64)
                    ins = V.tensor_tensor(ya_lo[r, :, SEQ:T], ps[r, 6:8, 0:16].rearrange("p c (b h) -> p c b h", h=2)[:, :, :, h],
                                          ya_hi[r, :, SEQ:T].bitcast(F32), ALU.subtract)
                    if h == 0:
                        link(ins)
                    else:
                        tell(ins, "decode_done")

            def bias():
                dve.wait_ge(sem("td_base"), 1)
                for g in (2, 1):
                    m = DILATION[g] - 1
                    w = tw[:, 0, 0:512].bitcast(I32)
                    link(V.tensor_scalar(w, tdi[:, :], m, None, ALU.bitwise_and))
                    link(V.tensor_scalar(tw[:, 1, 0:512], w, 1.0, BIG, ALU.min, ALU.mult))
                    link(V.tensor_tensor(td[:, g, :], tw[:, 1, 0:512], td[:, 1, :], ALU.add))

            def scores(n):
                h, i = ATT_STEPS[n]
                col = 0
                if n >= 2:
                    dve.wait_ge(sem("o_high"), n - 1)
                for g in range(N_GROUPS):
                    first = 0 if g else max(0, i - 1)
                    w = P * (i + 1 - first)
                    dve.wait_ge(sem("s_formed"), 3 * n + g + 1)
                    c0 = 384 + P * (first - i)
                    tell(V.scalar_tensor_tensor(sc[:, n % 2, col:col + w], td[:, g, c0:c0 + w], -8.0 * SLOPE[g][h],
                                                ps[:, 4 + g % 2, 0:w], ALU.mult, ALU.add), "scored")
                    col += w
                link(V.reduce_max(small[:, 12 + n % 2:13 + n % 2], sc[:, n % 2, 0:col], AX.X))
                tell(V.tensor_scalar(small[:, 8 + n % 2:9 + n % 2], small[:, 12 + n % 2:13 + n % 2], -0.125, None, ALU.mult),
                     "max_done")
                dve.wait_ge(sem("exp_done"), n + 1)
                link(V.reciprocal(small[:, 14 + n % 2:15 + n % 2], small[:, 10 + n % 2:11 + n % 2]))
                tell(V.tensor_scalar(sc[:, n % 2, 0:col], sc[:, n % 2, 0:col], small[:, 14 + n % 2:15 + n % 2], None,
                                     ALU.mult), "p_normed")

            def probs(n):
                h, i = ATT_STEPS[n]
                r = slice(64 * (h % 2), 64 * (h % 2) + 64)
                dve.wait_ge(sem("o_high"), n + 1)
                ins = V.tensor_tensor(ya_lo[r, h // 2, P * i:P * i + P], ps[r, 6, 0:P],
                                      ya_hi[r, h // 2, P * i:P * i + P].bitcast(F32), ALU.subtract)
                tell(ins, "o_split")

            def branch(p):
                n = (p - PAN_POOLBR) // 2 if p < PAN_QKV else (p - PAN_SSMBR) // 2
                dve.wait_ge(panel_done, p + 1)
                dve.wait_ge(drained[0], p // 2 + 1)
                if p < PAN_QKV:
                    V.scalar_tensor_tensor(rows(z[:, n, :]), rows(tg[:, n % 2, :]), 1.0, pair(1), ALU.add, ALU.mult
                                           ).then_inc(drained[1], 1)
                else:
                    link(V.scalar_tensor_tensor(rows(tw[:, 0, :]), rows(tg[:, n % 2, :]), 1.0, pair(1), ALU.add, ALU.mult))
                    V.tensor_tensor(z[:, n, :], z[:, n, :], tw[:, 0, :], ALU.add).then_inc(drained[1], 1)

            def glu(p):
                n = p - PAN_GLU
                dve.wait_ge(drained[p % 2], p // 2 + 1)
                t = tg[:, n % 2, :]
                link(V.scalar_tensor_tensor(u_ssm[:, n, 0:SEQ].rearrange("p (s c) -> p c s", s=CH),
                                            t[:, 0:SEQ].rearrange("p (c s) -> p c s", s=CH), 1.0,
                                            u_ssm[:, n, 0:SEQ].rearrange("p (s c) -> p c s", s=CH), ALU.add, ALU.mult))
                tell(V.scalar_tensor_tensor(u_ssm[:, n, SEQ:T], t[:, SEQ:T], 1.0, u_ssm[:, n, SEQ:T], ALU.add, ALU.mult),
                     "glu_used")

            todo = {"turn_params": lambda _: turn_params(), "params": lambda _: params(), "powers": powers, "ssm_prep": ssm_prep, "ssm_in": ssm_in,
                    "ssm_out": ssm_out, "gelu": gelu, "gelu_split": lambda _: gelu_split(),
                    "pool_diff": lambda _: pool_diff(), "pool_mix": lambda _: pool_mix(), "to_tokens": to_tokens,
                    "decode_v": lambda _: decode_v(), "decode_scores": lambda _: decode_scores(),
                    "decode_softmax": lambda _: decode_softmax(), "decode_out": lambda _: decode_out(),
                    "bias": lambda _: bias(), "scores": scores, "probs": probs}
            for p in range(PAN_ATTBR):
                if (PAN_POOLBR <= p < PAN_QKV or p >= PAN_SSMBR) and p % 2:
                    branch(p)
                if PAN_GLU <= p < PAN_SSMBR:
                    glu(p)
                for step in AFTER.get(p, []):
                    name, arg = step if isinstance(step, tuple) else (step, None)
                    if name in todo:
                        todo[name](arg)
                if p == PAN_SSMBR - 1:
                    for ct in range(4):
                        dve.wait_ge(sem("ys_high"), ct + 1)
                        low_rows(ys_lo, ys_hi, ct, 0.25, "ys_split")
            with dve.Fori(0, KD // 2) as i:
                for j in range(2):
                    c = bass.ds(i * 2 + j, 1)
                    dve.wait_ge(panel_done, i * 4 + (PAN_ATTBR + 2 * j + 2))
                    dve.wait_ge(drained[0], i * 2 + (PAN_ATTBR // 2 + j + 1))
                    V.scalar_tensor_tensor(rows(tw[:, j, :]), rows(tg[:, j, :]), 1.0, pair(1), ALU.add, ALU.mult
                                           ).then_inc(drained[1], 1)
                    dve.wait_ge(drained[1], i * 2 + (PAN_ATTBR // 2 + j + 1))
                    V.tensor_tensor(z[:, c, :], z[:, c, :], tw[:, j:j + 1, :], ALU.add).then_inc(sem("m_summed"), 1)
                    dve.wait_ge(sem("m_high"), i * 2 + (j + 1))
                    V.scalar_tensor_tensor(m_lo[:, c, :], z[:, c, :], 0.5, m_hi[:, c, :].bitcast(F32), ALU.mult,
                                           ALU.subtract).then_inc(sem("m_split"), 1)

            def residual(i, j, p_ready, per, base_drained, dest_base):
                c = bass.ds(i * per + j, 1)
                dve.wait_ge(panel_done, p_ready)
                b = j % 2
                V.scalar_tensor_tensor(rows(tw[:, b, :]), x_hi[:, c, :].bitcast(F32).rearrange("p o (h t) -> p (o h) t", h=2),
                                       ALPHA, pair(b), ALU.mult, ALU.add).then_inc(drained[b], 1)
                dve.wait_ge(drained[b], base_drained)
                V.scalar_tensor_tensor(z[:, c, :], x_lo[:, c, :].bitcast(F32), ALPHA, tw[:, b:b + 1, :], ALU.mult, ALU.add
                                       ).then_inc(sem("z_done"), 1)

            with dve.Fori(0, KD // 4) as i:
                for j in range(4):
                    residual(i, j, i * 4 + (PAN_OUT + j + 1), 4, i * 2 + ((PAN_OUT + j) // 2 + 1), 0)

            def norm(n):
                g_v, b_v = ((ln1g, ln1b), (ln2g, ln2b))[n]
                dve.wait_ge(sem("sum_done"), n + 1)
                link(V.tensor_scalar(rows(tw[:, 0, :]), pair(2), 1.0 / D, None, ALU.mult))
                for c in range(KD):
                    tell(V.tensor_tensor(z[:, c, :], z[:, c, :], tw[:, 0, :], ALU.subtract), "centred")
                dve.wait_ge(sem("square_summed"), KD * (n + 1))
                tell(V.tensor_scalar(rows(tw[:, 0, :]), pair(3), 1.0 / D, EPS, ALU.mult, ALU.add), "var_done")
                dve.wait_ge(sem("std_done"), n + 1)
                link(V.reciprocal(tw[:, 0, :], tw[:, 1, :]))
                for c in range(KD):
                    tell(V.tensor_tensor(z[:, c, :], z[:, c, :], tw[:, 0, :], ALU.mult), "scaled")
                    if n == 0:
                        link(V.tensor_scalar(tw[:, 1, :], z[:, c, :], g_v[:, c:c + 1], b_v[:, c:c + 1], ALU.mult, ALU.add))
                        dve.wait_ge(sem("x1_high"), c + 1)
                        tell(V.tensor_tensor(x_lo[:, c, :], tw[:, 1, :], x_hi[:, c, :].bitcast(F32), ALU.subtract), "x1_split")
                    else:
                        tell(V.tensor_scalar(z[:, c, :], z[:, c, :], g_v[:, c:c + 1], b_v[:, c:c + 1], ALU.mult, ALU.add),
                             "y_done")

            norm(0)

            with dve.Fori(0, KF // 2) as i:
                for j in range(2):
                    c = bass.ds(i * 2 + j, 1)
                    dve.wait_ge(sem("f_tanh"), i * 2 + (j + 1))
                    V.scalar_tensor_tensor(rows(tw[:, j, :]), rows(tg[:, j, :]), 1.0, pair(2 * j), ALU.add, ALU.mult
                                           ).then_inc(drained[2 * j], 1)
                    dve.wait_ge(drained[2 * j], i * 1 + ((PAN_FF // 2 if j == 0 else 0) + 1))
                    dve.wait_ge(panel_done, i * 4 + (PAN_FF + 2 * j + 2))
                    V.tensor_tensor(rows(tw[:, j, :]), rows(tw[:, j, :]), pair(2 * j + 1), ALU.mult).then_inc(drained[2 * j + 1], 1)
                    dve.wait_ge(sem("f_high"), i * 2 + (j + 1))
                    V.scalar_tensor_tensor(f_lo[:, c, :], tw[:, j:j + 1, :], 0.5, f_hi[:, c, :].bitcast(F32), ALU.mult,
                                           ALU.subtract).then_inc(sem("f_split"), 1)

            with dve.Fori(0, KD // 2) as i:
                for j in range(2):
                    residual(i, j, i * 8 + (PAN_DOWN + 4 * j + 4), 2, i * 1 + (PAN_FF // 2 + KF // 2 + 1), 0)
            norm(1)


N_PAR, N_VEC = 11, 8
_INS = ['x_prompt', 'x_sample', 'cache_k_w128', 'cache_v_w128', 'cache_k_w512', 'cache_v_w512', 'cache_k_w2048',
        'cache_v_w2048', 'state_pool', 'state_ssm_re', 'state_ssm_im', 'w_in', 'pool_w', 'pool_scale',
        'ssm_lambda_re', 'ssm_lambda_im', 'ssm_b_re', 'ssm_b_im', 'ssm_c_re', 'ssm_c_im', 'ssm_d', 'ssm_log_step',
        'ssm_w_glu', 'w_br_att', 'w_br_pool', 'w_br_ssm', 'w_out', 'ln1_g', 'ln1_b', 'ffn_w_gate', 'ffn_w_up',
        'ffn_w_down', 'ln2_g', 'ln2_b']
_OUTS = ([(1, SEQ, D), (DEC, 1, D)] + [(1, 1, min(w, SEQ), HEADS, E) for w in WINDOWS for _ in range(2)]
         + [(1, 1, PBUF, 512), (1, 1, 32, 64), (1, 1, 32, 64)] + [(1, DEC, 1, HEADS, E)] * 6
         + [(1, DEC, 1, 512), (1, DEC, 32, 64), (1, DEC, 32, 64)])


def kernel(**inputs):
    import numpy as _np
    import concourse.bacc as _bacc
    from concourse.bass_utils import run_bass_kernel_spmd as _run

    nc = _bacc.Bacc("TRN2", target_bir_lowering=False, num_devices=1, dynamic_dma_scratch_size=2048)
    arrays, ins, outs = {}, [], []
    for name in _INS:
        a = _np.ascontiguousarray(inputs[name])
        arrays[f"in_{name}"] = a
        ins.append(nc.dram_tensor(f"in_{name}", a.shape, F32, kind="ExternalInput").ap())
    for n, shape in enumerate(_OUTS):
        outs.append(nc.dram_tensor(f"out_{n}", shape, F32, kind="ExternalOutput").ap())
    build(nc, ins, outs)
    r = _run(nc, [arrays], core_ids=[0])
    return tuple(r.results[0][f"out_{n}"] for n in range(len(_OUTS)))
```

```python
import math
from contextlib import ExitStack

import numpy as np

import concourse.bass as bass
from concourse import mybir

F32 = mybir.dt.float32
F32R = mybir.dt.float32r
I32 = mybir.dt.int32
ALU = mybir.AluOpType
ACT = mybir.ActivationFunctionType
AX = mybir.AxisListType

P = 128
D = 1024
SEQ, DEC = 512, 8
T = SEQ + DEC
HALF = T // 2
KD = D // P
FF = 2816
KF = FF // P
ATT = 768
N_GROUPS, HEADS, E = 3, 4, 64
WINDOWS = (128, 512, 2048)
DILATION = (1, 4, 16)
PAST = 512
BACK = 128
POOL_W = (2, 4, 8, 16)
PBUF = 15
COL_K, COL_V, COL_POOL, COL_SSM, COL_GATE = 768, 1536, 2304, 2816, 3328
NT = SEQ // P
CH = 8
NC = SEQ // CH
ALPHA = 2.0 ** 0.25
EPS = 1e-5
BIG = 1e30
ROUND = 1.5 * 2.0 ** 23
SLOPE = [[2.0 ** (-8.0 * (4 * g + h + 1) / 12) for h in range(HEADS)] for g in range(N_GROUPS)]

PAN_SSM, PAN_POOL, PAN_POOLG, PAN_POOLB, PAN_QKV = 0, 4, 8, 16, 24
PAN_GLU, PAN_SSMBR, PAN_ATTG, PAN_ATTB, PAN_OUT = 42, 46, 62, 70, 78
PAN_FF, PAN_DOWN, PAN_END = 86, 130, 162
DOWN_K = (6, 6, 5, 5)
RAW, RING = 2, 4
SP_LAG = 8
LOOK = 3


def panel_blocks(p):
    if PAN_POOLB <= p < PAN_QKV or PAN_GLU <= p < PAN_SSMBR:
        return 4
    if PAN_SSMBR <= p < PAN_ATTG:
        return 8 if p % 2 == 0 else 4
    if PAN_ATTB <= p < PAN_OUT:
        return 2
    if p >= PAN_DOWN:
        return DOWN_K[(p - PAN_DOWN) % 4]
    return 8


def qkv_panel(p):
    n = p - PAN_QKV
    return (n % 9) // 3, n % 3, n // 9


AFTER = {
    -1: ["turn_params", "params", ("powers", 0)],
    8: ["pool_old", ("ssm_prep", 0), ("powers", 1)], 9: [("ssm_in", 0)], 10: ["pool_diff"], 12: [("ssm_prep", 1)],
    14: [("ssm_out", 0), ("powers", 2)], 15: ["pool_mix", ("ssm_in", 1)],
    16: [("ssm_prep", 2)], 17: [("ssm_out", 1), ("powers", 3)], 18: [("ssm_in", 2)], 19: [("ssm_prep", 3)],
    20: [("ssm_out", 2)], 21: [("ssm_in", 3)], 23: [("ssm_out", 3)],
    24: [("gelu", 0)], 25: [("gelu", 1)], 26: [("gelu", 2)], 27: [("gelu", 3)], 28: ["gelu_split"], 29: ["bias"],
    53: ["decode_consts"],
}
ATT_STEPS = [(h, i) for h in range(HEADS) for i in reversed(range(NT))]


def keys_of(g, i):
    return [kt for kt in range(NT) if kt <= i and (g or kt >= i - 1)]


def quads_of(n):
    blocks = [(g, kt) for g in range(N_GROUPS) for kt in keys_of(g, ATT_STEPS[n][1])]
    return [blocks[m:m + 4] for m in range(0, len(blocks), 4)]


def inner_steps():
    out = {}
    slots = [(p, k) for p in range(PAN_QKV + 9, PAN_ATTB) for k in range(panel_blocks(p))]
    where = 0
    for hc in range(2):
        if hc:
            where = slots.index((PAN_GLU, 0))
        parts = [[("v_tokens", hc, i)] for i in range(NT)] + [[("k_tokens", hc, i)] for i in range(NT)]
        steps = range(8 * hc, 8 * hc + 8)
        for n in list(steps) + [None]:
            before = None if n == steps[0] else (steps[-1] if n is None else n - 1)
            lead = [] if before is None else [("normalise", before)]
            if n is not None:
                parts += [lead + [("scores", n, 0)], [("scores", n, 1)], [("scores", n, 2)], []]
                lead = [("exp", n)]
            if before is not None:
                m = len(quads_of(before))
                if n is None:
                    parts += [lead + [("probs", before, 0)]]
                    lead = []
                else:
                    parts += [[("probs", before, 0)]]
                parts += [[("probs", before, j)] for j in range(1, m)] + [lead + [("probs", before, m)]]
            else:
                parts[-1] = lead
        for part in parts:
            out.setdefault(slots[where], []).extend(part)
            where += 1
        assert slots[where - 1] < (PAN_GLU, 0) or hc and slots[where - 1] < (PAN_DEC, 0)
    out[PAN_DEC, 0], out[PAN_DEC, 3], out[PAN_DEC + 1, 0] = [("decode_rep", 0)], [("decode_rep", 1)], [("decode_rep", 2)]
    out[PAN_DEC + 1, 3] = [("decode_own", 0)]
    at = slots.index((PAN_DEC + 2, 0))
    for n in range(12):
        out[slots[at + n]] = [("decode_spread", n)]
    out[PAN_DEC + 5, 0] = [("decode_scores", 0)]
    out[PAN_DEC + 7, 0] = [("decode_softmax", 0)]
    out[PAN_DEC + 8, 2] = [("decode_out", 0)]
    return out


PAN_DEC = 54
INNER = inner_steps()


def build(nc, ins, outs):
    (x_prompt, x_sample, ck128, cv128, ck512, cv512, ck2048, cv2048, state_pool, ssm_re, ssm_im, w_in, pool_w,
     pool_scale, lam_re, lam_im, b_re, b_im, c_re, c_im, ssm_d, log_step, w_glu, w_br_att, w_br_pool,
     w_br_ssm, w_out, ln1_g, ln1_b, w_gate, w_up, w_down, ln2_g, ln2_b) = ins
    (y_p, y_s, k128_p, v128_p, k512_p, v512_p, k2048_p, v2048_p, pool_p, ssmre_p, ssmim_p,
     k128_s, v128_s, k512_s, v512_s, k2048_s, v2048_s, pool_s, ssmre_s, ssmim_s) = outs
    cache_k, cache_v = (ck128, ck512, ck2048), (cv128, cv512, cv2048)
    kp, vp = (k128_p, k512_p, k2048_p), (v128_p, v512_p, v2048_p)
    ks, vs = (k128_s, k512_s, k2048_s), (v128_s, v512_s, v2048_s)

    ctx = ExitStack()
    with ctx:
        ctx.enter_context(nc.allow_non_contiguous_dma(reason="per-feature vectors: one element per partition"))
        place = [((nc.sbuf_base + 31) // 32) * 32]

        def at(name, shape, dt, offset=None):
            size = 4 * int(np.prod(shape[1:]))
            where = place[0] if offset is None else offset
            if offset is None:
                place[0] += (size + 31) // 32 * 32
            return nc.alloc_sbuf_tensor_at(name, shape, dt, offset=where)

        def region(size):
            where = place[0]
            place[0] += (size + 31) // 32 * 32
            return where

        raw = at("raw", [P, RAW, 1024], F32)
        w_hi = at("w_hi", [P, RING, 1024], F32R)
        w_lo = at("w_lo", [P, RING, 1024], F32R)
        x_hi = at("x_hi", [P, KD, T], F32R)
        x_lo = at("x_lo", [P, KD, T], F32R)
        r_z = region(4 * KD * T)
        z = at("z", [P, KD, T], F32, r_z)
        tg = at("tg", [P, 2, T], F32)
        tw = at("tw", [P, 2, T], F32)
        ident = at("ident", [P, P], F32)
        ones = at("ones", [P, P], F32)
        vecs = at("vecs", [P, 48], F32)
        rcnt = at("rcnt", [P, 4, 16], F32)
        wsel = at("wsel", [P, 4, DEC], F32)
        r_dec = region(6144)
        hmask = at("hmask", [32, 4, E], F32, r_dec)
        sc32 = at("sc32", [32, 3 * P], F32, r_dec + 1024)
        dist32 = at("dist32", [32, 3 * P], F32)
        small = at("small", [P, 64], F32)
        pt32 = at("pt32", [P, 3, 32], F32, r_dec + 2560)
        diag32 = at("diag32", [32, 3, 32], F32, r_dec + 2944)
        s32 = at("s32", [P, 3, 32], F32, r_dec + 3328)
        stage_dec = at("stage_dec", [32, 512], F32)
        ln1g, ln1b, ln2g, ln2b = (vecs[:, 8 * n:8 * n + 8] for n in range(4))
        pscale, dskip = vecs[:, 32:36], vecs[:, 36:40]

        dexp = at("dexp", [P, 3, 2, 3, 32], F32, r_dec + 3712)
        hfin = at("hfin", [P, 2, 36], F32)
        rotk = at("rotk", [P, 6, 2, 16], F32)
        oldsum = at("oldsum", [P, 4, DEC], F32)
        ein1 = at("ein1", [P, 2, 4, NC], F32)
        dec01 = at("dec01", [P, 4, NC], F32)
        r1, r2, r3 = region(36 * 1024), region(18432), region(16640)
        r_u, r_y, r4 = region(8320), region(8320), region(22784)
        assert place[0] <= nc.sbuf_usable_end, place[0]
        xtok = at("xtok", [P, NT, D], F32, r2)
        xstok = at("xstok", [DEC, D], F32, r3)
        bp = at("bp", [P, 2, 4, CH, 32], F32, r1)
        bt = [at(f"bt{n}", [P, 4, 2, P], F32, r1 + 8192 + 4096 * n) for n in range(2)]
        cp = [at(f"cp{m}", [P, CH + 1, 2, 4, 32], F32, (r1 + 16384, r3)[m]) for m in range(2)]
        kbd = [at(f"kbd{m}", [P, CH, P], F32, (r1 + 25600, r3 + 9216)[m]) for m in range(2)]
        bpc = tg[:, :, :].rearrange("p a b -> p (a b)")[:, 0:CH * P].rearrange("p (k n q c) -> p k n q c", k=CH, n=2, q=4)
        cpc = at("cpc", [P, CH + 1, 2, 4, 16], F32, r_dec)
        t1 = at("t1", [P, 1024], F32, r1 + 29696)
        t2 = tw[:, :, :].rearrange("p a b -> p (a b)")
        wide = [a[:, 0:SEQ + 16] for a in (t1, t2)]
        spool = at("spool", [120, 512], F32, r1 + 33792)
        ust = [at(f"ust{ct}", [P, 4, 2, NC + DEC], F32, b) for ct, b in enumerate((r2, r1 + 33792, r4, r4 + 2304))]
        poolw = at("poolw", [P, 4, P], F32, r3 + 13312)
        upool = at("upool", [P, 4, 16 + T], F32, r4)
        ein = [at("ein0", [P, 2, 4, NC], F32, r4 + 8704), ein1]
        dec0 = [at("dec00", [P, 4, NC], F32, r4 + 10752), dec01]
        vsb = at("vsb", [P, 4, 2 * 72], F32, r4 + 11776)
        wrot = at("wrot", [P, 2, 4, NC], F32, r4 + 14080)
        grot = at("grot", [P, 2, 4, NC], F32, r4 + 16128)
        hst = at("hst", [P, 2, 4, 73], F32, r4 + 18176)
        st_out = at("st_out", [36, 2, P], F32, r4 + 20512)
        bbar = at("bbar", [P, 2, 16, 16], F32, r_y)
        cc = at("cc", [P, 2, 16, 16], F32, r_y + 2048)
        h0 = at("h0", [P, 2, DEC, 16], F32, r_y + 4096)
        par = at("par", [P, 34, 16], F32, r_y + 5120)
        braw = at("braw", [P, 2, 16, 16], F32, r1 + 16384)
        craw = at("craw", [P, 2, 4, 2, E], F32, r1 + 18432)
        h0raw = at("h0raw", [P, 2, P], F32, r1 + 22528)
        lrow = at("lrow", [16, 3, P], F32, r1 + 23552)
        srow = at("srow", [16, 2], F32, r1 + 25088)
        u_ssm = at("u_ssm", [P, 4, T], F32, r_u)
        yp_hi = at("yp_hi", [P, 4, T], F32R, r2)
        yp_lo = at("yp_lo", [P, 4, T], F32R, r2 + 8320)
        ys_hi = at("ys_hi", [P, 4, T], F32R, r3)
        ys_lo = at("ys_lo", [P, 4, T], F32R, r3 + 8320)
        q_t = at("q_t", [P, 2, 3, T], F32, r1)
        k_t = at("k_t", [P, 2, 3, T], F32, r1 + 12480)
        v_t = at("v_t", [P, 3, T], F32, r1 + 24960)
        reps = [at("qrep", [32, 3, 256], F32, r1 + 31232), at("krep", [32, 3, 256], F32, r4 + 16384),
                at("vrep", [32, 3, 256], F32, r4 + 19456)]
        v_tok = at("v_tok", [P, NT, 3, 256], F32, r2)
        k_tok = at("k_tok", [P, NT, 3, P], F32, r2 + 12288)
        ya_hi = at("ya_hi", [P, 2, T], F32R, r_y)
        ya_lo = at("ya_lo", [P, 2, T], F32R, r_y + 4160)
        cbuf = [at(f"cbuf{n}", [P, DEC, 256], F32, b) for n, b in enumerate((r1, r1 + 8192, r1 + 16384, r4, r4 + 8192))]
        cbuf.append(cbuf[0])
        tga = at("tga", [P, KD, T], F32, r2)
        td = at("td", [P, 3, 512], F32, r4 + 14336)
        sc = at("sc", [P, 2, 1280], F32, r4)
        ptr = at("ptr", [P, 2, 512], F32, r4 + 10240)
        tdi = at("tdi", [P, 512], I32, r4)
        m_hi = at("m_hi", [P, KD, T], F32R, r1)
        m_lo = at("m_lo", [P, KD, T], F32R, r1 + 16640)
        assert r1 + 33280 <= r2
        f_hi = at("f_hi", [P, KF, T], F32R, r1)
        f_lo = at("f_lo", [P, KF, T], F32R, r1 + 45760)
        ytok = [at(f"ytok{n}", [P, D], F32, r1 + 4096 * n) for n in range(2)]
        assert r1 + 91520 <= r4 + 22784

        ps = ctx.enter_context(nc.psum_tensor("ps", [P, 8, 512], F32))

        def pair(n):
            return ps[:, 2 * n:2 * n + 2, 0:HALF]

        def rows(a):
            return a.rearrange("p (h t) -> p h t", h=2)

        sems = {}

        def sem(name):
            if name not in sems:
                sems[name] = ctx.enter_context(nc.semaphore(name))
            return sems[name]

        raw_full = [sem(f"raw_full{n}") for n in range(RAW)]
        hi_done, lo_done = sem("hi_done"), sem("lo_done")
        panel_done = sem("panel_done")
        drained = [sem(f"drained{n}") for n in range(4)]
        x_in, par_in, vec_in = sem("x_in"), sem("par_in"), sem("vec_in")
        consts = sem("consts")

        def w_view(w):
            return w[0].rearrange("(k p) n -> p k n", p=P)

        v_in, v_out, v_glu = w_view(w_in), w_view(w_out), w_view(w_glu)
        v_bra, v_brp, v_brs = w_view(w_br_att), w_view(w_br_pool), w_view(w_br_ssm)
        v_gate, v_up, v_down = w_view(w_gate), w_view(w_up), w_view(w_down)

        def panel_source(p):
            if p < PAN_POOL:
                return v_in[:, :, COL_SSM + P * p:COL_SSM + P * (p + 1)]
            if p < PAN_POOLG:
                c = COL_POOL + P * (p - PAN_POOL)
                return v_in[:, :, c:c + P]
            if p < PAN_POOLB:
                c = COL_GATE + D + P * (p - PAN_POOLG)
                return v_in[:, :, c:c + P]
            if p < PAN_QKV:
                return v_brp[:, :, P * (p - PAN_POOLB):P * (p - PAN_POOLB + 1)]
            if p < PAN_GLU:
                kind, g, hc = qkv_panel(p)
                c = (0, COL_K, COL_V)[kind] + 256 * g + P * hc
                return v_in[:, :, c:c + P]
            if p < PAN_SSMBR:
                return v_glu[:, :, P * (p - PAN_GLU):P * (p - PAN_GLU + 1)]
            if p >= PAN_ATTB:
                return v_bra[:, :, P * (p - PAN_ATTB):P * (p - PAN_ATTB + 1)]
            if p >= PAN_ATTG:
                return v_in[:, :, COL_GATE + P * (p - PAN_ATTG):COL_GATE + P * (p - PAN_ATTG + 1)]
            c = (p - PAN_SSMBR) // 2 * P
            return v_brs[:, :, c:c + P] if p % 2 else v_in[:, :, COL_GATE + 2 * D + c:COL_GATE + 2 * D + c + P]

        block = ctx.enter_context(nc.Block())

        @block.sync
        def _(sp):
            def load(p, slot, src, blocks, wait):
                if wait is not None:
                    sp.wait_ge(lo_done, wait)
                dst = raw[:, slot, 0:blocks * P].rearrange("p (k n) -> p k n", k=blocks)
                sp.dma_start(dst, src).then_inc(raw_full[slot], 16)

            sent = {}

            def store(dst, src, name):
                sent[name] = sent.get(name, 0) + 16
                sp.dma_start(dst, src).then_inc(sem(name), 16)

            for p in range(RAW):
                load(p, p, panel_source(p), panel_blocks(p), None)
            loads = [
                (lrow[:, 0, :], lam_re[0].rearrange("(a g) p -> a (g p)", g=2)),
                (lrow[:, 1, :], lam_im[0].rearrange("(a g) p -> a (g p)", g=2)),
                (srow[:, :], log_step[0].rearrange("(a g) -> a g", g=2)),
            ]
            for n, (b, c, h) in enumerate(((b_re, c_re, ssm_re), (b_im, c_im, ssm_im))):
                loads.append((braw[:, n, :, :], b[0].rearrange("(a g) p h -> (g p) a h", g=2)))
                for m in range(2):
                    loads.append((craw[:, n, :, m, :], c[0].rearrange("(t g) h p -> (g h) t p", t=4)))
                loads.append((h0raw[:, n, :], h[0].rearrange("b (a g) p -> (b a) (g p)", g=2)))
            for dst, src in loads:
                sp.dma_start(dst, src).then_inc(par_in, 16)
            assert len(loads) == N_PAR
            loads = [(spool[:, :], state_pool[0].rearrange("b r c -> (b r) c")),
                     (poolw[:, :, :], pool_w[0].rearrange("g c e -> c g e")),
                     (dskip, ssm_d[0].rearrange("(k p) -> p k", p=P)),
                     (pscale, pool_scale[0].rearrange("(k p) -> p k", p=P))]
            for n, vec in enumerate((ln1_g, ln1_b, ln2_g, ln2_b)):
                loads.append((vecs[:, 8 * n:8 * n + 8], vec[0].rearrange("(k p) -> p k", p=P)))
            for dst, src in loads:
                sp.dma_start(dst, src).then_inc(vec_in, 16)
            assert len(loads) == N_VEC

            def stack(ct):
                sp.wait_ge(sem("stack_zeros"), ct + 1)
                for q in range(4):
                    r = slice(32 * q, 32 * q + 32)
                    for a in range(4):
                        sp.dma_start(ust[ct][32 * a:32 * a + 32, q, :, 0:NC],
                                     u_ssm[r, ct, 0:SEQ].rearrange("p (j s c) -> p j s c", j=2, s=4)[:, :, 3 - a, :]
                                     ).then_inc(sem(f"stacked{ct}"), 16)
                    sp.dma_start(ust[ct][0:32, q, 1, NC:], u_ssm[r, ct, SEQ:T]).then_inc(sem(f"stacked{ct}"), 16)

            def cache_load(n):
                g, cache = n % 3, (cache_k, cache_v)[n // 3]
                keys, step = (P, DILATION[g]) if g < 2 else (PAST // DILATION[2], DILATION[2])
                src = cache[g][0].rearrange("b (r s) h e -> r s b (h e)", s=step)[:, 0]
                sp.dma_start(cbuf[n][0:keys, :, :], src).then_inc(sem(f"cache_in{n}"), 16)

            for p in range(RAW, PAN_OUT):
                load(p, p % RAW, panel_source(p), panel_blocks(p), p - RAW + 1)
                for step in AFTER.get(p - SP_LAG, []) + [x for k in range(8) for x in INNER.get((p - SP_LAG, k), [])]:
                    if step[0] == "ssm_out":
                        ct = step[1]
                        sp.wait_ge(sem("state_staged"), ct + 1)
                        for n, (prompt, sample) in enumerate(((ssmre_p, ssmre_s), (ssmim_p, ssmim_s))):
                            store(prompt[0, 0].rearrange("(a g) p -> a (g p)", g=2)[4 * ct:4 * ct + 4], st_out[0:4, n, :],
                                  f"state_sent{ct}")
                            store(sample[0].rearrange("b (a g) p -> b a (g p)", g=2)[:, 4 * ct:4 * ct + 4],
                                  st_out[4:36, n, :], f"state_sent{ct}")
                    if step == "pool_old":
                        sp.wait_ge(sem("pool_staged"), 1)
                        store(pool_p[0, 0], stage_dec[0:PBUF, :], "pool_sent")
                        store(pool_s[0].rearrange("b s c -> (b s) c"), stage_dec[PBUF:PBUF + DEC, :], "pool_sent")
                    if step[0] in ("v_tokens", "k_tokens"):
                        name, hc, i = step
                        sp.wait_ge(sem(name), NT * hc + i + 1)
                        c = slice(P * hc, P * hc + P)
                        for g in range(N_GROUPS):
                            if g or i == NT - 1:
                                dst = (vp, kp)[name == "k_tokens"][g][0, 0].rearrange("t h e -> t (h e)")
                                t0 = 0 if g == 0 else P * i
                                store(dst[t0:t0 + P, c], k_tok[:, i, g, :] if name == "k_tokens" else v_tok[:, i, g, c],
                                      f"{name}_sent{hc}")
                if p == 10:
                    sp.wait_ge(drained[0], 2)
                    sp.wait_ge(drained[1], 2)
                    stack(0)
                if p == 13:
                    stack(1)
                if p == 19:
                    stack(2)
                    stack(3)
                if p == PAN_DEC + 6:
                    sp.wait_ge(sem("o_split"), len(ATT_STEPS))
                    for n in range(5):
                        cache_load(n)
                if p == PAN_DEC + 8:
                    sp.wait_ge(sem("reps_done"), 3)
                    for g in range(N_GROUPS):
                        store(ks[g][0].rearrange("b s h e -> b (s h e)"), reps[1][0:32:4, g, :], "reps_sent")
                        store(vs[g][0].rearrange("b s h e -> b (s h e)"), reps[2][0:32:4, g, :], "reps_sent")
                if p == PAN_DEC + 10:
                    sp.wait_ge(sem("cache_scored"), 1)
                    cache_load(5)

            with sp.Fori(0, KD // 2) as i:
                for j in range(2):
                    load(None, j, v_out[:, :, bass.ds(i * (2 * P) + P * j, P)], 8, i * 2 + (PAN_OUT + j - RAW + 1))
            with sp.Fori(0, KF) as i:
                for j, view in enumerate((v_gate, v_up)):
                    load(None, j, view[:, :, bass.ds(i * P, P)], 8, i * 2 + (PAN_FF + j - RAW + 1))
            with sp.Fori(0, KD) as i:
                k0 = 0
                for j, blocks in enumerate(DOWN_K):
                    load(None, j % 2, v_down[:, k0:k0 + blocks, bass.ds(i * P, P)], blocks, i * 4 + (PAN_DOWN + j - RAW + 1))
                    k0 += blocks
            for i in range(NT + 1):
                sp.wait_ge(sem("y_staged"), i + 1)
                if i < NT:
                    store(y_p[0, P * i:P * i + P, :], ytok[i % 2][:, :], f"y_sent{i}")
                else:
                    store(y_s.rearrange("b s d -> (b s) d"), ytok[i % 2][0:DEC, :], f"y_sent{i}")
            for name, value in sent.items():
                sp.wait_ge(sem(name), value)

        @block.gpsimd
        def _(pool):
            count = [0]

            def link(ins):
                count[0] += 1
                ins.then_inc(sem("pool_seq"), 1)
                pool.wait_ge(sem("pool_seq"), count[0])

            def lo(slot, raw_slot, blocks, n):
                pool.wait_ge(hi_done, n + 1)
                nc.gpsimd.tensor_tensor(w_lo[:, slot, 0:blocks * P], raw[:, raw_slot, 0:blocks * P],
                                        w_hi[:, slot, 0:blocks * P].bitcast(F32), ALU.subtract).then_inc(lo_done, 1)

            nc.gpsimd.memset(ones[:, :], 1.0).then_inc(consts, 1)
            pool.wait_ge(consts, 1)
            nc.gpsimd.affine_select(out=ident[:, :], in_=ones[:, :], compare_op=ALU.is_equal, fill=0.0, base=0,
                                    pattern=[[-1, P]], channel_multiplier=1).then_inc(consts, 1)
            for p in range(2):
                lo(p % RING, p % RAW, panel_blocks(p), p)
            for g, w in enumerate(POOL_W):
                link(nc.gpsimd.affine_select(out=wsel[:, g, :], in_=ones[:, 0:DEC], compare_op=ALU.is_ge, fill=0.0,
                                             base=-(PBUF - w + 1), pattern=[[-PBUF, DEC]], channel_multiplier=1))
                link(nc.gpsimd.affine_select(out=wsel[:, g, :], in_=wsel[:, g, :], compare_op=ALU.is_ge, fill=0.0,
                                             base=PBUF - 1, pattern=[[PBUF, DEC]], channel_multiplier=-1))
            link(nc.gpsimd.iota(rcnt[:, 0, :], pattern=[[1, 16]], base=1, channel_multiplier=0,
                                allow_small_or_imprecise_dtypes=True))
            link(nc.gpsimd.iota(dist32[:, 0:128], pattern=[[-1, P]], base=P, channel_multiplier=0,
                                allow_small_or_imprecise_dtypes=True))
            link(nc.gpsimd.iota(dist32[:, 128:256], pattern=[[-4, P]], base=4 * P, channel_multiplier=0,
                                allow_small_or_imprecise_dtypes=True))
            nc.gpsimd.iota(dist32[:, 256:288], pattern=[[-16, 32]], base=512, channel_multiplier=0,
                           allow_small_or_imprecise_dtypes=True).then_inc(consts, 1)

            def bias_tables():
                pool.wait_ge(sem("state_turned"), 4)
                pool.wait_ge(sem("pool_split"), 4)
                link(nc.gpsimd.iota(tdi[:, :], pattern=[[-1, 512]], base=384, channel_multiplier=1))
                link(nc.gpsimd.iota(td[:, 1, :], pattern=[[-1, 512]], base=384, channel_multiplier=1,
                                    allow_small_or_imprecise_dtypes=True))
                link(nc.gpsimd.affine_select(out=td[:, 1, :], in_=td[:, 1, :], compare_op=ALU.is_ge, fill=BIG,
                                             base=384, pattern=[[-1, 512]], channel_multiplier=1))
                nc.gpsimd.affine_select(out=td[:, 0, :], in_=td[:, 1, :], compare_op=ALU.is_ge, fill=BIG,
                                        base=BACK - 384, pattern=[[1, 512]], channel_multiplier=-1
                                        ).then_inc(sem("td_base"), 1)

            for p in range(2, PAN_OUT):
                lo(p % RING, p % RAW, panel_blocks(p), p)
                for step in AFTER.get(p - 4, []):
                    if step == "bias":
                        bias_tables()
            with pool.Fori(0, (KD + 2 * KF) // 4) as i:
                for j in range(4):
                    lo((PAN_OUT + j) % RING, j % RAW, 8, i * 4 + (PAN_OUT + j))
            with pool.Fori(0, KD) as i:
                for j in range(4):
                    lo((PAN_DOWN + j) % RING, j % RAW, DOWN_K[j], i * 4 + (PAN_DOWN + j))

        @block.tensor
        def _(pe):
            mm = nc.tensor.matmul

            def tr(out, in_):
                n = in_.partition_size()
                return nc.tensor.transpose(out, in_, ident[0:n, 0:n])

            def multiply(slot, blocks, hi, lo, out_pair, k0=0, first=True, last=True, inner=None):
                for k in range(blocks):
                    wh, wl = (w[:, slot, P * k:P * k + P] for w in (w_hi, w_lo))
                    for m, (w, x) in enumerate(((wh, hi), (wh, lo), (wl, hi))):
                        for h in range(2):
                            ins = mm(ps[:, 2 * out_pair + h, 0:HALF], w, x[:, k0 + k, HALF * h:HALF * (h + 1)],
                                     start=(first and k == 0 and m == 0), stop=(last and k == blocks - 1 and m == 2))
                    if inner is not None:
                        if k == blocks - 1:
                            ins.then_inc(panel_done, 1)
                        for step in INNER.get((inner, k), []):
                            run(step)
                return ins

            def panel(p, hi, lo, wait=True):
                pe.wait_ge(lo_done, p + 1)
                if p >= 2:
                    pe.wait_ge(drained[p % 2], p // 2)
                multiply(p % RING, panel_blocks(p), hi, lo, p % 2, inner=p)

            pe.wait_ge(consts, 2)
            for c in range(KD):
                if c == 0:
                    pe.wait_ge(x_in, 16 * (NT + 1))
                if c >= 4:
                    pe.wait_ge(sem("x_split"), c - 3)
                for i in range(NT):
                    ins = tr(ps[:, 4 + c % 4, P * i:P * i + P], xtok[:, i, P * c:P * c + P])
                ins.then_inc(sem("x_turned"), 1)
            for c in range(KD):
                ins = tr(ps[:, 0, DEC * c:DEC * c + DEC], xstok[0:DEC, P * c:P * c + P])
            ins.then_inc(sem("x_turned"), 1)
            def turn_params():
                pe.wait_ge(par_in, 16 * N_PAR)
                pe.wait_ge(sem("steps_spread"), 1)
                for n in range(3):
                    ins = tr(ps[:, 4, 16 * n:16 * n + 16], lrow[:, n, :])
                ins.then_inc(sem("lam_turned"), 1)
                for n in range(2):
                    for ct in range(4):
                        ins = tr(ps[:, 5 + n, P * ct:P * ct + P], craw[:, n, ct, :, :].rearrange("p g e -> p (g e)"))
                ins.then_inc(sem("c_turned"), 1)
                for n in range(2):
                    ins = tr(ps[:, 7, P * n:P * n + P], h0raw[:, n, :])
                ins.then_inc(sem("h0_turned"), 1)

            def ssm_prep(ct):
                m = ct % 2
                pe.wait_ge(sem("spread"), ct + 1)
                if ct == 0:
                    pe.wait_ge(sem("par_read"), 3)
                    pe.wait_ge(sem("psum_old_read"), 1)
                    pe.wait_ge(sem("pool_staged"), 1)
                else:
                    pe.wait_ge(sem("v_copied"), ct)
                for n in range(2):
                    for k in range(CH):
                        q, half = k // 2, k % 2
                        ins = tr(ps[:, 4 + 2 * n + q // 2, P * (k % 4):P * (k % 4) + P],
                                 bp[:, n, q, 4 * half:4 * half + 4, :].rearrange("p k c -> p (k c)"))
                ins.then_inc(sem("bt_turned"), 1)
                pe.wait_ge(sem("bt_copied"), ct + 1)
                for q in range(4):
                    for n in range(2):
                        ins = mm(ps[32 * q:32 * q + 32, 4, 0:256], bp[:, n, q, 0, :], cp[m][:, 0:CH, n, q, :],
                                 start=n == 0, stop=n == 1)
                ins.then_inc(sem("k_formed"), 1)

            def ssm_in(ct):
                pe.wait_ge(sem("k_copied"), ct + 1)
                if ct >= 1:
                    pe.wait_ge(sem("y_read"), ct)
                    pe.wait_ge(sem("state_staged"), ct)
                    if ct == 1:
                        pe.wait_ge(sem("pool_scaled"), 4)
                pe.wait_ge(sem(f"stacked{ct}"), 16 * 20)
                pe.wait_ge(sem("stack_zeros"), ct + 1)
                for q in range(4):
                    for n in range(2):
                        mm(ps[:, 4 + q, 72 * n:72 * n + 72], bt[n][:, q, 0, :], ust[ct][:, q, 1, :],
                           start=True, stop=False, skip_group_check=True)
                        ins = mm(ps[:, 4 + q, 72 * n:72 * n + NC], bt[n][:, q, 1, :], ust[ct][:, q, 0, 0:NC],
                                 start=False, stop=True, skip_group_check=True)
                ins.then_inc(sem("v_formed"), 1)

            def ssm_out(ct):
                m = ct % 2
                pe.wait_ge(sem("h_done"), ct + 1)
                if ct < 3:
                    pe.wait_ge(sem("k_copied"), ct + 2)
                for j in range(CH):
                    mm(ps[:, 4, NC * j:512], kbd[m][:, j, :], u_ssm[:, ct, 0:NC * (CH - j)],
                       start=j == 0, stop=False, skip_group_check=True)
                for t in range(CH):
                    for n in range(2):
                        for q in range(4):
                            r = slice(32 * q, 32 * q + 32)
                            mm(ps[r, 4, NC * t:NC * t + NC], cp[m][:, t + 1, n, q, :], hst[:, n, q, 0:NC],
                               start=False, stop=n == 1, skip_group_check=True)
                for q in range(4):
                    for n in range(2):
                        ins = mm(ps[32 * q:32 * q + 32, 5, 0:DEC], cp[m][:, 0, n, q, :], hst[:, n, q, 65:73],
                                 start=n == 0, stop=n == 1)
                ins.then_inc(sem("y_formed"), 1)
                for n in range(2):
                    ins = tr(ps[0:36, 6, P * n:P * n + P], hfin[:, n, :])
                ins.then_inc(sem("state_turned"), 1)

            def pool_old():
                pe.wait_ge(consts, 3)
                pe.wait_ge(vec_in, 16 * N_VEC)
                pe.wait_ge(sem("par_read"), 3)
                pe.wait_ge(drained[0], PAN_POOLG // 2)
                pe.wait_ge(drained[1], PAN_POOLG // 2)
                for g in range(4):
                    ins = mm(ps[:, 4, DEC * g:DEC * g + DEC], spool[0:120, P * g:P * g + P], wsel[0:120, g, :],
                             start=True, stop=True)
                ins.then_inc(sem("psum_old"), 1)
                for g in range(4):
                    ins = tr(ps[0:PBUF + DEC, 5, P * g:P * g + P], upool[:, g, 16 + SEQ - PBUF:16 + T])
                ins.then_inc(sem("pool_turned"), 1)

            def pool_mix():
                for g in range(4):
                    pe.wait_ge(sem("diff_done"), g + 1)
                    if g == 0:
                        pe.wait_ge(sem("y_read"), 1)
                        pe.wait_ge(sem("state_staged"), 1)
                    if g >= 2:
                        pe.wait_ge(sem("pool_scaled"), g - 1)
                    for h in range(2):
                        ins = mm(ps[:, 4 + 2 * (g % 2) + h, 0:HALF], poolw[:, g, :],
                                 upool[:, g, 16 + HALF * h:16 + HALF * (h + 1)], start=True, stop=True)
                    ins.then_inc(sem("pool_mixed"), 1)

            def v_tokens(hc, i):
                pe.wait_ge(drained[(PAN_QKV + 9 * hc + 8) % 2], (PAN_QKV + 9 * hc + 8) // 2 + 1)
                pe.wait_ge(drained[(PAN_QKV + 9 * hc + 7) % 2], (PAN_QKV + 9 * hc + 7) // 2 + 1)
                if hc == 0:
                    pe.wait_ge(sem("y_read"), 4)
                    pe.wait_ge(sem("state_staged"), 4)
                else:
                    pe.wait_ge(sem("o_split"), 8)
                for g in range(N_GROUPS):
                    ins = tr(ps[:, 4 + i, P * g:P * g + P], v_t[:, g, P * i:P * i + P])
                ins.then_inc(sem("v_turned"), 1)

            def k_tokens(hc, i):
                pe.wait_ge(sem("v_tokens"), NT * hc + i + 1)
                for g in range(N_GROUPS):
                    if g or i == NT - 1:
                        ins = tr(ps[:, 4 + i, P * g:P * g + P], k_t[:, hc, g, P * i:P * i + P])
                ins.then_inc(sem("k_turned"), 1)

            def decode_rep(n):
                if n == 0:
                    pe.wait_ge(sem("o_split"), len(ATT_STEPS))
                    pe.wait_ge(sem("decode_kept"), 6)
                if n == 2:
                    pe.wait_ge(sem("reps_done"), 1)
                b = 4 + 2 * (n % 2)
                for g in range(N_GROUPS):
                    for hc in range(2):
                        c = 256 * g + P * hc
                        ins = tr(ps[0:32, b + c // 512, c % 512:c % 512 + P], dexp[:, n, hc, g, :])
                ins.then_inc(sem("rep_turned"), 1)

            def decode_spread(n):
                g, b2 = n // 4, n % 4
                if n == 0:
                    pe.wait_ge(sem("reps_done"), 3)
                if n >= 4:
                    pe.wait_ge(sem("qk_read"), n - 3)
                for b in range(2):
                    ins = mm(ps[:, 4 + n % 4, 256 * b:256 * b + 256],
                             ident[0:32, 4 * (2 * b2 + b):4 * (2 * b2 + b) + 1].broadcast_to([32, P]),
                             reps[0][:, g, :], start=True, stop=True)
                ins.then_inc(sem("q_spread"), 1)

            def decode_scores():
                pe.wait_ge(sem("qk_read"), 12)
                for g in range(N_GROUPS):
                    pe.wait_ge(sem("cache_scored"), g + 1)
                    keys = P if g < 2 else 32
                    ins = tr(ps[0:32, 4, P * g:P * g + keys], s32[0:keys, g, :])
                ins.then_inc(sem("s_turned"), 1)

            def decode_softmax():
                pe.wait_ge(sem("p_done"), 1)
                for g in range(N_GROUPS):
                    keys = P if g < 2 else 32
                    ins = tr(ps[0:keys, 5, 32 * g:32 * g + 32], sc32[:, P * g:P * g + keys])
                ins.then_inc(sem("p_turned"), 1)

            def decode_out():
                pe.wait_ge(sem("p_copied"), 1)
                pe.wait_ge(sem("diag_done"), 1)
                for hc in range(2):
                    for g in range(N_GROUPS):
                        ins = mm(ps[:, 6 + hc, 0:16], reps[2][:, g, P * hc:P * hc + P],
                                 diag32[:, g, :].rearrange("r (b h) -> r b h", h=4)[:, :, 2 * hc:2 * hc + 2],
                                 start=g == 0, stop=False, skip_group_check=True)
                for g in range(N_GROUPS):
                    keys = P if g < 2 else 32
                    pe.wait_ge(sem(f"cache_in{3 + g}"), 16)
                    for hc in range(2):
                        for b in range(DEC):
                            ins = mm(ps[:, 6 + hc, 2 * b:2 * b + 2], cbuf[3 + g][0:keys, b, P * hc:P * hc + P],
                                     pt32[0:keys, g, 4 * b + 2 * hc:4 * b + 2 * hc + 2],
                                     start=False, stop=g == 2, skip_group_check=True)
                    ins.then_inc(sem("cache_summed"), 1)

            def scores(n, g):
                h, i = ATT_STEPS[n]
                r = slice(64 * (h % 2), 64 * (h % 2) + 64)
                if n % 8 == 0 and g == 0:
                    pe.wait_ge(sem("k_tokens"), NT * (n // 8 + 1))
                if n > 0 or g == 2:
                    pe.wait_ge(sem("scored"), 3 * n + (0, -1, 1)[g])
                keys = keys_of(g, i)
                mm(ps[:, 4 + g % 2, 0:P * len(keys)], q_t[r, h // 2, g, P * i:P * i + P],
                   k_t[r, h // 2, g, P * keys[0]:P * (i + 1)], start=True, stop=True
                   ).then_inc(sem("s_formed"), 1)

            def probs(n, m):
                h, i = ATT_STEPS[n]
                r = slice(64 * (h % 2), 64 * (h % 2) + 64)
                quads = quads_of(n)
                turned = sum(len(quads_of(j)) for j in range(n)) + m
                if m == 0:
                    pe.wait_ge(sem("p_normed"), n + 1)
                if turned:
                    pe.wait_ge(sem("pt_copied"), turned)
                if m < len(quads):
                    for j, _ in enumerate(quads[m]):
                        c = P * (4 * m + j)
                        ins = tr(ps[:, 7, P * j:P * j + P], sc[:, n % 2, c:c + P])
                    ins.then_inc(sem("pt_turned"), 1)
                if m >= 1:
                    if m == 1 and n >= 1:
                        pe.wait_ge(sem("o_split"), n)
                    for j, (g, kt) in enumerate(quads[m - 1]):
                        ins = mm(ps[r, 6, 0:P], v_tok[:, kt, g, 64 * h:64 * h + 64],
                                 ptr[:, (turned - 1) % 2, P * j:P * j + P],
                                 start=m == 1 and j == 0, stop=m == len(quads) and j == len(quads[-1]) - 1)
                    ins.then_inc(sem("pt_used"), 1)

            todo = {"turn_params": turn_params, "ssm_prep": ssm_prep, "ssm_in": ssm_in, "ssm_out": ssm_out,
                    "pool_old": pool_old, "pool_mix": pool_mix, "v_tokens": v_tokens, "k_tokens": k_tokens,
                    "scores": scores, "probs": probs, "decode_rep": decode_rep, "decode_spread": decode_spread,
                    "decode_scores": lambda _: decode_scores(), "decode_softmax": lambda _: decode_softmax(),
                    "decode_out": lambda _: decode_out()}

            def run(step):
                name, args = (step[0], step[1:]) if isinstance(step, tuple) else (step, ())
                if name in todo:
                    todo[name](*args)

            for step in AFTER[-1]:
                run(step)
            pe.wait_ge(sem("x_split"), KD + 1)
            for p in range(PAN_OUT):
                if p == PAN_POOLB:
                    pe.wait_ge(sem("pool_split"), 4)
                if p == PAN_GLU:
                    pe.wait_ge(sem("gelu_split_done"), 4)
                if p == PAN_SSMBR + 1:
                    pe.wait_ge(sem("ys_split"), 4)
                if p == PAN_ATTB:
                    pe.wait_ge(sem("decode_done"), 1)
                rows_of = (x_hi, x_lo)
                if PAN_POOLB <= p < PAN_QKV:
                    rows_of = (yp_hi, yp_lo)
                if PAN_GLU <= p < PAN_SSMBR or (PAN_SSMBR <= p < PAN_ATTG and p % 2):
                    rows_of = (ys_hi, ys_lo)
                if PAN_ATTB <= p:
                    rows_of = (ya_hi, ya_lo)
                panel(p, *rows_of)
                for step in AFTER.get(p, []):
                    run(step)
            pe.wait_ge(sem("m_split"), KD)
            with pe.Fori(0, KD // 4) as i:
                for j in range(4):
                    pe.wait_ge(lo_done, i * 4 + (PAN_OUT + j + 1))
                    pe.wait_ge(drained[j % 2], i * 2 + (PAN_OUT + j) // 2)
                    multiply((PAN_OUT + j) % RING, 8, m_hi, m_lo, j % 2).then_inc(panel_done, 1)

            def norm_sums(n):
                for c in range(KD):
                    pe.wait_ge(sem("z_done"), KD * n + c + 1)
                    for h in range(2):
                        ins = mm(ps[:, 4 + h, 0:HALF], ones[:, :], z[:, c, HALF * h:HALF * (h + 1)],
                                 start=c == 0, stop=c == KD - 1)
                ins.then_inc(sem("sum_done"), 1)
                for c in range(KD):
                    pe.wait_ge(sem("squared"), KD * n + c + 1)
                    for h in range(2):
                        ins = mm(ps[:, 6 + h, 0:HALF], ones[:, :], tg[:, c % 2, HALF * h:HALF * (h + 1)],
                                 start=c == 0, stop=c == KD - 1)
                    ins.then_inc(sem("square_summed"), 1)

            norm_sums(0)
            pe.wait_ge(sem("x1_split"), KD)
            with pe.Fori(0, KF // 2) as i:
                for j in range(4):
                    pe.wait_ge(lo_done, i * 4 + (PAN_FF + j + 1))
                    pe.wait_ge(drained[j], i * 1 + (PAN_FF // 2 if j < 2 else 0))
                    multiply((PAN_FF + j) % RING, 8, x_hi, x_lo, j).then_inc(panel_done, 1)
            pe.wait_ge(sem("f_split"), KF)
            with pe.Fori(0, KD // 2) as i:
                for o in range(2):
                    k0 = 0
                    for j, blocks in enumerate(DOWN_K):
                        pe.wait_ge(lo_done, i * 8 + (PAN_DOWN + 4 * o + j + 1))
                        if j == 0:
                            pe.wait_ge(drained[o], i * 1 + (PAN_FF // 2 + KF // 2))
                        multiply((PAN_DOWN + j) % RING, blocks, f_hi, f_lo, o, k0, j == 0, j == 3).then_inc(panel_done, 1)
                        k0 += blocks
            norm_sums(1)
            for i in range(NT + 1):
                n = P if i < NT else DEC
                if i >= 4:
                    pe.wait_ge(sem("y_staged"), i - 3)
                for c in range(KD):
                    pe.wait_ge(sem("y_done"), c + 1)
                    ins = tr(ps[0:n, 2 * (i % 4) + c // 4, P * (c % 4):P * (c % 4) + P], z[:, c, P * i:P * i + n])
                ins.then_inc(sem("y_turned"), 1)

        @block.scalar
        def _(act):
            A = nc.scalar.activation

            def hi(slot, raw_slot, blocks, n, turn, used=None):
                act.wait_ge(raw_full[raw_slot], turn)
                if used is not None:
                    act.wait_ge(panel_done, used)
                A(w_hi[:, slot, 0:blocks * P], raw[:, raw_slot, 0:blocks * P], ACT.Copy).then_inc(hi_done, 1)

            def hi_static(p):
                if p < PAN_END:
                    hi(p % RING, p % RAW, panel_blocks(p), p, 16 * (p // RAW + 1), p - RING + 1 if p >= RING else None)

            for i in range(NT):
                act.dma_start(xtok[:, i, :], x_prompt[0, P * i:P * i + P, :]).then_inc(x_in, 16)
            act.dma_start(xstok[:, :], x_sample.rearrange("b s d -> (b s) d")).then_inc(x_in, 16)
            for p in range(2):
                hi_static(p)
            for c in range(KD):
                act.wait_ge(sem("x_turned"), c + 1)
                A(x_hi[:, c, 0:SEQ], ps[:, 4 + c % 4, :], ACT.Copy).then_inc(sem("x_high"), 1)
            act.wait_ge(sem("x_turned"), KD + 1)
            A(x_hi[:, :, SEQ:T], ps[:, 0, 0:DEC * KD].rearrange("p (c b) -> p c b", b=DEC), ACT.Copy).then_inc(sem("x_high"), 1)
            hi_static(2)

            def params():
                act.wait_ge(sem("angle_done"), 1)
                A(par[:, 6, :], par[:, 4, :], ACT.Sin).then_inc(sem("sin_done"), 1)
                A(par[:, 7, :], par[:, 5, :], ACT.Sin).then_inc(sem("sin_done"), 1)

            def evacuate(p):
                if p >= PAN_ATTB or PAN_POOLB <= p < PAN_QKV:
                    return
                act.wait_ge(panel_done, p + 1)
                b = 2 * (p % 2)
                if p < PAN_POOL:
                    u = u_ssm[:, p, 0:SEQ].rearrange("p (s c) -> p c s", s=CH)
                    A(u[:, 0:32, :], ps[:, b, 0:256].rearrange("p (c s) -> p c s", s=CH), ACT.Copy)
                    A(u[:, 32, 0:4], ps[:, b, 256:260], ACT.Copy)
                    A(u[:, 32, 4:8], ps[:, b + 1, 0:4], ACT.Copy)
                    A(u[:, 33:64, :], ps[:, b + 1, 4:252].rearrange("p (c s) -> p c s", s=CH), ACT.Copy)
                    A(u_ssm[:, p, SEQ:T], ps[:, b + 1, 252:260], ACT.Copy).then_inc(drained[p % 2], 1)
                elif p < PAN_POOLG:
                    A(rows(upool[:, p - PAN_POOL, 16:16 + T]), pair(p % 2), ACT.Copy).then_inc(drained[p % 2], 1)
                elif p < PAN_POOLB:
                    A(rows(z[:, p - PAN_POOLG, :]), pair(p % 2), ACT.Tanh, scale=0.5).then_inc(drained[p % 2], 1)
                elif p >= PAN_ATTG:
                    if p == PAN_ATTG:
                        for hc in range(2):
                            act.wait_ge(sem(f"v_tokens_sent{hc}"), 16 * 9)
                            act.wait_ge(sem(f"k_tokens_sent{hc}"), 16 * 9)
                    A(rows(tga[:, p - PAN_ATTG, :]), pair(p % 2), ACT.Tanh, scale=0.5).then_inc(drained[p % 2], 1)
                elif p >= PAN_SSMBR:
                    if p % 2 == 0:
                        if p in (PAN_SSMBR, PAN_SSMBR + 2):
                            act.wait_ge(sem("glu_used"), 4)
                        else:
                            act.wait_ge(drained[1], (p - 3) // 2 + 1)
                        A(rows(tg[:, (p - PAN_SSMBR) // 2 % 2, :]), pair(0), ACT.Tanh, scale=0.5).then_inc(drained[0], 1)
                elif p < PAN_GLU:
                    kind, g, hc = qkv_panel(p)
                    if p == PAN_QKV:
                        act.wait_ge(sem("y_formed"), 4)
                    if kind == 2 and hc == 1 and g == 0:
                        act.wait_ge(sem("v_turned"), NT)
                        act.wait_ge(sem("decode_kept"), 3)
                    dst = (q_t[:, hc, g, :], k_t[:, hc, g, :], v_t[:, g, :])[kind]
                    A(rows(dst), pair(p % 2), ACT.Copy).then_inc(drained[p % 2], 1)
                else:
                    n = p - PAN_GLU
                    if n >= 2:
                        act.wait_ge(sem("glu_used"), n - 1)
                    A(rows(tg[:, n % 2, :]), pair(p % 2), ACT.Tanh, scale=0.5).then_inc(drained[p % 2], 1)

            def ssm_prep(ct):
                act.wait_ge(sem("powers_done"), ct + 1)
                if ct >= 1:
                    act.wait_ge(sem("k_formed"), ct)
                if ct >= 2:
                    act.wait_ge(sem("y_formed"), ct - 1)
                for g in range(2):
                    r = slice(64 * g, 64 * g + 64)
                    A(bp[r].rearrange("p n q k c -> p (n q) k c")[:, :, :, 16 * g:16 * g + 16],
                      bpc[r].rearrange("p k n q c -> p (n q) k c"), ACT.Copy)
                    ins = A(cp[ct % 2][r].rearrange("p k n q c -> p (k n q) c")[:, :, 16 * g:16 * g + 16],
                            cpc[r].rearrange("p k n q c -> p (k n q) c"), ACT.Copy)
                ins.then_inc(sem("spread"), 1)
                act.wait_ge(sem("bt_turned"), ct + 1)
                for n in range(2):
                    for half in range(2):
                        ins = A(bt[n][:, 2 * half:2 * half + 2, :, :].rearrange("p q k c -> p (q k c)"),
                                ps[:, 4 + 2 * n + half, :], ACT.Copy)
                ins.then_inc(sem("bt_copied"), 1)

            def ssm_in(ct):
                act.wait_ge(sem("v_formed"), ct + 1)
                if ct >= 1:
                    act.wait_ge(sem("h_done"), ct)
                A(vsb[:, :, :], ps[:, 4:8, 0:144], ACT.Copy).then_inc(sem("v_copied"), 1)

            def ssm_out(ct):
                act.wait_ge(sem("state_turned"), ct + 1)
                if ct >= 1:
                    act.wait_ge(sem(f"state_sent{ct - 1}"), 64)
                A(st_out[:, :, :], ps[0:36, 6, 0:256].rearrange("p (n c) -> p n c", n=2), ACT.Copy).then_inc(sem("state_staged"), 1)

            def gelu(ct):
                act.wait_ge(sem("g_in"), ct + 1)
                A(t2_row, t1_row, ACT.Tanh, scale=math.sqrt(2 / math.pi)).then_inc(sem("g_tanh"), 1)

            def high_rows(dst, ct, scale):
                A(dst[:, ct, 0:SEQ].rearrange("p (c s) -> p c s", s=CH),
                  u_ssm[:, ct, 0:SEQ].rearrange("p (s c) -> p c s", s=CH), ACT.Copy, scale=scale)
                return A(dst[:, ct, SEQ:T], u_ssm[:, ct, SEQ:T], ACT.Copy, scale=scale)

            def gelu_split():
                act.wait_ge(sem("gelu_done"), 4)
                act.wait_ge(sem("y_formed"), 4)
                for ct in range(4):
                    high_rows(ys_hi, ct, 0.5).then_inc(sem("gelu_high"), 1)

            def pool_old():
                act.wait_ge(sem("pool_turned"), 1)
                A(stage_dec[0:PBUF + DEC, :], ps[0:PBUF + DEC, 5, :], ACT.Copy).then_inc(sem("pool_staged"), 1)

            def pool_mix():
                for g in range(4):
                    act.wait_ge(sem("pool_scaled"), g + 1)
                    A(yp_hi[:, g, :], tw[:, g % 2, :], ACT.Copy).then_inc(sem("pool_high"), 1)

            def v_tokens(hc, i):
                act.wait_ge(sem("v_turned"), NT * hc + i + 1)
                A(v_tok[:, i, :, P * hc:P * hc + P], ps[:, 4 + i, 0:384].rearrange("p (g c) -> p g c", g=3),
                  ACT.Copy).then_inc(sem("v_tokens"), 1)

            def k_tokens(hc, i):
                act.wait_ge(sem("k_turned"), NT * hc + i + 1)
                if hc == 1 and i == 0:
                    act.wait_ge(sem("k_tokens_sent0"), 16 * 9)
                g0 = 0 if i == NT - 1 else 1
                A(k_tok[:, i, g0:3, :], ps[:, 4 + i, P * g0:384].rearrange("p (g c) -> p g c", c=P),
                  ACT.Copy).then_inc(sem("k_tokens"), 1)

            def decode_rep(n):
                act.wait_ge(sem("rep_turned"), n + 1)
                b = 4 + 2 * (n % 2)
                A(reps[n][:, 0:2, :], ps[0:32, b, :].rearrange("p (g c) -> p g c", g=2), ACT.Copy)
                A(reps[n][:, 2, :], ps[0:32, b + 1, 0:256], ACT.Copy).then_inc(sem("reps_done"), 1)

            def decode_softmax():
                act.wait_ge(sem("s32_done"), 1)
                A(sc32[:, 0:291], sc32[:, 0:291], ACT.Exp, bias=small[0:32, 1:2], scale=0.125,
                  accum_out=small[0:32, 2:3]).then_inc(sem("e32_done"), 1)
                act.wait_ge(sem("p_turned"), 1)
                A(pt32[:, 0:2, :], ps[:, 5, 0:64].rearrange("p (g c) -> p g c", g=2), ACT.Copy)
                A(pt32[0:32, 2, :], ps[0:32, 5, 64:96], ACT.Copy).then_inc(sem("p_copied"), 1)

            def decode_out():
                act.wait_ge(sem("cache_summed"), 3)
                for h in range(2):
                    r = slice(64 * h, 64 * h + 64)
                    ins = A(ya_hi[r, :, SEQ:T], ps[r, 6:8, 0:16].rearrange("p c (b h) -> p c b h", h=2)[:, :, :, h], ACT.Copy)
                ins.then_inc(sem("od_high"), 1)

            def exp(n):
                act.wait_ge(sem("max_done"), n + 1)
                cols = P * sum(len(quad) for quad in quads_of(n))
                A(sc[:, n % 2, 0:cols], sc[:, n % 2, 0:cols], ACT.Exp, bias=small[:, 8 + n % 2:9 + n % 2], scale=0.125,
                  accum_out=small[:, 10 + n % 2:11 + n % 2]).then_inc(sem("exp_done"), 1)

            def probs(n, m):
                h, i = ATT_STEPS[n]
                quads = quads_of(n)
                turned = sum(len(quads_of(j)) for j in range(n)) + m
                if m < len(quads):
                    k = len(quads[m])
                    act.wait_ge(sem("pt_turned"), turned + 1)
                    if turned >= 2:
                        act.wait_ge(sem("pt_used"), turned - 1)
                    A(ptr[:, turned % 2, 0:P * k], ps[:, 7, 0:P * k], ACT.Copy).then_inc(sem("pt_copied"), 1)
                else:
                    act.wait_ge(sem("pt_used"), turned)
                    r = slice(64 * (h % 2), 64 * (h % 2) + 64)
                    A(ya_hi[r, h // 2, P * i:P * i + P], ps[r, 6, 0:P], ACT.Copy).then_inc(sem("o_high"), 1)

            t1_row = tw[:, 0, :]
            t2_row = tw[:, 1, :]

            todo = {"ssm_prep": ssm_prep, "ssm_in": ssm_in, "ssm_out": ssm_out, "v_tokens": v_tokens, "k_tokens": k_tokens,
                    "exp": exp, "probs": probs, "gelu": gelu, "params": params, "pool_old": pool_old, "pool_mix": pool_mix,
                    "gelu_split": gelu_split, "decode_rep": decode_rep, "decode_softmax": lambda _: decode_softmax(),
                    "decode_out": lambda _: decode_out()}

            def run(step):
                name, args = (step[0], step[1:]) if isinstance(step, tuple) else (step, ())
                if name in todo:
                    todo[name](*args)

            for step in AFTER[-1]:
                run(step)
            for p in range(PAN_OUT):
                hi_static(p + LOOK)
                for k in range(panel_blocks(p)):
                    for step in INNER.get((p, k), []):
                        run(step)
                evacuate(p)
                if p >= PAN_ATTB:
                    act.wait_ge(sem("m_summed"), p - PAN_ATTB + 1)
                    A(m_hi[:, p - PAN_ATTB, :], z[:, p - PAN_ATTB, :], ACT.Copy, scale=0.5).then_inc(sem("m_high"), 1)
                for step in AFTER.get(p, []):
                    run(step)
                if p == PAN_SSMBR - 1:
                    for ct in range(4):
                        act.wait_ge(sem("glu_used"), 4)
                        high_rows(ys_hi, ct, 0.25).then_inc(sem("ys_high"), 1)

            with act.Fori(0, KD // 4) as i:
                for j in range(4):
                    q = PAN_OUT + j + LOOK
                    hi(q % RING, q % RAW, 8, None, i * 32 + 16 * (q // RAW + 1), i * 4 + (q - RING + 1))

            def norm(n):
                g_v, b_v = ((ln1g, ln1b), (ln2g, ln2b))[n]
                for c in range(KD):
                    act.wait_ge(sem("centred"), KD * n + c + 1)
                    if c >= 2:
                        act.wait_ge(sem("square_summed"), KD * n + c - 1)
                    A(tg[:, c % 2, :], z[:, c, :], ACT.Square).then_inc(sem("squared"), 1)
                act.wait_ge(sem("var_done"), n + 1)
                A(tw[:, 1, :], tw[:, 0, :], ACT.Sqrt).then_inc(sem("std_done"), 1)
                for c in range(KD):
                    act.wait_ge(sem("scaled"), KD * n + c + 1)
                    if n == 0:
                        A(x_hi[:, c, :], z[:, c, :], ACT.Identity, bias=b_v[:, c:c + 1],
                          scale=g_v[:, c:c + 1]).then_inc(sem("x1_high"), 1)

            norm(0)

            def ff_turn(i, looks):
                for j in range(4):
                    if looks is None:
                        q = PAN_FF + j + LOOK
                        hi(q % RING, q % RAW, 8, None, i * 32 + 16 * (q // RAW + 1), i * 4 + (q - RING + 1))
                    else:
                        hi_static(looks + j + LOOK)
                    act.wait_ge(panel_done, i * 4 + (PAN_FF + j + 1))
                    if j % 2 == 0:
                        A(rows(tg[:, j // 2, :]), pair(j), ACT.Tanh, scale=0.5).then_inc(sem("f_tanh"), 1)
                    else:
                        act.wait_ge(drained[j], i * 1 + ((PAN_FF // 2 if j == 1 else 0) + 1))
                        A(f_hi[:, bass.ds(i * 2 + j // 2, 1), :], tw[:, bass.ds(j // 2, 1), :], ACT.Copy,
                          scale=0.5).then_inc(sem("f_high"), 1)

            with act.Fori(0, KF // 2 - 1) as i:
                ff_turn(i, None)
            ff_turn(KF // 2 - 1, PAN_DOWN - 4)

            with act.Fori(0, KD - 1) as i:
                for j in range(4):
                    q = PAN_DOWN + j + LOOK
                    hi(q % RING, q % RAW, panel_blocks(q), None, i * 32 + 16 * (q // RAW + 1), i * 4 + (q - RING + 1))
            for j in range(4):
                hi_static(PAN_END - 4 + j + LOOK)
            norm(1)
            for i in range(NT + 1):
                n = P if i < NT else DEC
                act.wait_ge(sem("y_turned"), i + 1)
                if i >= 2:
                    act.wait_ge(sem(f"y_sent{i - 2}"), 16)
                A(ytok[i % 2][0:n, :].rearrange("p (h c) -> p h c", h=2), ps[0:n, 2 * (i % 4):2 * (i % 4) + 2, :],
                  ACT.Copy).then_inc(sem("y_staged"), 1)

        @block.vector
        def _(dve):
            V = nc.vector
            count = [0]
            told = {}

            def link(ins):
                count[0] += 1
                ins.then_inc(sem("dve_seq"), 1)
                dve.wait_ge(sem("dve_seq"), count[0])

            def tell(ins, name):
                told[name] = told.get(name, 0) + 1
                ins.then_inc(sem(name), 1)
                dve.wait_ge(sem(name), told[name])

            def cmul(out_r, out_i, a, s_r, s_i, conj, u, w, part):
                tt = V.tensor_tensor
                tt(u, a, s_r, ALU.mult)
                link(tt(w, a, s_i, ALU.mult))
                tt(out_r, part(u, 0), part(w, 1), ALU.add if conj else ALU.subtract)
                link(tt(out_i, part(u, 1), part(w, 0), ALU.subtract if conj else ALU.add))

            for c in range(KD):
                dve.wait_ge(sem("x_high"), c + 1)
                tell(V.tensor_tensor(x_lo[:, c, 0:SEQ], ps[:, 4 + c % 4, :], x_hi[:, c, 0:SEQ].bitcast(F32), ALU.subtract),
                     "x_split")
            dve.wait_ge(sem("x_high"), KD + 1)
            tell(V.tensor_tensor(x_lo[:, :, SEQ:T], ps[:, 0, 0:DEC * KD].rearrange("p (c b) -> p c b", b=DEC),
                                 x_hi[:, :, SEQ:T].bitcast(F32), ALU.subtract), "x_split")

            LR, LI, ST, MAG, RED, RHALF, SIN, SHALF = range(8)
            (TMP, TMP2, TMP3, COS, LBR, LBI, CFR, CFI, L2R, L2I, L4R, L4I, L8R, L8I, PR, PI, A8, TH, KI, NUM, NUM2,
             W1, W2, W3, W4) = range(8, 33)

            def v(n):
                return par[:, n, :]

            dve.wait_ge(par_in, 16 * N_PAR)
            tell(V.tensor_copy(lrow[:, 2, :].rearrange("a (g p) -> a g p", g=2),
                               srow[:, :].unsqueeze(2).broadcast_to([16, 2, E])), "steps_spread")

            def turn_params():
                dve.wait_ge(sem("lam_turned"), 1)
                tell(V.tensor_copy(par[:, 0:3, :], ps[:, 4, 0:48].rearrange("p (n a) -> p n a", n=3)), "par_read")
                dve.wait_ge(sem("c_turned"), 1)
                for n in range(2):
                    src = ps[:, 5 + n, :].rearrange("p (a g h) -> p a g h", g=2, h=16)
                    for g in range(2):
                        r = slice(64 * g, 64 * g + 64)
                        ins = V.tensor_scalar(cc[r, n, :, :], src[r, :, g, :], (1.0, -1.0)[n], None, ALU.mult)
                        if n == 1 and g == 1:
                            tell(ins, "par_read")
                        else:
                            link(ins)
                dve.wait_ge(sem("h0_turned"), 1)
                tell(V.tensor_copy(h0[:, :, :, :], ps[:, 7, 0:256].rearrange("p (n b a) -> p n b a", n=2, b=DEC)), "par_read")

            def cmul_par(out, a, b, conj):
                s_r, s_i = (v(b + n).unsqueeze(1).broadcast_to([P, 2, 16]) for n in range(2))
                cmul(v(out), v(out + 1), par[:, a:a + 2, :], s_r, s_i, conj, par[:, W1:W1 + 2, :], par[:, W3:W3 + 2, :],
                     lambda x, n: x[:, n, :])

            def params():
                def ts(out, a, s1, s2, o1, o2):
                    link(V.tensor_scalar(v(out), v(a), s1, s2, o1, o2))

                def tt(out, a, b, op):
                    link(V.tensor_tensor(v(out), v(a), v(b), op))

                def stt(out, a, s, b, o1, o2):
                    link(V.scalar_tensor_tensor(v(out), v(a), s, v(b), o1, o2))

                def exp(out, a):
                    ts(a, a, -87.0, 88.0, ALU.max, ALU.min)
                    ts(TMP, a, math.log2(math.e), ROUND, ALU.mult, ALU.add)
                    ts(TMP, TMP, -ROUND, None, ALU.add, ALU.bypass)
                    stt(TMP2, TMP, -0.693359375, a, ALU.mult, ALU.add)
                    stt(TMP2, TMP, 2.12194440e-4, TMP2, ALU.mult, ALU.add)
                    ts(TMP3, TMP2, 1 / 5040.0, None, ALU.mult, ALU.bypass)
                    for f in (720.0, 120.0, 24.0, 6.0, 2.0, 1.0):
                        stt(TMP3, TMP3, 1 / f, TMP2, ALU.add, ALU.mult)
                    link(V.tensor_scalar(v(KI).bitcast(I32), v(TMP), 127.0, 2.0 ** 23, ALU.add, ALU.mult))
                    stt(out, TMP3, 1.0, KI, ALU.add, ALU.mult)

                exp(ST, ST)
                tt(MAG, LR, ST, ALU.mult)
                exp(MAG, MAG)
                tt(TH, LI, ST, ALU.mult)
                ts(TMP, TH, 1 / (2 * math.pi), ROUND, ALU.mult, ALU.add)
                ts(TMP, TMP, -ROUND, None, ALU.add, ALU.bypass)
                c1 = 6.28125
                c2 = float((np.float32(2 * math.pi - c1).view(np.uint32) & np.uint32(0xFFFFF000)).view(np.float32))
                c3 = 2 * math.pi - c1 - c2
                stt(RED, TMP, -c1, TH, ALU.mult, ALU.add)
                stt(RED, TMP, -c2, RED, ALU.mult, ALU.add)
                stt(RED, TMP, -c3, RED, ALU.mult, ALU.add)
                ts(RHALF, RED, 0.5, None, ALU.mult, ALU.bypass)
                tell(V.tensor_scalar(v(RED), v(RED), 3.1415925, -3.1415925, ALU.min, ALU.max), "angle_done")
                dve.wait_ge(sem("sin_done"), 2)
                tt(TMP, SHALF, SHALF, ALU.mult)
                ts(COS, TMP, -2.0, 1.0, ALU.mult, ALU.add)
                tt(LBR, MAG, COS, ALU.mult)
                tt(LBI, MAG, SIN, ALU.mult)
                ts(NUM, LBR, -1.0, None, ALU.add, ALU.bypass)
                link(V.tensor_copy(v(NUM2), v(LBI)))
                cmul_par(CFR, NUM, LR, True)
                tt(TMP, LR, LR, ALU.mult)
                tt(TMP2, LI, LI, ALU.mult)
                tt(TMP, TMP, TMP2, ALU.add)
                link(V.reciprocal(v(TMP), v(TMP)))
                tt(CFR, CFR, TMP, ALU.mult)
                tt(CFI, CFI, TMP, ALU.mult)
                for a, b in ((LBR, L2R), (L2R, L4R), (L4R, L8R)):
                    cmul_par(b, a, a, False)
                for a, b in ((MAG, A8), (A8, A8), (A8, A8)):
                    tt(b, a, a, ALU.mult)
                link(V.tensor_copy(v(PR), v(COS)))
                link(V.tensor_copy(v(PI), v(SIN)))
                for _ in range(3):
                    unit_square()
                cf = [v(n).unsqueeze(1).unsqueeze(3).broadcast_to([P, 2, 16, 16]) for n in (CFR, CFI)]
                w1, w2 = (x[:, 0:512].rearrange("p (n a h) -> p n a h", n=2, a=16) for x in (t1, t2))
                cmul(bbar[:, 0, :, :], bbar[:, 1, :, :], braw[:, :, :, :], cf[0], cf[1], False, w1, w2, lambda x, n: x[:, n])
                for m in range(2):
                    V.memset(kbd[m][:, :, :], 0.0)
                    V.memset(cp[m][:, :, :, :, :], 0.0)
                V.memset(bp[:, :, :, :, :], 0.0)
                tell(V.memset(ust[0][:, :, 1, NC:], 0.0), "stack_zeros")
                link(V.memset(hst[:, :, :, 0:1], 0.0))

            def unit_square():
                def tt(out, a, b, op):
                    link(V.tensor_tensor(v(out), v(a), v(b), op))
                both = par[:, PR:PR + 2, :]
                V.tensor_tensor(par[:, TMP:TMP + 2, :], both, both, ALU.mult)
                tt(TMP3, PR, PI, ALU.mult)
                V.tensor_tensor(v(PR), v(TMP), v(TMP2), ALU.subtract)
                link(V.tensor_scalar(v(PI), v(TMP3), 2.0, None, ALU.mult))
                link(V.tensor_tensor(par[:, TMP:TMP + 2, :], both, both, ALU.mult))
                tt(TMP, TMP, TMP2, ALU.add)
                link(V.tensor_scalar(v(TMP), v(TMP), -0.5, 1.5, ALU.mult, ALU.add))
                link(V.tensor_tensor(both, both, v(TMP).unsqueeze(1).broadcast_to([P, 2, 16]), ALU.mult))

            def powers(ct):
                aq = slice(4 * ct, 4 * ct + 4)
                if ct == 0:
                    for k in range(6):
                        link(V.tensor_copy(rotk[:, k, :, :], par[:, PR:PR + 2, :]))
                        if k < 5:
                            unit_square()
                else:
                    dve.wait_ge(sem("spread"), ct)
                V.tensor_copy(bpc[:, 0, :, :, :], bbar[:, :, aq, :])
                link(V.tensor_copy(cpc[:, 0, :, :, :], cc[:, :, aq, :]))
                for a, conj, top in ((bpc, False, CH), (cpc, True, CH + 1)):
                    for k, name in ((1, LBR), (2, L2R), (4, L4R), (8, L8R)):
                        if k >= top:
                            continue
                        c = min(k, top - k)
                        w1, w2 = (x[:, 0:128 * c].rearrange("p (k q c) -> p k q c", q=4, c=16) for x in (t1, t2))
                        s_r, s_i = (par[:, L, aq].unsqueeze(1).unsqueeze(3).broadcast_to([P, 2 * c, 4, 16])
                                    for L in (name, name + 1))
                        cmul(a[:, k:k + c, 0], a[:, k:k + c, 1], a[:, 0:c].rearrange("p k n q c -> p (k n) q c"), s_r, s_i,
                             conj, w1, w2, lambda x, n: x.rearrange("p (k n) q c -> p k n q c", n=2)[:, :, n])
                e = ein[ct % 2]
                V.memset(e[:, 0, :, 0:1], 1.0)
                link(V.memset(e[:, 1, :, 0:1], 0.0))
                for k in range(6):
                    c = 1 << k
                    s_r, s_i = (rotk[:, k, n, aq].unsqueeze(1).unsqueeze(3).broadcast_to([P, 2, 4, c]) for n in range(2))
                    w1, w2 = (x[:, 0:8 * c].rearrange("p (n q c) -> p n q c", n=2, q=4) for x in (t1, t2))
                    cmul(e[:, 0, :, c:2 * c], e[:, 1, :, c:2 * c], e[:, :, :, 0:c], s_r, s_i, False, w1, w2,
                         lambda x, n: x[:, n])
                link(V.tensor_copy(dec0[ct % 2][:, :, :], v(A8)[:, aq].unsqueeze(2).broadcast_to([P, 4, NC])))
                tell(V.memset(dec0[ct % 2][:, :, 0:1], 0.0), "powers_done")

            def ssm_prep(ct):
                dve.wait_ge(sem("k_formed"), ct + 1)
                for q in range(4):
                    r = slice(32 * q, 32 * q + 32)
                    ins = V.tensor_copy(kbd[ct % 2][r, :, 32 * q:32 * q + 32],
                                        ps[r, 4, 0:256].rearrange("p (j c) -> p j c", j=CH))
                    if q < 3:
                        link(ins)
                    else:
                        tell(ins, "k_copied")

            def ssm_in(ct):
                aq = slice(4 * ct, 4 * ct + 4)
                dve.wait_ge(sem("v_copied"), ct + 1)
                if ct >= 1:
                    dve.wait_ge(sem("state_turned"), ct)
                w1, w2 = (x[:, 0:8 * NC].rearrange("p (n q c) -> p n q c", n=2, q=4) for x in (t1, t2))
                e_r, e_i = (ein[ct % 2][:, n, :, :].unsqueeze(1).broadcast_to([P, 2, 4, NC]) for n in range(2))

                def part(x, n):
                    return x[:, n]

                both = vsb[:, :, :].rearrange("p q (n c) -> p n q c", n=2)
                cmul(wrot[:, 0], wrot[:, 1], both[:, :, :, 0:NC], e_r, e_i, True, w1, w2, part)
                d0 = dec0[ct % 2][:, :, :].rearrange("p q c -> p (q c)")
                for n in range(2):
                    link(V.tensor_tensor_scan(grot[:, n, :, :].rearrange("p q c -> p (q c)"), d0,
                                              wrot[:, n, :, :].rearrange("p q c -> p (q c)"), 0.0, ALU.mult, ALU.add))
                cmul(hst[:, 0, :, 1:65], hst[:, 1, :, 1:65], grot[:, :, :, :], e_r, e_i, False, w1, w2, part)
                for n in range(2):
                    L = (LBR, LBI)[n]
                    d = (t1, t2)[n][:, 0:64].rearrange("p (n b q) -> p n b q", n=2, q=4)
                    ins = V.tensor_tensor(d, h0[:, :, :, aq],
                                          par[:, L, aq].unsqueeze(1).unsqueeze(1).broadcast_to([P, 2, DEC, 4]), ALU.mult)
                link(ins)
                u, w = (x[:, 0:64].rearrange("p (n b q) -> p n q b", n=2, q=4) for x in (t1, t2))
                V.tensor_tensor(hst[:, 0, :, 65:73], u[:, 0], w[:, 1], ALU.subtract)
                link(V.tensor_tensor(hst[:, 1, :, 65:73], u[:, 1], w[:, 0], ALU.add))
                link(V.tensor_tensor(hst[:, 0, :, 65:73], hst[:, 0, :, 65:73], vsb[:, :, 64:72], ALU.add))
                link(V.tensor_tensor(hst[:, 1, :, 65:73], hst[:, 1, :, 65:73], vsb[:, :, 136:144], ALU.add))
                tell(V.tensor_copy(hfin[:, :, :].rearrange("p n (j q) -> p n q j", q=4), hst[:, :, :, 64:73]), "h_done")

            def ssm_out(ct):
                dve.wait_ge(sem("y_formed"), ct + 1)
                link(V.scalar_tensor_tensor(u_ssm[:, ct, 0:SEQ], u_ssm[:, ct, 0:SEQ], dskip[:, ct:ct + 1], ps[:, 4, :],
                                            ALU.mult, ALU.add))
                tell(V.scalar_tensor_tensor(u_ssm[:, ct, SEQ:T], u_ssm[:, ct, SEQ:T], dskip[:, ct:ct + 1],
                                            ps[:, 5, 0:DEC], ALU.mult, ALU.add), "y_read")

            def gelu(ct):
                u, a = u_ssm[:, ct, :], tw[:, 0, :]
                link(V.tensor_tensor(a, u, u, ALU.mult))
                link(V.tensor_scalar(a, a, 0.044715, 1.0, ALU.mult, ALU.add))
                tell(V.tensor_tensor(a, a, u, ALU.mult), "g_in")
                dve.wait_ge(sem("g_tanh"), ct + 1)
                tell(V.scalar_tensor_tensor(u, tw[:, 1, :], 1.0, u, ALU.add, ALU.mult), "gelu_done")

            def low_rows(dst, high, ct, scale, name):
                link(V.scalar_tensor_tensor(dst[:, ct, 0:SEQ].rearrange("p (c s) -> p c s", s=CH),
                                            u_ssm[:, ct, 0:SEQ].rearrange("p (s c) -> p c s", s=CH), scale,
                                            high[:, ct, 0:SEQ].bitcast(F32).rearrange("p (c s) -> p c s", s=CH),
                                            ALU.mult, ALU.subtract))
                tell(V.scalar_tensor_tensor(dst[:, ct, SEQ:T], u_ssm[:, ct, SEQ:T], scale,
                                            high[:, ct, SEQ:T].bitcast(F32), ALU.mult, ALU.subtract), name)

            def gelu_split():
                for ct in range(4):
                    dve.wait_ge(sem("gelu_high"), ct + 1)
                    low_rows(ys_lo, ys_hi, ct, 0.5, "gelu_split_done")

            def pool_old():
                dve.wait_ge(consts, 3)
                dve.wait_ge(vec_in, 16 * N_VEC)
                for g in (3, 2, 1, 0):
                    link(V.tensor_scalar(rcnt[:, g, :], rcnt[:, 0, :], float(POOL_W[g]), None, ALU.min))
                link(V.reciprocal(rcnt[:, :, :], rcnt[:, :, :]))
                dve.wait_ge(drained[(PAN_POOL + 2) % 2], (PAN_POOL + 2) // 2 + 1)
                dve.wait_ge(drained[(PAN_POOL + 3) % 2], (PAN_POOL + 3) // 2 + 1)
                link(V.memset(upool[:, :, 0:16], 0.0))
                dve.wait_ge(sem("psum_old"), 1)
                tell(V.tensor_copy(oldsum[:, :, :], ps[:, 4, 0:32].rearrange("p (g b) -> p g b", g=4)), "psum_old_read")
                tell(V.memset(ust[1][:, :, 1, NC:], 0.0), "stack_zeros")

            def pool_diff():
                dve.wait_ge(sem("pool_turned"), 1)
                for g, w in enumerate(POOL_W):
                    src = upool[:, g, 0:16 + SEQ]
                    n, size = 1, SEQ + 16
                    bufs = wide
                    cur, turn = src, 0
                    while n < w:
                        out = bufs[turn]
                        link(V.tensor_tensor(out[:, 2 * n - 1:size], cur[:, 2 * n - 1:size], cur[:, n - 1:size - n], ALU.add))
                        cur, turn, n = out, 1 - turn, 2 * n
                    tot = cur[:, 16:16 + SEQ]
                    link(V.tensor_tensor(small[:, 16:32], tot[:, 0:16], rcnt[:, g, :], ALU.mult))
                    link(V.tensor_tensor(oldsum[:, g, :], oldsum[:, g, :], upool[:, g, 16 + SEQ:16 + T], ALU.add))
                    link(V.scalar_tensor_tensor(upool[:, g, 16 + SEQ:16 + T], oldsum[:, g, :], 1.0 / w,
                                                upool[:, g, 16 + SEQ:16 + T], ALU.mult, ALU.subtract))
                    link(V.scalar_tensor_tensor(upool[:, g, 32:16 + SEQ], tot[:, 16:SEQ], 1.0 / w,
                                                upool[:, g, 32:16 + SEQ], ALU.mult, ALU.subtract))
                    tell(V.tensor_tensor(upool[:, g, 16:32], small[:, 16:32], upool[:, g, 16:32], ALU.subtract), "diff_done")

            def pool_mix():
                for g in range(4):
                    dve.wait_ge(sem("pool_mixed"), g + 1)
                    tell(V.tensor_scalar(rows(tw[:, g % 2, :]), pair(2 + g % 2), pscale[:, g:g + 1], None, ALU.mult),
                         "pool_scaled")
                    dve.wait_ge(sem("pool_high"), g + 1)
                    tell(V.tensor_tensor(yp_lo[:, g, :], tw[:, g % 2, :], yp_hi[:, g, :].bitcast(F32), ALU.subtract), "pool_split")
                for ct in (2, 3):
                    tell(V.memset(ust[ct][:, :, 1, NC:], 0.0), "stack_zeros")

            def v_tokens(hc, i):
                if i < NT - 1:
                    return
                dve.wait_ge(sem("v_turned"), NT * (hc + 1))
                for n, src in enumerate((q_t[:, hc, :, SEQ:T], k_t[:, hc, :, SEQ:T], v_t[:, :, SEQ:T])):
                    tell(V.tensor_copy(dexp[:, n, hc, :, :].rearrange("p g (b h) -> p g b h", h=4),
                                       src.unsqueeze(3).broadcast_to([P, 3, DEC, 4])), "decode_kept")

            def decode_consts():
                rep = ident[0:32, 0:32].rearrange("p (b h) -> p h b", h=4)
                link(V.tensor_reduce(small[0:32, 4:8], rep, AX.X, ALU.add))
                link(V.tensor_copy(hmask[:, :, :], small[0:32, 4:8].unsqueeze(2).broadcast_to([32, 4, E])))
                for g in range(N_GROUPS):
                    for h in range(HEADS):
                        link(V.memset(small[0:32, 32 + 4 * g + h:33 + 4 * g + h], -8.0 * SLOPE[g][h]))
                for g in range(N_GROUPS):
                    link(V.tensor_tensor(small[0:32, 12:16], small[0:32, 4:8], small[0:32, 32 + 4 * g:36 + 4 * g], ALU.mult))
                    link(V.tensor_reduce(small[0:32, 44 + g:45 + g], small[0:32, 12:16], AX.X, ALU.add))

            def decode_own(_):
                dve.wait_ge(sem("reps_done"), 3)
                for g in range(N_GROUPS):
                    w1 = tw[0:32, 0, 0:256]
                    link(V.tensor_tensor(w1, reps[0][:, g, :], reps[1][:, g, :], ALU.mult))
                    link(V.tensor_tensor(w1, w1, hmask[:, :, :].rearrange("p h e -> p (h e)"), ALU.mult))
                    link(V.tensor_reduce(sc32[:, 288 + g:289 + g], w1, AX.X, ALU.add))

            def decode_spread(n):
                g, b2 = n // 4, n % 4
                keys = P if g < 2 else 32
                buf = cbuf[g]
                if b2 == 0:
                    dve.wait_ge(sem(f"cache_in{g}"), 16)
                dve.wait_ge(sem("q_spread"), n + 1)
                tell(V.tensor_tensor(buf[0:keys, 2 * b2:2 * b2 + 2, :], buf[0:keys, 2 * b2:2 * b2 + 2, :],
                                     ps[0:keys, 4 + n % 4, :].rearrange("p (b c) -> p b c", b=2), ALU.mult), "qk_read")
                if b2 == 3:
                    tell(V.tensor_reduce(s32[0:keys, g, :], buf[0:keys, :, :].rearrange("p b (h e) -> p (b h) e", h=4),
                                         AX.X, ALU.add), "cache_scored")

            def decode_scores():
                dve.wait_ge(sem("s_turned"), 1)
                for g in range(N_GROUPS):
                    keys = P if g < 2 else 32
                    c = slice(P * g, P * g + keys)
                    link(V.scalar_tensor_tensor(sc32[:, c], dist32[:, c], small[0:32, 44 + g:45 + g], ps[0:32, 4, c],
                                                ALU.mult, ALU.add))

            def decode_softmax():
                link(V.reduce_max(small[0:32, 0:1], sc32[:, 0:291], AX.X))
                tell(V.tensor_scalar(small[0:32, 1:2], small[0:32, 0:1], -0.125, None, ALU.mult), "s32_done")
                dve.wait_ge(sem("e32_done"), 1)
                link(V.reciprocal(small[0:32, 3:4], small[0:32, 2:3]))
                tell(V.tensor_scalar(sc32[:, 0:291], sc32[:, 0:291], small[0:32, 3:4], None, ALU.mult), "p_done")
                for g in range(N_GROUPS):
                    ins = V.tensor_scalar(diag32[:, g, :], ident[0:32, 0:32], sc32[:, 288 + g:289 + g], None, ALU.mult)
                ins.then_inc(sem("diag_done"), 1)

            def decode_out():
                dve.wait_ge(sem("od_high"), 1)
                for h in range(2):
                    r = slice(64 * h, 64 * h + 64)
                    ins = V.tensor_tensor(ya_lo[r, :, SEQ:T], ps[r, 6:8, 0:16].rearrange("p c (b h) -> p c b h", h=2)[:, :, :, h],
                                          ya_hi[r, :, SEQ:T].bitcast(F32), ALU.subtract)
                    if h == 0:
                        link(ins)
                    else:
                        tell(ins, "decode_done")

            def bias():
                dve.wait_ge(sem("td_base"), 1)
                for g in (2, 1):
                    m = DILATION[g] - 1
                    w = tw[:, 0, 0:512].bitcast(I32)
                    link(V.tensor_scalar(w, tdi[:, :], m, None, ALU.bitwise_and))
                    link(V.tensor_scalar(tw[:, 1, 0:512], w, 1.0, BIG, ALU.min, ALU.mult))
                    link(V.tensor_tensor(td[:, g, :], tw[:, 1, 0:512], td[:, 1, :], ALU.add))

            def scores(n, g):
                h, i = ATT_STEPS[n]
                col = P * sum(len(keys_of(j, i)) for j in range(g))
                if n >= 2 and g == 0:
                    dve.wait_ge(sem("o_high"), n - 1)
                w = P * len(keys_of(g, i))
                dve.wait_ge(sem("s_formed"), 3 * n + g + 1)
                c0 = 384 + P * (keys_of(g, i)[0] - i)
                tell(V.scalar_tensor_tensor(sc[:, n % 2, col:col + w], td[:, g, c0:c0 + w], -8.0 * SLOPE[g][h],
                                            ps[:, 4 + g % 2, 0:w], ALU.mult, ALU.add), "scored")
                if g == N_GROUPS - 1:
                    link(V.reduce_max(small[:, 12 + n % 2:13 + n % 2], sc[:, n % 2, 0:col + w], AX.X))
                    tell(V.tensor_scalar(small[:, 8 + n % 2:9 + n % 2], small[:, 12 + n % 2:13 + n % 2], -0.125, None,
                                         ALU.mult), "max_done")

            def normalise(n):
                cols = P * sum(len(quad) for quad in quads_of(n))
                dve.wait_ge(sem("exp_done"), n + 1)
                link(V.reciprocal(small[:, 14 + n % 2:15 + n % 2], small[:, 10 + n % 2:11 + n % 2]))
                tell(V.tensor_scalar(sc[:, n % 2, 0:cols], sc[:, n % 2, 0:cols], small[:, 14 + n % 2:15 + n % 2], None,
                                     ALU.mult), "p_normed")

            def probs(n, m):
                if m < len(quads_of(n)):
                    return
                h, i = ATT_STEPS[n]
                r = slice(64 * (h % 2), 64 * (h % 2) + 64)
                dve.wait_ge(sem("o_high"), n + 1)
                tell(V.tensor_tensor(ya_lo[r, h // 2, P * i:P * i + P], ps[r, 6, 0:P],
                                     ya_hi[r, h // 2, P * i:P * i + P].bitcast(F32), ALU.subtract), "o_split")

            def branch(p):
                dve.wait_ge(panel_done, p + 1)
                if p < PAN_QKV:
                    n = p - PAN_POOLB
                    V.scalar_tensor_tensor(rows(z[:, n, :]), rows(z[:, n, :]), 1.0, pair(p % 2), ALU.add, ALU.mult
                                           ).then_inc(drained[p % 2], 1)
                elif p < PAN_ATTG:
                    n = (p - PAN_SSMBR) // 2
                    dve.wait_ge(drained[0], p // 2 + 1)
                    link(V.scalar_tensor_tensor(rows(tw[:, 0, :]), rows(tg[:, n % 2, :]), 1.0, pair(1), ALU.add, ALU.mult))
                    V.tensor_tensor(z[:, n, :], z[:, n, :], tw[:, 0, :], ALU.add).then_inc(drained[1], 1)
                else:
                    n, b = p - PAN_ATTB, p % 2
                    V.scalar_tensor_tensor(rows(tw[:, b, :]), rows(tga[:, n, :]), 1.0, pair(b), ALU.add, ALU.mult
                                           ).then_inc(drained[b], 1)
                    dve.wait_ge(drained[b], p // 2 + 1)
                    tell(V.tensor_tensor(z[:, n, :], z[:, n, :], tw[:, b, :], ALU.add), "m_summed")
                    dve.wait_ge(sem("m_high"), n + 1)
                    V.scalar_tensor_tensor(m_lo[:, n, :], z[:, n, :], 0.5, m_hi[:, n, :].bitcast(F32), ALU.mult,
                                           ALU.subtract).then_inc(sem("m_split"), 1)

            def glu(p):
                n = p - PAN_GLU
                dve.wait_ge(drained[p % 2], p // 2 + 1)
                t = tg[:, n % 2, :]
                link(V.scalar_tensor_tensor(u_ssm[:, n, 0:SEQ].rearrange("p (s c) -> p c s", s=CH),
                                            t[:, 0:SEQ].rearrange("p (c s) -> p c s", s=CH), 1.0,
                                            u_ssm[:, n, 0:SEQ].rearrange("p (s c) -> p c s", s=CH), ALU.add, ALU.mult))
                tell(V.scalar_tensor_tensor(u_ssm[:, n, SEQ:T], t[:, SEQ:T], 1.0, u_ssm[:, n, SEQ:T], ALU.add, ALU.mult),
                     "glu_used")

            todo = {"turn_params": turn_params, "params": params, "powers": powers, "ssm_prep": ssm_prep, "ssm_in": ssm_in,
                    "ssm_out": ssm_out, "gelu": gelu, "gelu_split": gelu_split, "pool_old": pool_old,
                    "pool_diff": pool_diff, "pool_mix": pool_mix, "v_tokens": v_tokens, "decode_consts": decode_consts,
                    "decode_own": decode_own, "decode_spread": decode_spread, "decode_scores": lambda _: decode_scores(),
                    "decode_softmax": lambda _: decode_softmax(), "decode_out": lambda _: decode_out(), "bias": bias,
                    "scores": scores, "normalise": normalise, "probs": probs}

            def run(step):
                name, args = (step[0], step[1:]) if isinstance(step, tuple) else (step, ())
                if name in todo:
                    todo[name](*args)

            for step in AFTER[-1]:
                run(step)
            for p in range(PAN_OUT):
                for k in range(panel_blocks(p)):
                    for step in INNER.get((p, k), []):
                        run(step)
                if PAN_POOLB <= p < PAN_QKV or (PAN_SSMBR <= p < PAN_ATTG and p % 2) or p >= PAN_ATTB:
                    branch(p)
                if PAN_GLU <= p < PAN_SSMBR:
                    glu(p)
                for step in AFTER.get(p, []):
                    run(step)
                if p == PAN_SSMBR - 1:
                    for ct in range(4):
                        dve.wait_ge(sem("ys_high"), ct + 1)
                        low_rows(ys_lo, ys_hi, ct, 0.25, "ys_split")

            def residual(i, j, p_ready, per, base_drained, dest_base):
                c = bass.ds(i * per + j, 1)
                dve.wait_ge(panel_done, p_ready)
                b = j % 2
                V.scalar_tensor_tensor(rows(tw[:, b, :]), x_hi[:, c, :].bitcast(F32).rearrange("p o (h t) -> p (o h) t", h=2),
                                       ALPHA, pair(b), ALU.mult, ALU.add).then_inc(drained[b], 1)
                dve.wait_ge(drained[b], base_drained)
                V.scalar_tensor_tensor(z[:, c, :], x_lo[:, c, :].bitcast(F32), ALPHA, tw[:, b:b + 1, :], ALU.mult, ALU.add
                                       ).then_inc(sem("z_done"), 1)

            with dve.Fori(0, KD // 4) as i:
                for j in range(4):
                    residual(i, j, i * 4 + (PAN_OUT + j + 1), 4, i * 2 + ((PAN_OUT + j) // 2 + 1), 0)

            def norm(n):
                g_v, b_v = ((ln1g, ln1b), (ln2g, ln2b))[n]
                dve.wait_ge(sem("sum_done"), n + 1)
                link(V.tensor_scalar(rows(tw[:, 0, :]), pair(2), 1.0 / D, None, ALU.mult))
                for c in range(KD):
                    tell(V.tensor_tensor(z[:, c, :], z[:, c, :], tw[:, 0, :], ALU.subtract), "centred")
                dve.wait_ge(sem("square_summed"), KD * (n + 1))
                tell(V.tensor_scalar(rows(tw[:, 0, :]), pair(3), 1.0 / D, EPS, ALU.mult, ALU.add), "var_done")
                dve.wait_ge(sem("std_done"), n + 1)
                link(V.reciprocal(tw[:, 0, :], tw[:, 1, :]))
                for c in range(KD):
                    tell(V.tensor_tensor(z[:, c, :], z[:, c, :], tw[:, 0, :], ALU.mult), "scaled")
                    if n == 0:
                        link(V.tensor_scalar(tw[:, 1, :], z[:, c, :], g_v[:, c:c + 1], b_v[:, c:c + 1], ALU.mult, ALU.add))
                        dve.wait_ge(sem("x1_high"), c + 1)
                        tell(V.tensor_tensor(x_lo[:, c, :], tw[:, 1, :], x_hi[:, c, :].bitcast(F32), ALU.subtract), "x1_split")
                    else:
                        tell(V.tensor_scalar(z[:, c, :], z[:, c, :], g_v[:, c:c + 1], b_v[:, c:c + 1], ALU.mult, ALU.add),
                             "y_done")

            norm(0)

            with dve.Fori(0, KF // 2) as i:
                for j in range(2):
                    c = bass.ds(i * 2 + j, 1)
                    dve.wait_ge(sem("f_tanh"), i * 2 + (j + 1))
                    V.scalar_tensor_tensor(rows(tw[:, j, :]), rows(tg[:, j, :]), 1.0, pair(2 * j), ALU.add, ALU.mult
                                           ).then_inc(drained[2 * j], 1)
                    dve.wait_ge(drained[2 * j], i * 1 + ((PAN_FF // 2 if j == 0 else 0) + 1))
                    dve.wait_ge(panel_done, i * 4 + (PAN_FF + 2 * j + 2))
                    V.tensor_tensor(rows(tw[:, j, :]), rows(tw[:, j, :]), pair(2 * j + 1), ALU.mult).then_inc(drained[2 * j + 1], 1)
                    dve.wait_ge(sem("f_high"), i * 2 + (j + 1))
                    V.scalar_tensor_tensor(f_lo[:, c, :], tw[:, j:j + 1, :], 0.5, f_hi[:, c, :].bitcast(F32), ALU.mult,
                                           ALU.subtract).then_inc(sem("f_split"), 1)

            with dve.Fori(0, KD // 2) as i:
                for j in range(2):
                    residual(i, j, i * 8 + (PAN_DOWN + 4 * j + 4), 2, i * 1 + (PAN_FF // 2 + KF // 2 + 1), 0)
            norm(1)


N_PAR, N_VEC = 11, 8
_INS = ['x_prompt', 'x_sample', 'cache_k_w128', 'cache_v_w128', 'cache_k_w512', 'cache_v_w512', 'cache_k_w2048',
        'cache_v_w2048', 'state_pool', 'state_ssm_re', 'state_ssm_im', 'w_in', 'pool_w', 'pool_scale',
        'ssm_lambda_re', 'ssm_lambda_im', 'ssm_b_re', 'ssm_b_im', 'ssm_c_re', 'ssm_c_im', 'ssm_d', 'ssm_log_step',
        'ssm_w_glu', 'w_br_att', 'w_br_pool', 'w_br_ssm', 'w_out', 'ln1_g', 'ln1_b', 'ffn_w_gate', 'ffn_w_up',
        'ffn_w_down', 'ln2_g', 'ln2_b']
_OUTS = ([(1, SEQ, D), (DEC, 1, D)] + [(1, 1, min(w, SEQ), HEADS, E) for w in WINDOWS for _ in range(2)]
         + [(1, 1, PBUF, 512), (1, 1, 32, 64), (1, 1, 32, 64)] + [(1, DEC, 1, HEADS, E)] * 6
         + [(1, DEC, 1, 512), (1, DEC, 32, 64), (1, DEC, 32, 64)])


def kernel(**inputs):
    import numpy as _np
    import concourse.bacc as _bacc
    from concourse.bass_utils import run_bass_kernel_spmd as _run

    nc = _bacc.Bacc("TRN2", target_bir_lowering=False, num_devices=1, dynamic_dma_scratch_size=2048)
    arrays, ins, outs = {}, [], []
    for name in _INS:
        a = _np.ascontiguousarray(inputs[name])
        arrays[f"in_{name}"] = a
        ins.append(nc.dram_tensor(f"in_{name}", a.shape, F32, kind="ExternalInput").ap())
    for n, shape in enumerate(_OUTS):
        outs.append(nc.dram_tensor(f"out_{n}", shape, F32, kind="ExternalOutput").ap())
    build(nc, ins, outs)
    r = _run(nc, [arrays], core_ids=[0])
    return tuple(r.results[0][f"out_{n}"] for n in range(len(_OUTS)))
```

```python
import math
from contextlib import ExitStack

import numpy as np

import concourse.bass as bass
from concourse import mybir

F32 = mybir.dt.float32
F32R = mybir.dt.float32r
I32 = mybir.dt.int32
ALU = mybir.AluOpType
ACT = mybir.ActivationFunctionType
AX = mybir.AxisListType

P = 128
D = 1024
SEQ, DEC = 512, 8
T = SEQ + DEC
HALF = T // 2
KD = D // P
FF = 2816
KF = FF // P
ATT = 768
N_GROUPS, HEADS, E = 3, 4, 64
WINDOWS = (128, 512, 2048)
DILATION = (1, 4, 16)
PAST = 512
BACK = 128
POOL_W = (2, 4, 8, 16)
PBUF = 15
COL_K, COL_V, COL_POOL, COL_SSM, COL_GATE = 768, 1536, 2304, 2816, 3328
NT = SEQ // P
CH = 8
NC = SEQ // CH
ALPHA = 2.0 ** 0.25
EPS = 1e-5
BIG = 1e30
ROUND = 1.5 * 2.0 ** 23
SLOPE = [[2.0 ** (-8.0 * (4 * g + h + 1) / 12) for h in range(HEADS)] for g in range(N_GROUPS)]

PAN_SSM, PAN_POOL, PAN_POOLG, PAN_POOLB, PAN_QKV = 0, 4, 8, 16, 24
PAN_GLU, PAN_SSMBR, PAN_ATTG, PAN_ATTB, PAN_OUT = 42, 46, 62, 70, 72
PAN_FF, PAN_DOWN, PAN_END = 80, 124, 156
OUT_ATTB, OUT_OUT = PAN_ATTB, PAN_ATTB + 8
READ_FF = (OUT_OUT + 4) // 2
DOWN_K = (6, 6, 5, 5)
RAW, RING = 2, 4
POOL_ADDS = (1, 3)
STACK = {9: (0, [0]), 10: (0, [1]), 11: (0, [2]), 12: (0, [3]), 13: (1, [0]), 14: (1, [1]), 15: (1, [2]), 16: (1, [3]),
         17: (2, [0, 1]), 18: (2, [2, 3]), 19: (3, [0]), 20: (3, [1]), 21: (3, [2]), 22: (3, [3])}
SP_LAG = 6
LOOK = 3


def panel_blocks(p):
    if PAN_POOLB <= p < PAN_QKV or PAN_GLU <= p < PAN_SSMBR:
        return 4
    if PAN_SSMBR <= p < PAN_ATTG:
        return 8 if p % 2 == 0 else 4
    if p >= PAN_DOWN:
        return DOWN_K[(p - PAN_DOWN) % 4]
    return 8


def qkv_panel(p):
    n = p - PAN_QKV
    return (n % 9) // 3, n % 3, n // 9


AFTER = {
    -1: ["turn_params", "params", ("powers", 0)],
    9: ["pool_old", ("expand", 0), ("powers", 1)], 10: [("ssm_prep", 0)],
    11: [("ssm_in", 0), ("expand", 1), ("scan", 0), "pool_diff"],
    12: [("ssm_prep", 1), ("powers", 2)], 13: [("ssm_in", 1), ("ssm_out", 0), ("expand", 2)], 14: ["pool_mix"],
    15: [("scan", 1), ("ssm_prep", 2), ("powers", 3)], 16: [("ssm_in", 2)], 17: [("ssm_out", 1), ("expand", 3)],
    18: [("scan", 2)], 19: [("ssm_prep", 3)], 20: [("ssm_in", 3), ("ssm_out", 2)], 21: [("scan", 3)], 22: [("ssm_out", 3)],
    24: [("gelu", 0)], 25: [("gelu", 1)], 26: [("gelu", 2)], 27: [("gelu", 3)], 28: ["gelu_split"], 29: ["bias"],
    53: ["decode_consts"],
}
ATT_STEPS = [(h, i) for h in range(HEADS) for i in reversed(range(NT))]


def keys_of(g, i):
    return [kt for kt in range(NT) if kt <= i and (g or kt >= i - 1)]


def quads_of(n):
    blocks = [(g, kt) for g in range(N_GROUPS) for kt in keys_of(g, ATT_STEPS[n][1])]
    return [blocks[m:m + 4] for m in range(0, len(blocks), 4)]


def inner_steps():
    out = {}
    slots = [(p, k) for p in range(PAN_QKV + 9, PAN_ATTB) for k in range(panel_blocks(p))]
    where = 0
    for hc in range(2):
        if hc:
            where = slots.index((PAN_GLU, 0))
        parts = [[("v_tokens", hc, i)] for i in range(NT)] + [[("k_tokens", hc, i)] for i in range(NT)]
        steps = range(8 * hc, 8 * hc + 8)
        for n in list(steps) + [None]:
            before = None if n == steps[0] else (steps[-1] if n is None else n - 1)
            lead = [] if before is None else [("normalise", before)]
            if n is not None:
                parts += [lead + [("scores", n, 0)], [("scores", n, 1)], [("scores", n, 2)], []]
                lead = [("exp", n)]
            if before is not None:
                m = len(quads_of(before))
                if n is None:
                    parts += [lead + [("probs", before, 0)]]
                    lead = []
                else:
                    parts += [[("probs", before, 0)]]
                parts += [[("probs", before, j)] for j in range(1, m)] + [lead + [("probs", before, m)]]
            else:
                parts[-1] = lead
        for part in parts:
            out.setdefault(slots[where], []).extend(part)
            where += 1
        assert slots[where - 1] < (PAN_GLU, 0) or hc and slots[where - 1] < (PAN_DEC, 0)
    out[PAN_DEC, 0], out[PAN_DEC, 3], out[PAN_DEC + 1, 0] = [("decode_rep", 0)], [("decode_rep", 1)], [("decode_rep", 2)]
    out[PAN_DEC + 1, 3] = [("decode_own", 0)]
    at = slots.index((PAN_DEC + 2, 0))
    for n in range(12):
        out[slots[at + n]] = [("decode_spread", n)]
    out[PAN_DEC + 5, 0] = [("decode_scores", 0)]
    out[PAN_DEC + 7, 0] = [("decode_softmax", 0)]
    out[PAN_DEC + 8, 2] = [("decode_out", 0)]
    return out


PAN_DEC = 54
INNER = inner_steps()


def build(nc, ins, outs):
    (x_prompt, x_sample, ck128, cv128, ck512, cv512, ck2048, cv2048, state_pool, ssm_re, ssm_im, w_in, pool_w,
     pool_scale, lam_re, lam_im, b_re, b_im, c_re, c_im, ssm_d, log_step, w_glu, w_br_att, w_br_pool,
     w_br_ssm, w_out, ln1_g, ln1_b, w_gate, w_up, w_down, ln2_g, ln2_b) = ins
    (y_p, y_s, k128_p, v128_p, k512_p, v512_p, k2048_p, v2048_p, pool_p, ssmre_p, ssmim_p,
     k128_s, v128_s, k512_s, v512_s, k2048_s, v2048_s, pool_s, ssmre_s, ssmim_s) = outs
    cache_k, cache_v = (ck128, ck512, ck2048), (cv128, cv512, cv2048)
    kp, vp = (k128_p, k512_p, k2048_p), (v128_p, v512_p, v2048_p)
    ks, vs = (k128_s, k512_s, k2048_s), (v128_s, v512_s, v2048_s)

    ctx = ExitStack()
    with ctx:
        ctx.enter_context(nc.allow_non_contiguous_dma(reason="per-feature vectors: one element per partition"))
        place = [((nc.sbuf_base + 31) // 32) * 32]

        def at(name, shape, dt, offset=None):
            size = 4 * int(np.prod(shape[1:]))
            where = place[0] if offset is None else offset
            if offset is None:
                place[0] += (size + 31) // 32 * 32
            return nc.alloc_sbuf_tensor_at(name, shape, dt, offset=where)

        def region(size):
            where = place[0]
            place[0] += (size + 31) // 32 * 32
            return where

        raw = at("raw", [P, RAW, 1024], F32)
        w_hi = at("w_hi", [P, RING, 1024], F32R)
        w_lo = at("w_lo", [P, RING, 1024], F32R)
        r_xhi, r_xlo = region(4 * KD * T), region(4 * KD * T)
        x_hi = at("x_hi", [P, KD, T], F32R, r_xhi)
        x_lo = at("x_lo", [P, KD, T], F32R, r_xlo)
        r_z = region(4 * KD * T)
        z = at("z", [P, KD, T], F32, r_z)
        tg = at("tg", [P, 2, T], F32)
        tw = at("tw", [P, 2, T], F32)
        ident = at("ident", [P, P], F32)
        ones = at("ones", [P, P], F32)
        vecs = at("vecs", [P, 48], F32)
        rcnt = at("rcnt", [P, 4, 16], F32)
        wsel = at("wsel", [P, 4, DEC], F32)
        r_dec = region(6016)
        hmask = at("hmask", [32, 4, E], F32, r_dec)
        sc32 = at("sc32", [32, 3 * P], F32, r_dec + 1024)
        dist32 = at("dist32", [32, 3 * P], F32)
        small = at("small", [P, 64], F32)
        pt32 = at("pt32", [P, 3, 32], F32, r_dec + 2560)
        diag32 = at("diag32", [32, 3, 32], F32, r_dec + 2944)
        s32 = at("s32", [P, 3, 32], F32, r_dec + 3328)
        stage_dec = at("stage_dec", [32, 512], F32)
        ln1g, ln1b, ln2g, ln2b = (vecs[:, 8 * n:8 * n + 8] for n in range(4))
        pscale, dskip = vecs[:, 32:36], vecs[:, 36:40]

        dexp = at("dexp", [P, 3, 2, 3, 32], F32, r_dec + 3712)
        hfin = at("hfin", [P, 2, 36], F32)
        rotk = at("rotk", [P, 6, 2, 16], F32)
        oldsum = at("oldsum", [P, 4, DEC], F32)
        ein1 = at("ein1", [P, 2, 4, NC], F32)
        dec01 = at("dec01", [P, 4, NC], F32)
        r1, r2, r3 = region(36096), region(18432), region(16640)
        r_u, r_y, r4 = region(8320), region(8320), region(23840)
        assert place[0] <= nc.sbuf_usable_end, place[0]
        xtok = at("xtok", [P, NT, D], F32, r2)
        xstok = at("xstok", [DEC, D], F32, r3)
        bp = at("bp", [P, 2, 4, CH, 32], F32, r1)
        bt = [at(f"bt{n}", [P, 4, 2, P], F32, r1 + 8192 + 4096 * n) for n in range(2)]
        cp = [at(f"cp{m}", [P, CH + 1, 2, 4, 32], F32, (r1 + 16384, r3)[m]) for m in range(2)]
        kbd = [at(f"kbd{m}", [P, CH, P], F32, (r1 + 25600, r3 + 9216)[m]) for m in range(2)]
        bpc = tg[:, :, :].rearrange("p a b -> p (a b)")[:, 0:CH * P].rearrange("p (k n q c) -> p k n q c", k=CH, n=2, q=4)
        cpc = at("cpc", [P, CH + 1, 2, 4, 16], F32, r_dec)
        t1 = at("t1", [P, 1024], F32, r1 + 29696)
        t2 = tw[:, :, :].rearrange("p a b -> p (a b)")
        wide = [a[:, 0:SEQ + 16] for a in (t1, t2)]
        spool = at("spool", [120, 512], F32, r1 + 33792)
        ust = [at(f"ust{ct}", [P, 4, 2, NC + DEC], F32, b) for ct, b in enumerate((r2, r1 + 33792, r4 + 21536))]
        ust.append(ust[1])
        poolw = at("poolw", [P, 4, P], F32, r3 + 13312)
        upool = at("upool", [P, 4, 16 + T], F32, r4)
        ein = [at("ein0", [P, 2, 4, NC], F32, r4 + 8704), ein1]
        dec0 = [at("dec00", [P, 4, NC], F32, r4 + 10752), dec01]
        vsb = at("vsb", [P, 4, 2 * 72], F32, r4 + 11776)
        wrot = at("wrot", [P, 2, 4, NC], F32, r4 + 14080)
        grot = at("grot", [P, 2, 4, NC], F32, r4 + 16128)
        hst = at("hst", [P, 2, 4, 73], F32, r4 + 18176)
        st_out = at("st_out", [36, 2, P], F32, r4 + 20512)
        bbar = at("bbar", [P, 2, 16, 16], F32, r_y)
        cc = at("cc", [P, 2, 16, 16], F32, r_y + 2048)
        h0 = at("h0", [P, 2, DEC, 16], F32, r_y + 4096)
        par = at("par", [P, 34, 16], F32, r_y + 5120)
        braw = at("braw", [P, 2, 16, 16], F32, r1 + 16384)
        craw = at("craw", [P, 2, 4, 2, E], F32, r1 + 18432)
        h0raw = at("h0raw", [P, 2, P], F32, r1 + 22528)
        lrow = at("lrow", [16, 3, P], F32, r1 + 23552)
        srow = at("srow", [16, 2], F32, r1 + 25088)
        u_ssm = at("u_ssm", [P, 4, T], F32, r_u)
        yp_hi = at("yp_hi", [P, 4, T], F32R, r2)
        yp_lo = at("yp_lo", [P, 4, T], F32R, r2 + 8320)
        ys_hi = at("ys_hi", [P, 4, T], F32R, r3)
        ys_lo = at("ys_lo", [P, 4, T], F32R, r3 + 8320)
        q_t = at("q_t", [P, 2, 3, T], F32, r1)
        k_t = at("k_t", [P, 2, 3, T], F32, r1 + 12480)
        v_t = at("v_t", [P, 3, T], F32, r1 + 24960)
        reps = [at("qrep", [32, 3, 256], F32, r1 + 31232), at("krep", [32, 3, 256], F32, r4 + 16384),
                at("vrep", [32, 3, 256], F32, r4 + 19456)]
        v_tok = at("v_tok", [P, NT, 3, 256], F32, r2)
        k_tok = at("k_tok", [P, NT, 3, P], F32, r2 + 12288)
        ya_hi = at("ya_hi", [P, 2, T], F32R, r_y)
        ya_lo = at("ya_lo", [P, 2, T], F32R, r_y + 4160)
        cbuf = [at(f"cbuf{n}", [P, DEC, 256], F32, b) for n, b in enumerate((r1, r1 + 8192, r1 + 16384, r4, r4 + 8192))]
        cbuf.append(cbuf[0])
        tga = at("tga", [P, KD, T], F32, r2)
        td = at("td", [P, 3, 512], F32, r4 + 14336)
        sc = at("sc", [P, 2, 1280], F32, r4)
        ptr = at("ptr", [P, 2, 512], F32, r4 + 10240)
        tdi = at("tdi", [P, 512], I32, r4)
        m_hi = at("m_hi", [P, KD, T], F32R, r1)
        m_lo = at("m_lo", [P, KD, T], F32R, r1 + 16640)
        assert r1 + 33280 <= r2
        f_hi = at("f_hi", [P, KF, T], F32R, r1)
        f_lo = at("f_lo", [P, KF, T], F32R, r1 + 45760)
        (L_SHIFT, L_ACC, L_ACCQ, L_SQ, L_RSTD, L_OFF, L_MEAN) = (0, 1, 2, 3, 5, 6, 7)
        lnr = at("lnr", [P, 8, T], F32, r2)
        ztok = at("ztok", [P, NT, D], F32, r_xhi)
        zdec = at("zdec", [DEC, D], F32, r_xlo)
        gb = at("gb", [P, 2, D], F32, r1 + 91520)
        stats = at("stats", [P, NT + 1, KD, 6], F32, r1 + 91520 + 8192)
        mv = at("mv", [P, NT + 1, 2], F32, r1 + 91520 + 8192 + 960)
        rn = at("rn", [P, 2, NT + 1], F32, r1 + 91520 + 8192 + 1024)
        assert r1 + 91520 + 9280 <= r4 + 23840

        ps = ctx.enter_context(nc.psum_tensor("ps", [P, 8, 512], F32))

        def pair(n):
            return ps[:, 2 * n:2 * n + 2, 0:HALF]

        def rows(a):
            return a.rearrange("p (h t) -> p h t", h=2)

        sems = {}

        def sem(name):
            if name not in sems:
                sems[name] = ctx.enter_context(nc.semaphore(name))
            return sems[name]

        raw_full = [sem(f"raw_full{n}") for n in range(RAW)]
        hi_done, lo_done = sem("hi_done"), sem("lo_done")
        panel_done = sem("panel_done")
        drained = [sem(f"drained{n}") for n in range(4)]
        x_in, par_in, vec_in = sem("x_in"), sem("par_in"), sem("vec_in")
        consts = sem("consts")

        def w_view(w):
            return w[0].rearrange("(k p) n -> p k n", p=P)

        v_in, v_out, v_glu = w_view(w_in), w_view(w_out), w_view(w_glu)
        v_bra, v_brp, v_brs = w_view(w_br_att), w_view(w_br_pool), w_view(w_br_ssm)
        v_gate, v_up, v_down = w_view(w_gate), w_view(w_up), w_view(w_down)

        def panel_source(p):
            if p < PAN_POOL:
                return v_in[:, :, COL_SSM + P * p:COL_SSM + P * (p + 1)]
            if p < PAN_POOLG:
                c = COL_POOL + P * (p - PAN_POOL)
                return v_in[:, :, c:c + P]
            if p < PAN_POOLB:
                c = COL_GATE + D + P * (p - PAN_POOLG)
                return v_in[:, :, c:c + P]
            if p < PAN_QKV:
                return v_brp[:, :, P * (p - PAN_POOLB):P * (p - PAN_POOLB + 1)]
            if p < PAN_GLU:
                kind, g, hc = qkv_panel(p)
                c = (0, COL_K, COL_V)[kind] + 256 * g + P * hc
                return v_in[:, :, c:c + P]
            if p < PAN_SSMBR:
                return v_glu[:, :, P * (p - PAN_GLU):P * (p - PAN_GLU + 1)]
            if p >= PAN_ATTB:
                return v_bra[:, :, 512 * (p - PAN_ATTB):512 * (p - PAN_ATTB + 1)]
            if p >= PAN_ATTG:
                return v_in[:, :, COL_GATE + P * (p - PAN_ATTG):COL_GATE + P * (p - PAN_ATTG + 1)]
            c = (p - PAN_SSMBR) // 2 * P
            return v_brs[:, :, c:c + P] if p % 2 else v_in[:, :, COL_GATE + 2 * D + c:COL_GATE + 2 * D + c + P]

        block = ctx.enter_context(nc.Block())

        @block.sync
        def _(sp):
            def load(p, slot, src, blocks, wait, rows_of=None):
                if wait is not None:
                    sp.wait_ge(lo_done, wait)
                dst = raw[:, slot, 0:blocks * P].rearrange("p (k n) -> p k n", k=rows_of or blocks)
                sp.dma_start(dst, src).then_inc(raw_full[slot], 16)

            sent = {}

            def store(dst, src, name):
                sent[name] = sent.get(name, 0) + 16
                sp.dma_start(dst, src).then_inc(sem(name), 16)

            for p in range(RAW):
                load(p, p, panel_source(p), panel_blocks(p), None)
            loads = [
                (lrow[:, 0, :], lam_re[0].rearrange("(a g) p -> a (g p)", g=2)),
                (lrow[:, 1, :], lam_im[0].rearrange("(a g) p -> a (g p)", g=2)),
                (srow[:, :], log_step[0].rearrange("(a g) -> a g", g=2)),
            ]
            for n, (b, c, h) in enumerate(((b_re, c_re, ssm_re), (b_im, c_im, ssm_im))):
                loads.append((braw[:, n, :, :], b[0].rearrange("(a g) p h -> (g p) a h", g=2)))
                for m in range(2):
                    loads.append((craw[:, n, :, m, :], c[0].rearrange("(t g) h p -> (g h) t p", t=4)))
                loads.append((h0raw[:, n, :], h[0].rearrange("b (a g) p -> (b a) (g p)", g=2)))
            for dst, src in loads:
                sp.dma_start(dst, src).then_inc(par_in, 16)
            assert len(loads) == N_PAR
            loads = [(spool[:, :], state_pool[0].rearrange("b r c -> (b r) c")),
                     (poolw[:, :, :], pool_w[0].rearrange("g c e -> c g e")),
                     (dskip, ssm_d[0].rearrange("(k p) -> p k", p=P)),
                     (pscale, pool_scale[0].rearrange("(k p) -> p k", p=P))]
            for n, vec in enumerate((ln1_g, ln1_b, ln2_g, ln2_b)):
                loads.append((vecs[:, 8 * n:8 * n + 8], vec[0].rearrange("(k p) -> p k", p=P)))
            for dst, src in loads:
                sp.dma_start(dst, src).then_inc(vec_in, 16)
            assert len(loads) == N_VEC

            def stack(ct, pairs):
                if ct < 3:
                    sp.wait_ge(sem("stack_zeros"), (1, 3, 2)[ct])
                else:
                    sp.wait_ge(sem("v_formed"), 2)
                for q in pairs:
                    r = slice(32 * q, 32 * q + 32)
                    for a in range(4):
                        sp.dma_start(ust[ct][32 * a:32 * a + 32, q, :, 0:NC],
                                     u_ssm[r, ct, 0:SEQ].rearrange("p (j s c) -> p j s c", j=2, s=4)[:, :, 3 - a, :]
                                     ).then_inc(sem(f"stacked{ct}"), 16)
                    sp.dma_start(ust[ct][0:32, q, 1, NC:], u_ssm[r, ct, SEQ:T]).then_inc(sem(f"stacked{ct}"), 16)

            def cache_load(n):
                g, cache = n % 3, (cache_k, cache_v)[n // 3]
                keys, step = (P, DILATION[g]) if g < 2 else (PAST // DILATION[2], DILATION[2])
                src = cache[g][0].rearrange("b (r s) h e -> r s b (h e)", s=step)[:, 0]
                sp.dma_start(cbuf[n][0:keys, :, :], src).then_inc(sem(f"cache_in{n}"), 16)

            for p in range(RAW, PAN_OUT):
                load(p, p % RAW, panel_source(p), panel_blocks(p), p - RAW + 1, 2 if p >= PAN_ATTB else None)
                for step in AFTER.get(p - SP_LAG, []) + [x for k in range(8) for x in INNER.get((p - SP_LAG, k), [])]:
                    if step[0] == "ssm_out":
                        ct = step[1]
                        sp.wait_ge(sem("state_staged"), ct + 1)
                        for n, (prompt, sample) in enumerate(((ssmre_p, ssmre_s), (ssmim_p, ssmim_s))):
                            store(prompt[0, 0].rearrange("(a g) p -> a (g p)", g=2)[4 * ct:4 * ct + 4], st_out[0:4, n, :],
                                  f"state_sent{ct}")
                            store(sample[0].rearrange("b (a g) p -> b a (g p)", g=2)[:, 4 * ct:4 * ct + 4],
                                  st_out[4:36, n, :], f"state_sent{ct}")
                    if step == "pool_old":
                        sp.wait_ge(sem("pool_staged"), 1)
                        store(pool_p[0, 0], stage_dec[0:PBUF, :], "pool_sent")
                        store(pool_s[0].rearrange("b s c -> (b s) c"), stage_dec[PBUF:PBUF + DEC, :], "pool_sent")
                    if step[0] in ("v_tokens", "k_tokens"):
                        name, hc, i = step
                        sp.wait_ge(sem(name), NT * hc + i + 1)
                        c = slice(P * hc, P * hc + P)
                        for g in range(N_GROUPS):
                            if g or i == NT - 1:
                                dst = (vp, kp)[name == "k_tokens"][g][0, 0].rearrange("t h e -> t (h e)")
                                t0 = 0 if g == 0 else P * i
                                store(dst[t0:t0 + P, c], k_tok[:, i, g, :] if name == "k_tokens" else v_tok[:, i, g, c],
                                      f"{name}_sent{hc}")
                if p == 9:
                    sp.wait_ge(drained[0], 2)
                    sp.wait_ge(drained[1], 2)
                if p in STACK:
                    stack(*STACK[p])
                if p == PAN_DEC + 6:
                    sp.wait_ge(sem("o_split"), len(ATT_STEPS))
                    for n in range(5):
                        cache_load(n)
                if p == PAN_DEC + 8:
                    sp.wait_ge(sem("reps_done"), 3)
                    for g in range(N_GROUPS):
                        store(ks[g][0].rearrange("b s h e -> b (s h e)"), reps[1][0:32:4, g, :], "reps_sent")
                        store(vs[g][0].rearrange("b s h e -> b (s h e)"), reps[2][0:32:4, g, :], "reps_sent")
                if p == PAN_DEC + 10:
                    sp.wait_ge(sem("cache_scored"), 1)
                    cache_load(5)

            with sp.Fori(0, KD // 2) as i:
                for j in range(2):
                    load(None, j, v_out[:, :, bass.ds(i * (2 * P) + P * j, P)], 8, i * 2 + (PAN_OUT + j - RAW + 1))
            sp.wait_ge(sem("decode_done"), 1)
            sp.wait_ge(sem("reps_sent"), 16 * 2 * N_GROUPS)
            for n, vec in enumerate((ln2_g, ln2_b)):
                sp.dma_start(gb[:, n, :], vec[0].unsqueeze(0).broadcast_to([P, D])).then_inc(sem("gb_in"), 16)
            with sp.Fori(0, KF) as i:
                for j, view in enumerate((v_gate, v_up)):
                    load(None, j, view[:, :, bass.ds(i * P, P)], 8, i * 2 + (PAN_FF + j - RAW + 1))
            with sp.Fori(0, KD) as i:
                k0 = 0
                for j, blocks in enumerate(DOWN_K):
                    load(None, j % 2, v_down[:, k0:k0 + blocks, bass.ds(i * P, P)], blocks, i * 4 + (PAN_DOWN + j - RAW + 1))
                    k0 += blocks
            for i in range(NT + 1):
                if i in POOL_ADDS:
                    sp.wait_ge(sem("y_added_pool"), POOL_ADDS.index(i) + 1)
                else:
                    sp.wait_ge(sem("y_added"), len([n for n in range(i + 1) if n not in POOL_ADDS]))
                if i < NT:
                    store(y_p[0, P * i:P * i + P, :], ztok[:, i, :], f"y_sent{i}")
                else:
                    store(y_s.rearrange("b s d -> (b s) d"), zdec[:, :], f"y_sent{i}")
            for name, value in sent.items():
                sp.wait_ge(sem(name), value)

        @block.gpsimd
        def _(pool):
            count = [0]

            def link(ins):
                count[0] += 1
                ins.then_inc(sem("pool_seq"), 1)
                pool.wait_ge(sem("pool_seq"), count[0])

            def lo(slot, raw_slot, blocks, n):
                pool.wait_ge(hi_done, n + 1)
                nc.gpsimd.tensor_tensor(w_lo[:, slot, 0:blocks * P], raw[:, raw_slot, 0:blocks * P],
                                        w_hi[:, slot, 0:blocks * P].bitcast(F32), ALU.subtract).then_inc(lo_done, 1)

            nc.gpsimd.memset(ones[:, :], 1.0).then_inc(consts, 1)
            pool.wait_ge(consts, 1)
            nc.gpsimd.affine_select(out=ident[:, :], in_=ones[:, :], compare_op=ALU.is_equal, fill=0.0, base=0,
                                    pattern=[[-1, P]], channel_multiplier=1).then_inc(consts, 1)
            for p in range(2):
                lo(p % RING, p % RAW, panel_blocks(p), p)
            for g, w in enumerate(POOL_W):
                link(nc.gpsimd.affine_select(out=wsel[:, g, :], in_=ones[:, 0:DEC], compare_op=ALU.is_ge, fill=0.0,
                                             base=-(PBUF - w + 1), pattern=[[-PBUF, DEC]], channel_multiplier=1))
                link(nc.gpsimd.affine_select(out=wsel[:, g, :], in_=wsel[:, g, :], compare_op=ALU.is_ge, fill=0.0,
                                             base=PBUF - 1, pattern=[[PBUF, DEC]], channel_multiplier=-1))
            link(nc.gpsimd.iota(rcnt[:, 0, :], pattern=[[1, 16]], base=1, channel_multiplier=0,
                                allow_small_or_imprecise_dtypes=True))
            link(nc.gpsimd.iota(dist32[:, 0:128], pattern=[[-1, P]], base=P, channel_multiplier=0,
                                allow_small_or_imprecise_dtypes=True))
            link(nc.gpsimd.iota(dist32[:, 128:256], pattern=[[-4, P]], base=4 * P, channel_multiplier=0,
                                allow_small_or_imprecise_dtypes=True))
            nc.gpsimd.iota(dist32[:, 256:288], pattern=[[-16, 32]], base=512, channel_multiplier=0,
                           allow_small_or_imprecise_dtypes=True).then_inc(consts, 1)

            def bias_tables():
                pool.wait_ge(sem("state_turned"), 4)
                pool.wait_ge(sem("pool_split"), 4)
                link(nc.gpsimd.iota(tdi[:, :], pattern=[[-1, 512]], base=384, channel_multiplier=1))
                link(nc.gpsimd.iota(td[:, 1, :], pattern=[[-1, 512]], base=384, channel_multiplier=1,
                                    allow_small_or_imprecise_dtypes=True))
                link(nc.gpsimd.affine_select(out=td[:, 1, :], in_=td[:, 1, :], compare_op=ALU.is_ge, fill=BIG,
                                             base=384, pattern=[[-1, 512]], channel_multiplier=1))
                nc.gpsimd.affine_select(out=td[:, 0, :], in_=td[:, 1, :], compare_op=ALU.is_ge, fill=BIG,
                                        base=BACK - 384, pattern=[[1, 512]], channel_multiplier=-1
                                        ).then_inc(sem("td_base"), 1)

            for p in range(2, PAN_OUT):
                lo(p % RING, p % RAW, panel_blocks(p), p)
                for step in AFTER.get(p - 4, []):
                    if step == "bias":
                        bias_tables()
            for p in range(PAN_OUT, PAN_FF + LOOK):
                lo(p % RING, p % RAW, 8, p)
            for c in range(KD):
                pool.wait_ge(sem("x1_high"), c + 1)
                nc.gpsimd.tensor_tensor(x_lo[:, c, :], z[:, c, :], x_hi[:, c, :].bitcast(F32), ALU.subtract
                                        ).then_inc(sem("x1_split"), 1)
            lo(LOOK % RING, LOOK % RAW, 8, PAN_FF + LOOK)
            with pool.Fori(0, KF // 2 - 1) as i:
                for j in range(4):
                    lo((PAN_FF + j) % RING, j % RAW, 8, i * 4 + (PAN_FF + 4 + j))
            with pool.Fori(0, KD) as i:
                for j in range(4):
                    lo((PAN_DOWN + j) % RING, j % RAW, DOWN_K[j], i * 4 + (PAN_DOWN + j))
            for n, t in enumerate(POOL_ADDS):
                pool.wait_ge(sem("y_scaled"), t + 1)
                nc.gpsimd.tensor_tensor(ztok[:, t, :], ztok[:, t, :], gb[:, 1, :], ALU.add).then_inc(sem("y_added_pool"), 1)

        @block.tensor
        def _(pe):
            mm = nc.tensor.matmul

            def tr(out, in_):
                n = in_.partition_size()
                return nc.tensor.transpose(out, in_, ident[0:n, 0:n])

            def multiply(slot, blocks, hi, lo, out_pair, k0=0, first=True, last=True, inner=None,
                         ready=None, middle=None):
                for k in range(blocks):
                    if ready is not None:
                        pe.wait_ge(ready, k + 1)
                    wh, wl = (w[:, slot, P * k:P * k + P] for w in (w_hi, w_lo))
                    for m, (w, x) in enumerate(((wh, hi), (wh, lo), (wl, hi))):
                        for h in range(2):
                            ins = mm(ps[:, 2 * out_pair + h, 0:HALF], w, x[:, k0 + k, HALF * h:HALF * (h + 1)],
                                     start=(first and k == 0 and m == 0), stop=(last and k == blocks - 1 and m == 2))
                    if inner is not None:
                        if k == blocks - 1:
                            ins.then_inc(panel_done, 1)
                        for step in INNER.get((inner, k), []):
                            run(step)
                    if middle is not None and k == 4:
                        middle()
                return ins

            def panel(p, hi, lo, wait=True):
                pe.wait_ge(lo_done, p + 1)
                if p >= 2:
                    pe.wait_ge(drained[p % 2], p // 2)
                multiply(p % RING, panel_blocks(p), hi, lo, p % 2, inner=p)

            pe.wait_ge(consts, 2)
            for i in range(NT):
                pe.wait_ge(sem(f"x_in{i}"), 16)
                for c in range(KD):
                    ins = tr(ps[:, 2 * i + c // 4, P * (c % 4):P * (c % 4) + P], xtok[:, i, P * c:P * c + P])
                ins.then_inc(sem("x_turned"), 1)
            pe.wait_ge(x_in, 16)
            pe.wait_ge(sem("x_split"), 1)
            for c in range(KD):
                ins = tr(ps[:, 0, DEC * c:DEC * c + DEC], xstok[0:DEC, P * c:P * c + P])
            ins.then_inc(sem("x_turned"), 1)

            def turn_params():
                pe.wait_ge(sem("x_split"), NT)
                pe.wait_ge(par_in, 16 * N_PAR)
                pe.wait_ge(sem("steps_spread"), 1)
                for n in range(3):
                    ins = tr(ps[:, 4, 16 * n:16 * n + 16], lrow[:, n, :])
                ins.then_inc(sem("lam_turned"), 1)
                for n in range(2):
                    for ct in range(4):
                        ins = tr(ps[:, 5 + n, P * ct:P * ct + P], craw[:, n, ct, :, :].rearrange("p g e -> p (g e)"))
                ins.then_inc(sem("c_turned"), 1)
                for n in range(2):
                    ins = tr(ps[:, 7, P * n:P * n + P], h0raw[:, n, :])
                ins.then_inc(sem("h0_turned"), 1)

            def ssm_prep(ct):
                m = ct % 2
                pe.wait_ge(sem("spread"), ct + 1)
                if ct == 0:
                    pe.wait_ge(sem("par_read"), 3)
                    pe.wait_ge(sem("psum_old_read"), 1)
                    pe.wait_ge(sem("pool_staged"), 1)
                else:
                    pe.wait_ge(sem("v_copied"), ct)
                    pe.wait_ge(sem("k_copied"), ct)
                if ct == 2:
                    pe.wait_ge(sem("pool_scaled"), 4)
                if ct >= 2:
                    pe.wait_ge(sem("y_read"), ct - 1)
                    pe.wait_ge(sem("state_staged"), ct - 1)
                for n in range(2):
                    for k in range(CH):
                        q, half = k // 2, k % 2
                        ins = tr(ps[:, 4 + 2 * n + q // 2, P * (k % 4):P * (k % 4) + P],
                                 bp[:, n, q, 4 * half:4 * half + 4, :].rearrange("p k c -> p (k c)"))
                ins.then_inc(sem("bt_turned"), 1)
                pe.wait_ge(sem("bt_copied"), ct + 1)
                for q in range(4):
                    for n in range(2):
                        ins = mm(ps[32 * q:32 * q + 32, 4, 0:256], bp[:, n, q, 0, :], cp[m][:, 0:CH, n, q, :],
                                 start=n == 0, stop=n == 1)
                ins.then_inc(sem("k_formed"), 1)

            def ssm_in(ct):
                pe.wait_ge(sem(f"stacked{ct}"), 16 * 20)
                for q in range(4):
                    for n in range(2):
                        c = 144 * (q % 2) + 72 * n
                        mm(ps[:, 6 + q // 2, c:c + 72], bt[n][:, q, 0, :], ust[ct][:, q, 1, :],
                           start=True, stop=False, skip_group_check=True)
                        ins = mm(ps[:, 6 + q // 2, c:c + NC], bt[n][:, q, 1, :], ust[ct][:, q, 0, 0:NC],
                                 start=False, stop=True, skip_group_check=True)
                ins.then_inc(sem("v_formed"), 1)

            def ssm_out(ct):
                m = ct % 2
                pe.wait_ge(sem("h_done"), ct + 1)
                if ct < 3:
                    pe.wait_ge(sem("k_copied"), ct + 2)
                    pe.wait_ge(sem("v_copied"), ct + 2)
                else:
                    pe.wait_ge(sem("y_read"), ct)
                    pe.wait_ge(sem("state_staged"), ct)
                if ct == 2:
                    pe.wait_ge(sem("y_read"), ct)
                for j in range(CH):
                    mm(ps[:, 4, NC * j:512], kbd[m][:, j, :], u_ssm[:, ct, 0:NC * (CH - j)],
                       start=j == 0, stop=False, skip_group_check=True)
                for t in range(CH):
                    for n in range(2):
                        for q in range(4):
                            r = slice(32 * q, 32 * q + 32)
                            mm(ps[r, 4, NC * t:NC * t + NC], cp[m][:, t + 1, n, q, :], hst[:, n, q, 0:NC],
                               start=False, stop=n == 1, skip_group_check=True)
                for q in range(4):
                    for n in range(2):
                        ins = mm(ps[32 * q:32 * q + 32, 5, 0:DEC], cp[m][:, 0, n, q, :], hst[:, n, q, 65:73],
                                 start=n == 0, stop=n == 1)
                ins.then_inc(sem("y_formed"), 1)
                for n in range(2):
                    ins = tr(ps[0:36, 6, P * n:P * n + P], hfin[:, n, :])
                ins.then_inc(sem("state_turned"), 1)

            def pool_old():
                pe.wait_ge(consts, 3)
                pe.wait_ge(vec_in, 16 * N_VEC)
                pe.wait_ge(sem("par_read"), 3)
                pe.wait_ge(drained[0], PAN_POOLG // 2)
                pe.wait_ge(drained[1], PAN_POOLG // 2)
                for g in range(4):
                    ins = mm(ps[:, 4, DEC * g:DEC * g + DEC], spool[0:120, P * g:P * g + P], wsel[0:120, g, :],
                             start=True, stop=True)
                ins.then_inc(sem("psum_old"), 1)
                for g in range(4):
                    ins = tr(ps[0:PBUF + DEC, 5, P * g:P * g + P], upool[:, g, 16 + SEQ - PBUF:16 + T])
                ins.then_inc(sem("pool_turned"), 1)

            def pool_mix():
                for g in range(4):
                    pe.wait_ge(sem("diff_done"), g + 1)
                    if g == 0:
                        pe.wait_ge(sem("y_read"), 1)
                        pe.wait_ge(sem("state_staged"), 1)
                        pe.wait_ge(sem("v_copied"), 2)
                    if g >= 2:
                        pe.wait_ge(sem("pool_scaled"), g - 1)
                    for h in range(2):
                        ins = mm(ps[:, 4 + 2 * (g % 2) + h, 0:HALF], poolw[:, g, :],
                                 upool[:, g, 16 + HALF * h:16 + HALF * (h + 1)], start=True, stop=True)
                    ins.then_inc(sem("pool_mixed"), 1)

            def v_tokens(hc, i):
                pe.wait_ge(drained[(PAN_QKV + 9 * hc + 8) % 2], (PAN_QKV + 9 * hc + 8) // 2 + 1)
                pe.wait_ge(drained[(PAN_QKV + 9 * hc + 7) % 2], (PAN_QKV + 9 * hc + 7) // 2 + 1)
                if hc == 0:
                    pe.wait_ge(sem("y_read"), 4)
                    pe.wait_ge(sem("state_staged"), 4)
                else:
                    pe.wait_ge(sem("o_split"), 8)
                for g in range(N_GROUPS):
                    ins = tr(ps[:, 4 + i, P * g:P * g + P], v_t[:, g, P * i:P * i + P])
                ins.then_inc(sem("v_turned"), 1)

            def k_tokens(hc, i):
                pe.wait_ge(sem("v_tokens"), NT * hc + i + 1)
                for g in range(N_GROUPS):
                    if g or i == NT - 1:
                        ins = tr(ps[:, 4 + i, P * g:P * g + P], k_t[:, hc, g, P * i:P * i + P])
                ins.then_inc(sem("k_turned"), 1)

            def decode_rep(n):
                if n == 0:
                    pe.wait_ge(sem("o_split"), len(ATT_STEPS))
                    pe.wait_ge(sem("decode_kept"), 6)
                if n == 2:
                    pe.wait_ge(sem("reps_done"), 1)
                b = 4 + 2 * (n % 2)
                for g in range(N_GROUPS):
                    for hc in range(2):
                        c = 256 * g + P * hc
                        ins = tr(ps[0:32, b + c // 512, c % 512:c % 512 + P], dexp[:, n, hc, g, :])
                ins.then_inc(sem("rep_turned"), 1)

            def decode_spread(n):
                g, b2 = n // 4, n % 4
                if n == 0:
                    pe.wait_ge(sem("reps_done"), 3)
                if n >= 4:
                    pe.wait_ge(sem("qk_read"), n - 3)
                for b in range(2):
                    ins = mm(ps[:, 4 + n % 4, 256 * b:256 * b + 256],
                             ident[0:32, 4 * (2 * b2 + b):4 * (2 * b2 + b) + 1].broadcast_to([32, P]),
                             reps[0][:, g, :], start=True, stop=True)
                ins.then_inc(sem("q_spread"), 1)

            def decode_scores():
                pe.wait_ge(sem("qk_read"), 12)
                for g in range(N_GROUPS):
                    pe.wait_ge(sem("cache_scored"), g + 1)
                    keys = P if g < 2 else 32
                    ins = tr(ps[0:32, 4, P * g:P * g + keys], s32[0:keys, g, :])
                ins.then_inc(sem("s_turned"), 1)

            def decode_softmax():
                pe.wait_ge(sem("p_done"), 1)
                for g in range(N_GROUPS):
                    keys = P if g < 2 else 32
                    ins = tr(ps[0:keys, 5, 32 * g:32 * g + 32], sc32[:, P * g:P * g + keys])
                ins.then_inc(sem("p_turned"), 1)

            def decode_out():
                pe.wait_ge(sem("p_copied"), 1)
                pe.wait_ge(sem("diag_done"), 1)
                for hc in range(2):
                    for g in range(N_GROUPS):
                        ins = mm(ps[:, 6 + hc, 0:16], reps[2][:, g, P * hc:P * hc + P],
                                 diag32[:, g, :].rearrange("r (b h) -> r b h", h=4)[:, :, 2 * hc:2 * hc + 2],
                                 start=g == 0, stop=False, skip_group_check=True)
                for g in range(N_GROUPS):
                    keys = P if g < 2 else 32
                    pe.wait_ge(sem(f"cache_in{3 + g}"), 16)
                    for hc in range(2):
                        for b in range(DEC):
                            ins = mm(ps[:, 6 + hc, 2 * b:2 * b + 2], cbuf[3 + g][0:keys, b, P * hc:P * hc + P],
                                     pt32[0:keys, g, 4 * b + 2 * hc:4 * b + 2 * hc + 2],
                                     start=False, stop=g == 2, skip_group_check=True)
                    ins.then_inc(sem("cache_summed"), 1)

            def scores(n, g):
                h, i = ATT_STEPS[n]
                r = slice(64 * (h % 2), 64 * (h % 2) + 64)
                if n % 8 == 0 and g == 0:
                    pe.wait_ge(sem("k_tokens"), NT * (n // 8 + 1))
                if n > 0 or g == 2:
                    pe.wait_ge(sem("scored"), 3 * n + (0, -1, 1)[g])
                keys = keys_of(g, i)
                mm(ps[:, 4 + g % 2, 0:P * len(keys)], q_t[r, h // 2, g, P * i:P * i + P],
                   k_t[r, h // 2, g, P * keys[0]:P * (i + 1)], start=True, stop=True
                   ).then_inc(sem("s_formed"), 1)

            def probs(n, m):
                h, i = ATT_STEPS[n]
                r = slice(64 * (h % 2), 64 * (h % 2) + 64)
                quads = quads_of(n)
                turned = sum(len(quads_of(j)) for j in range(n)) + m
                if m == 0:
                    pe.wait_ge(sem("p_normed"), n + 1)
                if turned:
                    pe.wait_ge(sem("pt_copied"), turned)
                if m < len(quads):
                    for j, _ in enumerate(quads[m]):
                        c = P * (4 * m + j)
                        ins = tr(ps[:, 7, P * j:P * j + P], sc[:, n % 2, c:c + P])
                    ins.then_inc(sem("pt_turned"), 1)
                if m >= 1:
                    if m == 1 and n >= 1:
                        pe.wait_ge(sem("o_split"), n)
                    for j, (g, kt) in enumerate(quads[m - 1]):
                        ins = mm(ps[r, 6, 0:P], v_tok[:, kt, g, 64 * h:64 * h + 64],
                                 ptr[:, (turned - 1) % 2, P * j:P * j + P],
                                 start=m == 1 and j == 0, stop=m == len(quads) and j == len(quads[-1]) - 1)
                    ins.then_inc(sem("pt_used"), 1)

            todo = {"turn_params": turn_params, "ssm_prep": ssm_prep, "ssm_in": ssm_in, "ssm_out": ssm_out,
                    "pool_old": pool_old, "pool_mix": pool_mix, "v_tokens": v_tokens, "k_tokens": k_tokens,
                    "scores": scores, "probs": probs, "decode_rep": decode_rep, "decode_spread": decode_spread,
                    "decode_scores": lambda _: decode_scores(), "decode_softmax": lambda _: decode_softmax(),
                    "decode_out": lambda _: decode_out()}

            def run(step):
                name, args = (step[0], step[1:]) if isinstance(step, tuple) else (step, ())
                if name in todo:
                    todo[name](*args)

            for step in AFTER[-1]:
                run(step)
            pe.wait_ge(sem("x_split"), NT + 1)
            for p in range(PAN_ATTB):
                if p == PAN_POOLB:
                    pe.wait_ge(sem("pool_split"), 4)
                if p == PAN_GLU:
                    pe.wait_ge(sem("gelu_split_done"), 4)
                if p == PAN_SSMBR + 1:
                    pe.wait_ge(sem("ys_split"), 4)
                rows_of = (x_hi, x_lo)
                if PAN_POOLB <= p < PAN_QKV:
                    rows_of = (yp_hi, yp_lo)
                if PAN_GLU <= p < PAN_SSMBR or (PAN_SSMBR <= p < PAN_ATTG and p % 2):
                    rows_of = (ys_hi, ys_lo)
                panel(p, *rows_of)
                for step in AFTER.get(p, []):
                    run(step)
            pe.wait_ge(sem("decode_done"), 1)
            for p in range(PAN_ATTB, PAN_OUT):
                pe.wait_ge(lo_done, p + 1)
                for o in range(4):
                    n = OUT_ATTB + 4 * (p - PAN_ATTB) + o
                    pe.wait_ge(drained[n % 2], n // 2)
                    for k in range(2):
                        wh, wl = (w[:, p % RING, 512 * k + P * o:512 * k + P * o + P] for w in (w_hi, w_lo))
                        for m, (w, x) in enumerate(((wh, ya_hi), (wh, ya_lo), (wl, ya_hi))):
                            for h in range(2):
                                ins = mm(ps[:, 2 * (n % 2) + h, 0:HALF], w, x[:, k, HALF * h:HALF * (h + 1)],
                                         start=k == 0 and m == 0, stop=k == 1 and m == 2)
                    ins.then_inc(sem("att_out") if o < 3 else panel_done, 1)

            def row_sum(n, row, start, stop):
                for h in range(2):
                    ins = mm(ps[:, 4 + 2 * n + h, 0:HALF], ones[:, :], row[:, HALF * h:HALF * (h + 1)], start=start, stop=stop)
                return ins

            def shift_sum():
                pe.wait_ge(sem("four_summed"), 1)
                row_sum(0, lnr[:, L_ACC, :], True, True).then_inc(sem("shift_formed"), 1)

            for c in range(KD):
                p, n = PAN_OUT + c, OUT_OUT + c
                pe.wait_ge(lo_done, p + 1)
                if c < 6:
                    pe.wait_ge(drained[n % 2], n // 2)
                else:
                    pe.wait_ge(sem("centred"), c - 1)
                multiply(p % RING, 8, m_hi, m_lo, n % 2, ready=sem("m_split") if c == 0 else None,
                         middle=shift_sum if c == 4 else None).then_inc(panel_done, 1)
            pe.wait_ge(sem("shift_read"), 1)
            pe.wait_ge(sem("square_used"), KD - 1)
            row_sum(0, lnr[:, L_ACC, :], True, False)
            row_sum(1, lnr[:, L_ACCQ, :], True, False)
            pe.wait_ge(sem("centred"), KD)
            row_sum(0, z[:, KD - 1, :], False, True).then_inc(sem("sum_done"), 1)
            pe.wait_ge(sem("squared"), KD)
            row_sum(1, lnr[:, L_SQ + 1, :], False, True).then_inc(sem("square_summed"), 1)
            with pe.Fori(0, KF // 2) as i:
                for j in range(4):
                    pe.wait_ge(lo_done, i * 4 + (PAN_FF + j + 1))
                    if j < 2:
                        pe.wait_ge(drained[j], i * 1 + READ_FF)
                    else:
                        pe.wait_ge(drained[j], i * 1 + 1)
                    multiply((PAN_FF + j) % RING, 8, x_hi, x_lo, j, ready=sem("x1_split") if j == 0 else None
                             ).then_inc(panel_done, 1)
            pe.wait_ge(sem("f_split"), KF)

            def turn(o, read, free):
                pe.wait_ge(drained[o], read)
                pe.wait_ge(drained[2 + o], free)
                for i in range(NT):
                    tr(ps[:, 4 + 2 * o, P * i:P * i + P], tw[:, o, P * i:P * i + P])
                tr(ps[0:DEC, 5 + 2 * o, 0:P], tw[:, o, SEQ:T]).then_inc(sem("z_turned"), 1)

            def down_turn(i, first):
                for o in range(2):
                    k0 = 0
                    for j, blocks in enumerate(DOWN_K):
                        pe.wait_ge(lo_done, i * 8 + (PAN_DOWN + 4 * o + j + 1))
                        if j == 0:
                            pe.wait_ge(drained[o], i * 1 + (READ_FF + KF // 2))
                        multiply((PAN_DOWN + j) % RING, blocks, f_hi, f_lo, o, k0, j == 0, j == 3).then_inc(panel_done, 1)
                        k0 += blocks
                        if j == 0 and o == 1:
                            turn(0, i * 1 + (READ_FF + KF // 2 + 1), i * 1 + (FF_READS + KF // 2))
                        if j == 0 and o == 0 and not first:
                            turn(1, i * 1 + (READ_FF + KF // 2), i * 1 + (FF_READS + KF // 2 - 1))

            down_turn(0, True)
            with pe.Fori(1, KD // 2) as i:
                down_turn(i, False)
            turn(1, READ_FF + KF // 2 + KD // 2, FF_READS + KF // 2 + KD // 2 - 1)

        @block.scalar
        def _(act):
            A = nc.scalar.activation

            def hi(slot, raw_slot, blocks, n, turn, used=None):
                act.wait_ge(raw_full[raw_slot], turn)
                if used is not None:
                    act.wait_ge(panel_done, used)
                A(w_hi[:, slot, 0:blocks * P], raw[:, raw_slot, 0:blocks * P], ACT.Copy).then_inc(hi_done, 1)

            def hi_static(p):
                if p < PAN_END:
                    hi(p % RING, p % RAW, panel_blocks(p), p, 16 * (p // RAW + 1), p - RING + 1 if p >= RING else None)

            for i in range(NT):
                act.dma_start(xtok[:, i, :], x_prompt[0, P * i:P * i + P, :]).then_inc(sem(f"x_in{i}"), 16)
            act.dma_start(xstok[:, :], x_sample.rearrange("b s d -> (b s) d")).then_inc(x_in, 16)
            for i in range(NT):
                act.wait_ge(sem("x_turned"), i + 1)
                A(x_hi[:, :, P * i:P * i + P], ps[:, 2 * i:2 * i + 2, :].rearrange("p b (c t) -> p (b c) t", t=P), ACT.Copy
                  ).then_inc(sem("x_high"), 1)
            act.wait_ge(sem("x_turned"), NT + 1)
            A(x_hi[:, :, SEQ:T], ps[:, 0, 0:DEC * KD].rearrange("p (c b) -> p c b", b=DEC), ACT.Copy).then_inc(sem("x_high"), 1)
            for p in range(2):
                hi_static(p)
            hi_static(2)

            def params():
                act.wait_ge(sem("angle_done"), 1)
                A(par[:, 6, :], par[:, 4, :], ACT.Sin).then_inc(sem("sin_done"), 1)
                A(par[:, 7, :], par[:, 5, :], ACT.Sin).then_inc(sem("sin_done"), 1)

            def evacuate(p):
                if p >= PAN_ATTB or PAN_POOLB <= p < PAN_QKV:
                    return
                act.wait_ge(panel_done, p + 1)
                b = 2 * (p % 2)
                if p < PAN_POOL:
                    u = u_ssm[:, p, 0:SEQ].rearrange("p (s c) -> p c s", s=CH)
                    A(u[:, 0:32, :], ps[:, b, 0:256].rearrange("p (c s) -> p c s", s=CH), ACT.Copy)
                    A(u[:, 32, 0:4], ps[:, b, 256:260], ACT.Copy)
                    A(u[:, 32, 4:8], ps[:, b + 1, 0:4], ACT.Copy)
                    A(u[:, 33:64, :], ps[:, b + 1, 4:252].rearrange("p (c s) -> p c s", s=CH), ACT.Copy)
                    A(u_ssm[:, p, SEQ:T], ps[:, b + 1, 252:260], ACT.Copy).then_inc(drained[p % 2], 1)
                elif p < PAN_POOLG:
                    A(rows(upool[:, p - PAN_POOL, 16:16 + T]), pair(p % 2), ACT.Copy).then_inc(drained[p % 2], 1)
                elif p < PAN_POOLB:
                    A(rows(z[:, p - PAN_POOLG, :]), pair(p % 2), ACT.Tanh, scale=0.5).then_inc(drained[p % 2], 1)
                elif p >= PAN_ATTG:
                    if p == PAN_ATTG:
                        for hc in range(2):
                            act.wait_ge(sem(f"v_tokens_sent{hc}"), 16 * 9)
                            act.wait_ge(sem(f"k_tokens_sent{hc}"), 16 * 9)
                    A(rows(tga[:, p - PAN_ATTG, :]), pair(p % 2), ACT.Tanh, scale=0.5).then_inc(drained[p % 2], 1)
                elif p >= PAN_SSMBR:
                    if p % 2 == 0:
                        if p in (PAN_SSMBR, PAN_SSMBR + 2):
                            act.wait_ge(sem("glu_used"), 4)
                        else:
                            act.wait_ge(drained[1], (p - 3) // 2 + 1)
                        A(rows(tg[:, (p - PAN_SSMBR) // 2 % 2, :]), pair(0), ACT.Tanh, scale=0.5).then_inc(drained[0], 1)
                elif p < PAN_GLU:
                    kind, g, hc = qkv_panel(p)
                    if p == PAN_QKV:
                        act.wait_ge(sem("y_formed"), 4)
                    if kind == 2 and hc == 1 and g == 0:
                        act.wait_ge(sem("v_turned"), NT)
                        act.wait_ge(sem("decode_kept"), 3)
                    dst = (q_t[:, hc, g, :], k_t[:, hc, g, :], v_t[:, g, :])[kind]
                    A(rows(dst), pair(p % 2), ACT.Copy).then_inc(drained[p % 2], 1)
                else:
                    n = p - PAN_GLU
                    if n >= 2:
                        act.wait_ge(sem("glu_used"), n - 1)
                    A(rows(tg[:, n % 2, :]), pair(p % 2), ACT.Tanh, scale=0.5).then_inc(drained[p % 2], 1)

            def expand(ct):
                act.wait_ge(sem("powers_done"), ct + 1)
                if ct >= 1:
                    act.wait_ge(sem("k_formed"), ct)
                if ct >= 2:
                    act.wait_ge(sem("y_formed"), ct - 1)
                for g in range(2):
                    r = slice(64 * g, 64 * g + 64)
                    A(bp[r].rearrange("p n q k c -> p (n q) k c")[:, :, :, 16 * g:16 * g + 16],
                      bpc[r].rearrange("p k n q c -> p (n q) k c"), ACT.Copy)
                    ins = A(cp[ct % 2][r].rearrange("p k n q c -> p (k n q) c")[:, :, 16 * g:16 * g + 16],
                            cpc[r].rearrange("p k n q c -> p (k n q) c"), ACT.Copy)
                ins.then_inc(sem("spread"), 1)

            def ssm_prep(ct):
                act.wait_ge(sem("bt_turned"), ct + 1)
                for n in range(2):
                    for half in range(2):
                        ins = A(bt[n][:, 2 * half:2 * half + 2, :, :].rearrange("p q k c -> p (q k c)"),
                                ps[:, 4 + 2 * n + half, :], ACT.Copy)
                ins.then_inc(sem("bt_copied"), 1)

            def ssm_in(ct):
                act.wait_ge(sem("v_formed"), ct + 1)
                if ct >= 1:
                    act.wait_ge(sem("h_done"), ct)
                A(vsb[:, :, :].rearrange("p (b q) c -> p b (q c)", b=2), ps[:, 6:8, 0:288], ACT.Copy).then_inc(sem("v_copied"), 1)

            def ssm_out(ct):
                act.wait_ge(sem("state_turned"), ct + 1)
                if ct >= 1:
                    act.wait_ge(sem(f"state_sent{ct - 1}"), 64)
                A(st_out[:, :, :], ps[0:36, 6, 0:256].rearrange("p (n c) -> p n c", n=2), ACT.Copy).then_inc(sem("state_staged"), 1)

            def gelu(ct):
                act.wait_ge(sem("g_in"), ct + 1)
                A(t2_row, t1_row, ACT.Tanh, scale=math.sqrt(2 / math.pi)).then_inc(sem("g_tanh"), 1)

            def high_rows(dst, ct, scale):
                A(dst[:, ct, 0:SEQ].rearrange("p (c s) -> p c s", s=CH),
                  u_ssm[:, ct, 0:SEQ].rearrange("p (s c) -> p c s", s=CH), ACT.Copy, scale=scale)
                return A(dst[:, ct, SEQ:T], u_ssm[:, ct, SEQ:T], ACT.Copy, scale=scale)

            def gelu_split():
                act.wait_ge(sem("gelu_done"), 4)
                act.wait_ge(sem("y_formed"), 4)
                for ct in range(4):
                    high_rows(ys_hi, ct, 0.5).then_inc(sem("gelu_high"), 1)

            def pool_old():
                act.wait_ge(sem("pool_turned"), 1)
                A(stage_dec[0:PBUF + DEC, :], ps[0:PBUF + DEC, 5, :], ACT.Copy).then_inc(sem("pool_staged"), 1)

            def pool_mix():
                for g in range(4):
                    act.wait_ge(sem("pool_scaled"), g + 1)
                    A(yp_hi[:, g, :], tw[:, g % 2, :], ACT.Copy).then_inc(sem("pool_high"), 1)

            def v_tokens(hc, i):
                act.wait_ge(sem("v_turned"), NT * hc + i + 1)
                A(v_tok[:, i, :, P * hc:P * hc + P], ps[:, 4 + i, 0:384].rearrange("p (g c) -> p g c", g=3),
                  ACT.Copy).then_inc(sem("v_tokens"), 1)

            def k_tokens(hc, i):
                act.wait_ge(sem("k_turned"), NT * hc + i + 1)
                if hc == 1 and i == 0:
                    act.wait_ge(sem("k_tokens_sent0"), 16 * 9)
                g0 = 0 if i == NT - 1 else 1
                A(k_tok[:, i, g0:3, :], ps[:, 4 + i, P * g0:384].rearrange("p (g c) -> p g c", c=P),
                  ACT.Copy).then_inc(sem("k_tokens"), 1)

            def decode_rep(n):
                act.wait_ge(sem("rep_turned"), n + 1)
                b = 4 + 2 * (n % 2)
                A(reps[n][:, 0:2, :], ps[0:32, b, :].rearrange("p (g c) -> p g c", g=2), ACT.Copy)
                A(reps[n][:, 2, :], ps[0:32, b + 1, 0:256], ACT.Copy).then_inc(sem("reps_done"), 1)

            def decode_softmax():
                act.wait_ge(sem("s32_done"), 1)
                A(sc32[:, 0:291], sc32[:, 0:291], ACT.Exp, bias=small[0:32, 1:2], scale=0.125,
                  accum_out=small[0:32, 2:3]).then_inc(sem("e32_done"), 1)
                act.wait_ge(sem("p_turned"), 1)
                A(pt32[:, 0:2, :], ps[:, 5, 0:64].rearrange("p (g c) -> p g c", g=2), ACT.Copy)
                A(pt32[0:32, 2, :], ps[0:32, 5, 64:96], ACT.Copy).then_inc(sem("p_copied"), 1)

            def decode_out():
                act.wait_ge(sem("cache_summed"), 3)
                for h in range(2):
                    r = slice(64 * h, 64 * h + 64)
                    ins = A(ya_hi[r, :, SEQ:T], ps[r, 6:8, 0:16].rearrange("p c (b h) -> p c b h", h=2)[:, :, :, h], ACT.Copy)
                ins.then_inc(sem("od_high"), 1)

            def exp(n):
                act.wait_ge(sem("max_done"), n + 1)
                cols = P * sum(len(quad) for quad in quads_of(n))
                A(sc[:, n % 2, 0:cols], sc[:, n % 2, 0:cols], ACT.Exp, bias=small[:, 8 + n % 2:9 + n % 2], scale=0.125,
                  accum_out=small[:, 10 + n % 2:11 + n % 2]).then_inc(sem("exp_done"), 1)

            def probs(n, m):
                h, i = ATT_STEPS[n]
                quads = quads_of(n)
                turned = sum(len(quads_of(j)) for j in range(n)) + m
                if m < len(quads):
                    k = len(quads[m])
                    act.wait_ge(sem("pt_turned"), turned + 1)
                    if turned >= 2:
                        act.wait_ge(sem("pt_used"), turned - 1)
                    A(ptr[:, turned % 2, 0:P * k], ps[:, 7, 0:P * k], ACT.Copy).then_inc(sem("pt_copied"), 1)
                else:
                    act.wait_ge(sem("pt_used"), turned)
                    r = slice(64 * (h % 2), 64 * (h % 2) + 64)
                    A(ya_hi[r, h // 2, P * i:P * i + P], ps[r, 6, 0:P], ACT.Copy).then_inc(sem("o_high"), 1)

            t1_row = tw[:, 0, :]
            t2_row = tw[:, 1, :]

            todo = {"expand": expand, "ssm_prep": ssm_prep, "ssm_in": ssm_in, "ssm_out": ssm_out,
                    "v_tokens": v_tokens, "k_tokens": k_tokens, "exp": exp, "probs": probs, "gelu": gelu, "params": params, "pool_old": pool_old, "pool_mix": pool_mix,
                    "gelu_split": gelu_split, "decode_rep": decode_rep, "decode_softmax": lambda _: decode_softmax(),
                    "decode_out": lambda _: decode_out()}

            def run(step):
                name, args = (step[0], step[1:]) if isinstance(step, tuple) else (step, ())
                if name in todo:
                    todo[name](*args)

            for step in AFTER[-1]:
                run(step)
            for p in range(PAN_OUT):
                hi_static(p + LOOK)
                for k in range(panel_blocks(p)):
                    for step in INNER.get((p, k), []):
                        run(step)
                evacuate(p)
                if p >= PAN_ATTB:
                    for n in range(4 * (p - PAN_ATTB), 4 * (p - PAN_ATTB) + 4):
                        act.wait_ge(sem("m_summed"), n + 1)
                        A(m_hi[:, n, :], z[:, n, :], ACT.Copy, scale=0.5).then_inc(sem("m_high"), 1)
                for step in AFTER.get(p, []):
                    run(step)
                if p == PAN_SSMBR - 1:
                    for ct in range(4):
                        act.wait_ge(sem("glu_used"), 4)
                        high_rows(ys_hi, ct, 0.25).then_inc(sem("ys_high"), 1)

            def square(c):
                act.wait_ge(sem("centred"), c + 1)
                if c >= 2:
                    act.wait_ge(sem("square_used"), c - 1)
                A(lnr[:, L_SQ + c % 2, :], z[:, c, :], ACT.Square).then_inc(sem("squared"), 1)

            for c in range(KD):
                hi_static(PAN_OUT + c + LOOK)
                if c == 4:
                    for n in range(4):
                        square(n)
                if c > 4:
                    square(c - 1)
            square(KD - 1)
            act.wait_ge(drained[3], 1)
            A(lnr[:, L_SQ, :], lnr[:, L_RSTD, :], ACT.Sqrt, bias=small[:, 48:49]).then_inc(sem("std_done"), 1)

            def offset(c):
                if c == 0:
                    act.wait_ge(sem("offset_done"), 1)
                else:
                    act.wait_ge(sem("x1_full"), c - 1)
                A(lnr[:, L_SQ + c % 2, :], lnr[:, L_OFF, :], ACT.Identity, bias=ln1b[:, c:c + 1],
                  scale=ln1g[:, c:c + 1]).then_inc(sem("offset_row"), 1)

            offset(0)
            for c in range(KD):
                if c + 1 < KD:
                    offset(c + 1)
                act.wait_ge(sem("x1_full"), c + 1)
                A(x_hi[:, c, :], z[:, c, :], ACT.Copy).then_inc(sem("x1_high"), 1)

            def ff_turn(i, looks):
                for j in range(4):
                    if looks is None:
                        q = PAN_FF + j + LOOK
                        hi(q % RING, q % RAW, 8, None, i * 32 + 16 * (q // RAW + 1), i * 4 + (q - RING + 1))
                    else:
                        hi_static(looks + j + LOOK)
                    act.wait_ge(panel_done, i * 4 + (PAN_FF + j + 1))
                    if j % 2 == 0:
                        A(rows(tg[:, j // 2, :]), pair(j), ACT.Tanh, scale=0.5).then_inc(sem("f_tanh"), 1)
                    else:
                        act.wait_ge(drained[j], i * 1 + ((READ_FF if j == 1 else FF_READS) + 1))
                        A(f_hi[:, bass.ds(i * 2 + j // 2, 1), :], tw[:, bass.ds(j // 2, 1), :], ACT.Copy,
                          scale=0.5).then_inc(sem("f_high"), 1)

            with act.Fori(0, KF // 2 - 1) as i:
                ff_turn(i, None)
            ff_turn(KF // 2 - 1, PAN_DOWN - 4)

            def to_rows(o, output):
                act.wait_ge(sem("z_turned"), output)
                c = bass.ds(output * P - P, P)
                A(ztok[:, :, c], ps[:, 4 + 2 * o, :].rearrange("p (t c) -> p t c", t=NT), ACT.Copy)
                A(zdec[:, c], ps[0:DEC, 5 + 2 * o, 0:P], ACT.Copy).then_inc(drained[2 + o], 1)

            def down_turn(i, first, looks):
                for j in range(8):
                    if looks is None:
                        q = PAN_DOWN + j + LOOK
                        hi(q % RING, q % RAW, panel_blocks(q), None, i * 64 + 16 * (q // RAW + 1), i * 8 + (q - RING + 1))
                    else:
                        hi_static(looks + j + LOOK)
                    if j == 5:
                        to_rows(0, i * 2 + 1)
                    if j == 1 and not first:
                        to_rows(1, i * 2)

            down_turn(0, True, PAN_DOWN)
            with act.Fori(1, KD // 2 - 1) as i:
                down_turn(i, False, None)
            down_turn(KD // 2 - 1, False, PAN_END - 8)
            to_rows(1, KD)
            act.wait_ge(sem("var2_done"), 1)
            A(rn[:, 0, :], mv[:, :, 1], ACT.Sqrt, bias=small[:, 48:49]).then_inc(sem("std2_done"), 1)
            act.wait_ge(sem("rstd2_done"), 1)
            for t in range(NT + 1):
                row, n = (ztok[:, t, :], P) if t < NT else (zdec[:, :], DEC)
                A(row, row, ACT.Identity, bias=rn[0:n, 1, t:t + 1], scale=rn[0:n, 0, t:t + 1]).then_inc(sem("y_normed"), 1)

        @block.vector
        def _(dve):
            V = nc.vector
            count = [0]
            told = {}

            def link(ins):
                count[0] += 1
                ins.then_inc(sem("dve_seq"), 1)
                dve.wait_ge(sem("dve_seq"), count[0])

            def tell(ins, name):
                told[name] = told.get(name, 0) + 1
                ins.then_inc(sem(name), 1)
                dve.wait_ge(sem(name), told[name])

            def cmul(out_r, out_i, a, s_r, s_i, conj, u, w, part):
                tt = V.tensor_tensor
                tt(u, a, s_r, ALU.mult)
                link(tt(w, a, s_i, ALU.mult))
                tt(out_r, part(u, 0), part(w, 1), ALU.add if conj else ALU.subtract)
                link(tt(out_i, part(u, 1), part(w, 0), ALU.subtract if conj else ALU.add))

            for i in range(NT):
                dve.wait_ge(sem("x_high"), i + 1)
                tell(V.tensor_tensor(x_lo[:, :, P * i:P * i + P], ps[:, 2 * i:2 * i + 2, :].rearrange("p b (c t) -> p (b c) t", t=P),
                                     x_hi[:, :, P * i:P * i + P].bitcast(F32), ALU.subtract), "x_split")
            dve.wait_ge(sem("x_high"), NT + 1)
            tell(V.tensor_tensor(x_lo[:, :, SEQ:T], ps[:, 0, 0:DEC * KD].rearrange("p (c b) -> p c b", b=DEC),
                                 x_hi[:, :, SEQ:T].bitcast(F32), ALU.subtract), "x_split")

            LR, LI, ST, MAG, RED, RHALF, SIN, SHALF = range(8)
            (TMP, TMP2, TMP3, COS, LBR, LBI, CFR, CFI, L2R, L2I, L4R, L4I, L8R, L8I, PR, PI, A8, TH, KI, NUM, NUM2,
             W1, W2, W3, W4) = range(8, 33)

            def v(n):
                return par[:, n, :]

            dve.wait_ge(par_in, 16 * N_PAR)
            tell(V.tensor_copy(lrow[:, 2, :].rearrange("a (g p) -> a g p", g=2),
                               srow[:, :].unsqueeze(2).broadcast_to([16, 2, E])), "steps_spread")

            def turn_params():
                dve.wait_ge(sem("lam_turned"), 1)
                tell(V.tensor_copy(par[:, 0:3, :], ps[:, 4, 0:48].rearrange("p (n a) -> p n a", n=3)), "par_read")
                dve.wait_ge(sem("c_turned"), 1)
                for n in range(2):
                    src = ps[:, 5 + n, :].rearrange("p (a g h) -> p a g h", g=2, h=16)
                    for g in range(2):
                        r = slice(64 * g, 64 * g + 64)
                        ins = V.tensor_scalar(cc[r, n, :, :], src[r, :, g, :], (1.0, -1.0)[n], None, ALU.mult)
                        if n == 1 and g == 1:
                            tell(ins, "par_read")
                        else:
                            link(ins)
                dve.wait_ge(sem("h0_turned"), 1)
                tell(V.tensor_copy(h0[:, :, :, :], ps[:, 7, 0:256].rearrange("p (n b a) -> p n b a", n=2, b=DEC)), "par_read")

            def cmul_par(out, a, b, conj):
                s_r, s_i = (v(b + n).unsqueeze(1).broadcast_to([P, 2, 16]) for n in range(2))
                cmul(v(out), v(out + 1), par[:, a:a + 2, :], s_r, s_i, conj, par[:, W1:W1 + 2, :], par[:, W3:W3 + 2, :],
                     lambda x, n: x[:, n, :])

            def params():
                def ts(out, a, s1, s2, o1, o2):
                    link(V.tensor_scalar(v(out), v(a), s1, s2, o1, o2))

                def tt(out, a, b, op):
                    link(V.tensor_tensor(v(out), v(a), v(b), op))

                def stt(out, a, s, b, o1, o2):
                    link(V.scalar_tensor_tensor(v(out), v(a), s, v(b), o1, o2))

                def exp(out, a):
                    ts(a, a, -87.0, 88.0, ALU.max, ALU.min)
                    ts(TMP, a, math.log2(math.e), ROUND, ALU.mult, ALU.add)
                    ts(TMP, TMP, -ROUND, None, ALU.add, ALU.bypass)
                    stt(TMP2, TMP, -0.693359375, a, ALU.mult, ALU.add)
                    stt(TMP2, TMP, 2.12194440e-4, TMP2, ALU.mult, ALU.add)
                    ts(TMP3, TMP2, 1 / 5040.0, None, ALU.mult, ALU.bypass)
                    for f in (720.0, 120.0, 24.0, 6.0, 2.0, 1.0):
                        stt(TMP3, TMP3, 1 / f, TMP2, ALU.add, ALU.mult)
                    link(V.tensor_scalar(v(KI).bitcast(I32), v(TMP), 127.0, 2.0 ** 23, ALU.add, ALU.mult))
                    stt(out, TMP3, 1.0, KI, ALU.add, ALU.mult)

                exp(ST, ST)
                tt(MAG, LR, ST, ALU.mult)
                exp(MAG, MAG)
                tt(TH, LI, ST, ALU.mult)
                ts(TMP, TH, 1 / (2 * math.pi), ROUND, ALU.mult, ALU.add)
                ts(TMP, TMP, -ROUND, None, ALU.add, ALU.bypass)
                c1 = 6.28125
                c2 = float((np.float32(2 * math.pi - c1).view(np.uint32) & np.uint32(0xFFFFF000)).view(np.float32))
                c3 = 2 * math.pi - c1 - c2
                stt(RED, TMP, -c1, TH, ALU.mult, ALU.add)
                stt(RED, TMP, -c2, RED, ALU.mult, ALU.add)
                stt(RED, TMP, -c3, RED, ALU.mult, ALU.add)
                ts(RHALF, RED, 0.5, None, ALU.mult, ALU.bypass)
                tell(V.tensor_scalar(v(RED), v(RED), 3.1415925, -3.1415925, ALU.min, ALU.max), "angle_done")
                dve.wait_ge(sem("sin_done"), 2)
                tt(TMP, SHALF, SHALF, ALU.mult)
                ts(COS, TMP, -2.0, 1.0, ALU.mult, ALU.add)
                tt(LBR, MAG, COS, ALU.mult)
                tt(LBI, MAG, SIN, ALU.mult)
                ts(NUM, LBR, -1.0, None, ALU.add, ALU.bypass)
                link(V.tensor_copy(v(NUM2), v(LBI)))
                cmul_par(CFR, NUM, LR, True)
                tt(TMP, LR, LR, ALU.mult)
                tt(TMP2, LI, LI, ALU.mult)
                tt(TMP, TMP, TMP2, ALU.add)
                link(V.reciprocal(v(TMP), v(TMP)))
                tt(CFR, CFR, TMP, ALU.mult)
                tt(CFI, CFI, TMP, ALU.mult)
                for a, b in ((LBR, L2R), (L2R, L4R), (L4R, L8R)):
                    cmul_par(b, a, a, False)
                for a, b in ((MAG, A8), (A8, A8), (A8, A8)):
                    tt(b, a, a, ALU.mult)
                link(V.tensor_copy(v(PR), v(COS)))
                link(V.tensor_copy(v(PI), v(SIN)))
                for _ in range(3):
                    unit_square()
                cf = [v(n).unsqueeze(1).unsqueeze(3).broadcast_to([P, 2, 16, 16]) for n in (CFR, CFI)]
                w1, w2 = (x[:, 0:512].rearrange("p (n a h) -> p n a h", n=2, a=16) for x in (t1, t2))
                cmul(bbar[:, 0, :, :], bbar[:, 1, :, :], braw[:, :, :, :], cf[0], cf[1], False, w1, w2, lambda x, n: x[:, n])
                for m in range(2):
                    V.memset(kbd[m][:, :, :], 0.0)
                    V.memset(cp[m][:, :, :, :, :], 0.0)
                V.memset(bp[:, :, :, :, :], 0.0)
                tell(V.memset(ust[0][:, :, 1, NC:], 0.0), "stack_zeros")
                tell(V.memset(ust[2][:, :, 1, NC:], 0.0), "stack_zeros")
                link(V.memset(hst[:, :, :, 0:1], 0.0))

            def unit_square():
                def tt(out, a, b, op):
                    link(V.tensor_tensor(v(out), v(a), v(b), op))
                both = par[:, PR:PR + 2, :]
                V.tensor_tensor(par[:, TMP:TMP + 2, :], both, both, ALU.mult)
                tt(TMP3, PR, PI, ALU.mult)
                V.tensor_tensor(v(PR), v(TMP), v(TMP2), ALU.subtract)
                link(V.tensor_scalar(v(PI), v(TMP3), 2.0, None, ALU.mult))
                link(V.tensor_tensor(par[:, TMP:TMP + 2, :], both, both, ALU.mult))
                tt(TMP, TMP, TMP2, ALU.add)
                link(V.tensor_scalar(v(TMP), v(TMP), -0.5, 1.5, ALU.mult, ALU.add))
                link(V.tensor_tensor(both, both, v(TMP).unsqueeze(1).broadcast_to([P, 2, 16]), ALU.mult))

            def powers(ct):
                aq = slice(4 * ct, 4 * ct + 4)
                if ct == 0:
                    for k in range(6):
                        link(V.tensor_copy(rotk[:, k, :, :], par[:, PR:PR + 2, :]))
                        if k < 5:
                            unit_square()
                else:
                    dve.wait_ge(sem("spread"), ct)
                V.tensor_copy(bpc[:, 0, :, :, :], bbar[:, :, aq, :])
                link(V.tensor_copy(cpc[:, 0, :, :, :], cc[:, :, aq, :]))
                for a, conj, top in ((bpc, False, CH), (cpc, True, CH + 1)):
                    for k, name in ((1, LBR), (2, L2R), (4, L4R), (8, L8R)):
                        if k >= top:
                            continue
                        c = min(k, top - k)
                        w1, w2 = (x[:, 0:128 * c].rearrange("p (k q c) -> p k q c", q=4, c=16) for x in (t1, t2))
                        s_r, s_i = (par[:, L, aq].unsqueeze(1).unsqueeze(3).broadcast_to([P, 2 * c, 4, 16])
                                    for L in (name, name + 1))
                        cmul(a[:, k:k + c, 0], a[:, k:k + c, 1], a[:, 0:c].rearrange("p k n q c -> p (k n) q c"), s_r, s_i,
                             conj, w1, w2, lambda x, n: x.rearrange("p (k n) q c -> p k n q c", n=2)[:, :, n])
                e = ein[ct % 2]
                V.memset(e[:, 0, :, 0:1], 1.0)
                link(V.memset(e[:, 1, :, 0:1], 0.0))
                for k in range(6):
                    c = 1 << k
                    s_r, s_i = (rotk[:, k, n, aq].unsqueeze(1).unsqueeze(3).broadcast_to([P, 2, 4, c]) for n in range(2))
                    w1, w2 = (x[:, 0:8 * c].rearrange("p (n q c) -> p n q c", n=2, q=4) for x in (t1, t2))
                    cmul(e[:, 0, :, c:2 * c], e[:, 1, :, c:2 * c], e[:, :, :, 0:c], s_r, s_i, False, w1, w2,
                         lambda x, n: x[:, n])
                link(V.tensor_copy(dec0[ct % 2][:, :, :], v(A8)[:, aq].unsqueeze(2).broadcast_to([P, 4, NC])))
                tell(V.memset(dec0[ct % 2][:, :, 0:1], 0.0), "powers_done")

            def ssm_prep(ct):
                dve.wait_ge(sem("k_formed"), ct + 1)
                for q in range(4):
                    r = slice(32 * q, 32 * q + 32)
                    ins = V.tensor_copy(kbd[ct % 2][r, :, 32 * q:32 * q + 32],
                                        ps[r, 4, 0:256].rearrange("p (j c) -> p j c", j=CH))
                    if q < 3:
                        link(ins)
                    else:
                        tell(ins, "k_copied")

            def scan(ct):
                aq = slice(4 * ct, 4 * ct + 4)
                dve.wait_ge(sem("v_copied"), ct + 1)
                if ct >= 1:
                    dve.wait_ge(sem("state_turned"), ct)
                w1, w2 = (x[:, 0:8 * NC].rearrange("p (n q c) -> p n q c", n=2, q=4) for x in (t1, t2))
                e_r, e_i = (ein[ct % 2][:, n, :, :].unsqueeze(1).broadcast_to([P, 2, 4, NC]) for n in range(2))

                def part(x, n):
                    return x[:, n]

                both = vsb[:, :, :].rearrange("p q (n c) -> p n q c", n=2)
                cmul(wrot[:, 0], wrot[:, 1], both[:, :, :, 0:NC], e_r, e_i, True, w1, w2, part)
                d0 = dec0[ct % 2][:, :, :].rearrange("p q c -> p (q c)")
                for n in range(2):
                    link(V.tensor_tensor_scan(grot[:, n, :, :].rearrange("p q c -> p (q c)"), d0,
                                              wrot[:, n, :, :].rearrange("p q c -> p (q c)"), 0.0, ALU.mult, ALU.add))
                cmul(hst[:, 0, :, 1:65], hst[:, 1, :, 1:65], grot[:, :, :, :], e_r, e_i, False, w1, w2, part)
                for n in range(2):
                    L = (LBR, LBI)[n]
                    d = (t1, t2)[n][:, 0:64].rearrange("p (n b q) -> p n b q", n=2, q=4)
                    ins = V.tensor_tensor(d, h0[:, :, :, aq],
                                          par[:, L, aq].unsqueeze(1).unsqueeze(1).broadcast_to([P, 2, DEC, 4]), ALU.mult)
                link(ins)
                u, w = (x[:, 0:64].rearrange("p (n b q) -> p n q b", n=2, q=4) for x in (t1, t2))
                V.tensor_tensor(hst[:, 0, :, 65:73], u[:, 0], w[:, 1], ALU.subtract)
                link(V.tensor_tensor(hst[:, 1, :, 65:73], u[:, 1], w[:, 0], ALU.add))
                link(V.tensor_tensor(hst[:, 0, :, 65:73], hst[:, 0, :, 65:73], vsb[:, :, 64:72], ALU.add))
                link(V.tensor_tensor(hst[:, 1, :, 65:73], hst[:, 1, :, 65:73], vsb[:, :, 136:144], ALU.add))
                tell(V.tensor_copy(hfin[:, :, :].rearrange("p n (j q) -> p n q j", q=4), hst[:, :, :, 64:73]), "h_done")

            def ssm_out(ct):
                dve.wait_ge(sem("y_formed"), ct + 1)
                link(V.scalar_tensor_tensor(u_ssm[:, ct, 0:SEQ], u_ssm[:, ct, 0:SEQ], dskip[:, ct:ct + 1], ps[:, 4, :],
                                            ALU.mult, ALU.add))
                tell(V.scalar_tensor_tensor(u_ssm[:, ct, SEQ:T], u_ssm[:, ct, SEQ:T], dskip[:, ct:ct + 1],
                                            ps[:, 5, 0:DEC], ALU.mult, ALU.add), "y_read")

            def gelu(ct):
                u, a = u_ssm[:, ct, :], tw[:, 0, :]
                link(V.tensor_tensor(a, u, u, ALU.mult))
                link(V.tensor_scalar(a, a, 0.044715, 1.0, ALU.mult, ALU.add))
                tell(V.tensor_tensor(a, a, u, ALU.mult), "g_in")
                dve.wait_ge(sem("g_tanh"), ct + 1)
                tell(V.scalar_tensor_tensor(u, tw[:, 1, :], 1.0, u, ALU.add, ALU.mult), "gelu_done")

            def low_rows(dst, high, ct, scale, name):
                link(V.scalar_tensor_tensor(dst[:, ct, 0:SEQ].rearrange("p (c s) -> p c s", s=CH),
                                            u_ssm[:, ct, 0:SEQ].rearrange("p (s c) -> p c s", s=CH), scale,
                                            high[:, ct, 0:SEQ].bitcast(F32).rearrange("p (c s) -> p c s", s=CH),
                                            ALU.mult, ALU.subtract))
                tell(V.scalar_tensor_tensor(dst[:, ct, SEQ:T], u_ssm[:, ct, SEQ:T], scale,
                                            high[:, ct, SEQ:T].bitcast(F32), ALU.mult, ALU.subtract), name)

            def gelu_split():
                for ct in range(4):
                    dve.wait_ge(sem("gelu_high"), ct + 1)
                    low_rows(ys_lo, ys_hi, ct, 0.5, "gelu_split_done")

            def pool_old():
                dve.wait_ge(consts, 3)
                dve.wait_ge(vec_in, 16 * N_VEC)
                for g in (3, 2, 1, 0):
                    link(V.tensor_scalar(rcnt[:, g, :], rcnt[:, 0, :], float(POOL_W[g]), None, ALU.min))
                link(V.reciprocal(rcnt[:, :, :], rcnt[:, :, :]))
                dve.wait_ge(drained[(PAN_POOL + 2) % 2], (PAN_POOL + 2) // 2 + 1)
                dve.wait_ge(drained[(PAN_POOL + 3) % 2], (PAN_POOL + 3) // 2 + 1)
                link(V.memset(upool[:, :, 0:16], 0.0))
                dve.wait_ge(sem("psum_old"), 1)
                tell(V.tensor_copy(oldsum[:, :, :], ps[:, 4, 0:32].rearrange("p (g b) -> p g b", g=4)), "psum_old_read")
                tell(V.memset(ust[1][:, :, 1, NC:], 0.0), "stack_zeros")

            def pool_diff():
                dve.wait_ge(sem("pool_turned"), 1)
                for g, w in enumerate(POOL_W):
                    src = upool[:, g, 0:16 + SEQ]
                    n, size = 1, SEQ + 16
                    bufs = wide
                    cur, turn = src, 0
                    while n < w:
                        out = bufs[turn]
                        link(V.tensor_tensor(out[:, 2 * n - 1:size], cur[:, 2 * n - 1:size], cur[:, n - 1:size - n], ALU.add))
                        cur, turn, n = out, 1 - turn, 2 * n
                    tot = cur[:, 16:16 + SEQ]
                    link(V.tensor_tensor(small[:, 16:32], tot[:, 0:16], rcnt[:, g, :], ALU.mult))
                    link(V.tensor_tensor(oldsum[:, g, :], oldsum[:, g, :], upool[:, g, 16 + SEQ:16 + T], ALU.add))
                    link(V.scalar_tensor_tensor(upool[:, g, 16 + SEQ:16 + T], oldsum[:, g, :], 1.0 / w,
                                                upool[:, g, 16 + SEQ:16 + T], ALU.mult, ALU.subtract))
                    link(V.scalar_tensor_tensor(upool[:, g, 32:16 + SEQ], tot[:, 16:SEQ], 1.0 / w,
                                                upool[:, g, 32:16 + SEQ], ALU.mult, ALU.subtract))
                    tell(V.tensor_tensor(upool[:, g, 16:32], small[:, 16:32], upool[:, g, 16:32], ALU.subtract), "diff_done")

            def pool_mix():
                for g in range(4):
                    dve.wait_ge(sem("pool_mixed"), g + 1)
                    tell(V.tensor_scalar(rows(tw[:, g % 2, :]), pair(2 + g % 2), pscale[:, g:g + 1], None, ALU.mult),
                         "pool_scaled")
                    dve.wait_ge(sem("pool_high"), g + 1)
                    tell(V.tensor_tensor(yp_lo[:, g, :], tw[:, g % 2, :], yp_hi[:, g, :].bitcast(F32), ALU.subtract), "pool_split")


            def v_tokens(hc, i):
                if i < NT - 1:
                    return
                dve.wait_ge(sem("v_turned"), NT * (hc + 1))
                for n, src in enumerate((q_t[:, hc, :, SEQ:T], k_t[:, hc, :, SEQ:T], v_t[:, :, SEQ:T])):
                    tell(V.tensor_copy(dexp[:, n, hc, :, :].rearrange("p g (b h) -> p g b h", h=4),
                                       src.unsqueeze(3).broadcast_to([P, 3, DEC, 4])), "decode_kept")

            def decode_consts():
                rep = ident[0:32, 0:32].rearrange("p (b h) -> p h b", h=4)
                link(V.tensor_reduce(small[0:32, 4:8], rep, AX.X, ALU.add))
                link(V.tensor_copy(hmask[:, :, :], small[0:32, 4:8].unsqueeze(2).broadcast_to([32, 4, E])))
                for g in range(N_GROUPS):
                    for h in range(HEADS):
                        link(V.memset(small[0:32, 32 + 4 * g + h:33 + 4 * g + h], -8.0 * SLOPE[g][h]))
                for g in range(N_GROUPS):
                    link(V.tensor_tensor(small[0:32, 12:16], small[0:32, 4:8], small[0:32, 32 + 4 * g:36 + 4 * g], ALU.mult))
                    link(V.tensor_reduce(small[0:32, 44 + g:45 + g], small[0:32, 12:16], AX.X, ALU.add))

            def decode_own(_):
                dve.wait_ge(sem("reps_done"), 3)
                for g in range(N_GROUPS):
                    w1 = tw[0:32, 0, 0:256]
                    link(V.tensor_tensor(w1, reps[0][:, g, :], reps[1][:, g, :], ALU.mult))
                    link(V.tensor_tensor(w1, w1, hmask[:, :, :].rearrange("p h e -> p (h e)"), ALU.mult))
                    link(V.tensor_reduce(sc32[:, 288 + g:289 + g], w1, AX.X, ALU.add))

            def decode_spread(n):
                g, b2 = n // 4, n % 4
                keys = P if g < 2 else 32
                buf = cbuf[g]
                if b2 == 0:
                    dve.wait_ge(sem(f"cache_in{g}"), 16)
                dve.wait_ge(sem("q_spread"), n + 1)
                tell(V.tensor_tensor(buf[0:keys, 2 * b2:2 * b2 + 2, :], buf[0:keys, 2 * b2:2 * b2 + 2, :],
                                     ps[0:keys, 4 + n % 4, :].rearrange("p (b c) -> p b c", b=2), ALU.mult), "qk_read")
                if b2 == 3:
                    tell(V.tensor_reduce(s32[0:keys, g, :], buf[0:keys, :, :].rearrange("p b (h e) -> p (b h) e", h=4),
                                         AX.X, ALU.add), "cache_scored")

            def decode_scores():
                dve.wait_ge(sem("s_turned"), 1)
                for g in range(N_GROUPS):
                    keys = P if g < 2 else 32
                    c = slice(P * g, P * g + keys)
                    link(V.scalar_tensor_tensor(sc32[:, c], dist32[:, c], small[0:32, 44 + g:45 + g], ps[0:32, 4, c],
                                                ALU.mult, ALU.add))

            def decode_softmax():
                link(V.reduce_max(small[0:32, 0:1], sc32[:, 0:291], AX.X))
                tell(V.tensor_scalar(small[0:32, 1:2], small[0:32, 0:1], -0.125, None, ALU.mult), "s32_done")
                dve.wait_ge(sem("e32_done"), 1)
                link(V.reciprocal(small[0:32, 3:4], small[0:32, 2:3]))
                tell(V.tensor_scalar(sc32[:, 0:291], sc32[:, 0:291], small[0:32, 3:4], None, ALU.mult), "p_done")
                for g in range(N_GROUPS):
                    ins = V.tensor_scalar(diag32[:, g, :], ident[0:32, 0:32], sc32[:, 288 + g:289 + g], None, ALU.mult)
                ins.then_inc(sem("diag_done"), 1)

            def decode_out():
                dve.wait_ge(sem("od_high"), 1)
                for h in range(2):
                    r = slice(64 * h, 64 * h + 64)
                    ins = V.tensor_tensor(ya_lo[r, :, SEQ:T], ps[r, 6:8, 0:16].rearrange("p c (b h) -> p c b h", h=2)[:, :, :, h],
                                          ya_hi[r, :, SEQ:T].bitcast(F32), ALU.subtract)
                    if h == 0:
                        link(ins)
                    else:
                        tell(ins, "decode_done")

            def bias():
                dve.wait_ge(sem("td_base"), 1)
                for g in (2, 1):
                    m = DILATION[g] - 1
                    w = tw[:, 0, 0:512].bitcast(I32)
                    link(V.tensor_scalar(w, tdi[:, :], m, None, ALU.bitwise_and))
                    link(V.tensor_scalar(tw[:, 1, 0:512], w, 1.0, BIG, ALU.min, ALU.mult))
                    link(V.tensor_tensor(td[:, g, :], tw[:, 1, 0:512], td[:, 1, :], ALU.add))

            def scores(n, g):
                h, i = ATT_STEPS[n]
                col = P * sum(len(keys_of(j, i)) for j in range(g))
                if n >= 2 and g == 0:
                    dve.wait_ge(sem("o_high"), n - 1)
                w = P * len(keys_of(g, i))
                dve.wait_ge(sem("s_formed"), 3 * n + g + 1)
                c0 = 384 + P * (keys_of(g, i)[0] - i)
                tell(V.scalar_tensor_tensor(sc[:, n % 2, col:col + w], td[:, g, c0:c0 + w], -8.0 * SLOPE[g][h],
                                            ps[:, 4 + g % 2, 0:w], ALU.mult, ALU.add), "scored")
                if g == N_GROUPS - 1:
                    link(V.reduce_max(small[:, 12 + n % 2:13 + n % 2], sc[:, n % 2, 0:col + w], AX.X))
                    tell(V.tensor_scalar(small[:, 8 + n % 2:9 + n % 2], small[:, 12 + n % 2:13 + n % 2], -0.125, None,
                                         ALU.mult), "max_done")

            def normalise(n):
                cols = P * sum(len(quad) for quad in quads_of(n))
                dve.wait_ge(sem("exp_done"), n + 1)
                link(V.reciprocal(small[:, 14 + n % 2:15 + n % 2], small[:, 10 + n % 2:11 + n % 2]))
                tell(V.tensor_scalar(sc[:, n % 2, 0:cols], sc[:, n % 2, 0:cols], small[:, 14 + n % 2:15 + n % 2], None,
                                     ALU.mult), "p_normed")

            def probs(n, m):
                if m < len(quads_of(n)):
                    return
                h, i = ATT_STEPS[n]
                r = slice(64 * (h % 2), 64 * (h % 2) + 64)
                dve.wait_ge(sem("o_high"), n + 1)
                tell(V.tensor_tensor(ya_lo[r, h // 2, P * i:P * i + P], ps[r, 6, 0:P],
                                     ya_hi[r, h // 2, P * i:P * i + P].bitcast(F32), ALU.subtract), "o_split")

            def branch(p):
                dve.wait_ge(panel_done, p + 1)
                if p < PAN_QKV:
                    n = p - PAN_POOLB
                    V.scalar_tensor_tensor(rows(z[:, n, :]), rows(z[:, n, :]), 1.0, pair(p % 2), ALU.add, ALU.mult
                                           ).then_inc(drained[p % 2], 1)
                elif p < PAN_ATTG:
                    n = (p - PAN_SSMBR) // 2
                    dve.wait_ge(drained[0], p // 2 + 1)
                    link(V.scalar_tensor_tensor(rows(tw[:, 0, :]), rows(tg[:, n % 2, :]), 1.0, pair(1), ALU.add, ALU.mult))
                    V.tensor_tensor(z[:, n, :], z[:, n, :], tw[:, 0, :], ALU.add).then_inc(drained[1], 1)

            def att_branch(p):
                for n in range(4 * (p - PAN_ATTB), 4 * (p - PAN_ATTB) + 4):
                    b, v = n % 2, OUT_ATTB + n
                    if n % 4 < 3:
                        dve.wait_ge(sem("att_out"), 3 * (p - PAN_ATTB) + n % 4 + 1)
                    else:
                        dve.wait_ge(panel_done, p + 1)
                    V.scalar_tensor_tensor(rows(tw[:, b, :]), rows(tga[:, n, :]), 1.0, pair(b), ALU.add, ALU.mult
                                           ).then_inc(drained[b], 1)
                    dve.wait_ge(drained[b], v // 2 + 1)
                    tell(V.tensor_tensor(z[:, n, :], z[:, n, :], tw[:, b, :], ALU.add), "m_summed")
                    if n > 0:
                        m_low(n - 1)
                    if n == KD - 1:
                        m_low(n)

            def m_low(n):
                dve.wait_ge(sem("m_high"), n + 1)
                V.scalar_tensor_tensor(m_lo[:, n, :], z[:, n, :], 0.5, m_hi[:, n, :].bitcast(F32), ALU.mult,
                                       ALU.subtract).then_inc(sem("m_split"), 1)

            def glu(p):
                n = p - PAN_GLU
                dve.wait_ge(drained[p % 2], p // 2 + 1)
                t = tg[:, n % 2, :]
                link(V.scalar_tensor_tensor(u_ssm[:, n, 0:SEQ].rearrange("p (s c) -> p c s", s=CH),
                                            t[:, 0:SEQ].rearrange("p (c s) -> p c s", s=CH), 1.0,
                                            u_ssm[:, n, 0:SEQ].rearrange("p (s c) -> p c s", s=CH), ALU.add, ALU.mult))
                tell(V.scalar_tensor_tensor(u_ssm[:, n, SEQ:T], t[:, SEQ:T], 1.0, u_ssm[:, n, SEQ:T], ALU.add, ALU.mult),
                     "glu_used")

            todo = {"turn_params": turn_params, "params": params, "powers": powers, "ssm_prep": ssm_prep, "scan": scan,
                    "ssm_out": ssm_out, "gelu": gelu, "gelu_split": gelu_split, "pool_old": pool_old,
                    "pool_diff": pool_diff, "pool_mix": pool_mix, "v_tokens": v_tokens, "decode_consts": decode_consts,
                    "decode_own": decode_own, "decode_spread": decode_spread, "decode_scores": lambda _: decode_scores(),
                    "decode_softmax": lambda _: decode_softmax(), "decode_out": lambda _: decode_out(), "bias": bias,
                    "scores": scores, "normalise": normalise, "probs": probs}

            def run(step):
                name, args = (step[0], step[1:]) if isinstance(step, tuple) else (step, ())
                if name in todo:
                    todo[name](*args)

            for step in AFTER[-1]:
                run(step)
            for p in range(PAN_OUT):
                for k in range(panel_blocks(p)):
                    for step in INNER.get((p, k), []):
                        run(step)
                if PAN_POOLB <= p < PAN_QKV or (PAN_SSMBR <= p < PAN_ATTG and p % 2):
                    branch(p)
                if p >= PAN_ATTB:
                    att_branch(p)
                if PAN_GLU <= p < PAN_SSMBR:
                    glu(p)
                for step in AFTER.get(p, []):
                    run(step)
                if p == PAN_SSMBR - 1:
                    for ct in range(4):
                        dve.wait_ge(sem("ys_high"), ct + 1)
                        low_rows(ys_lo, ys_hi, ct, 0.25, "ys_split")

            stt = V.scalar_tensor_tensor
            acc, accq, shift = lnr[:, L_ACC, :], lnr[:, L_ACCQ, :], lnr[:, L_SHIFT, :]

            def add_square(c):
                dve.wait_ge(sem("squared"), c + 1)
                sq = lnr[:, L_SQ + c % 2, :]
                if c == 0:
                    tell(V.tensor_copy(accq, sq), "square_used")
                else:
                    tell(V.tensor_tensor(accq, accq, sq, ALU.add), "square_used")

            V.memset(small[:, 48:49], EPS)
            for c in range(KD):
                p, b = PAN_OUT + c, (OUT_OUT + c) % 2
                x_c = [x[:, c, :].bitcast(F32) for x in (x_hi, x_lo)]
                if c < 4:
                    if c == 0:
                        dve.wait_ge(sem("m_high"), KD)
                    link(V.tensor_tensor(z[:, c, :], x_c[0], x_c[1], ALU.add))
                    dve.wait_ge(panel_done, p + 1)
                    stt(rows(z[:, c, :]), rows(z[:, c, :]), ALPHA, pair(b), ALU.mult, ALU.add).then_inc(drained[b], 1)
                    dve.wait_ge(drained[b], (OUT_OUT + c) // 2 + 1)
                    if c == 1:
                        link(V.tensor_tensor(acc, z[:, 0, :], z[:, 1, :], ALU.add))
                    elif c == 2:
                        link(V.tensor_tensor(acc, acc, z[:, c, :], ALU.add))
                    elif c == 3:
                        tell(V.tensor_tensor(acc, acc, z[:, c, :], ALU.add), "four_summed")
                        dve.wait_ge(sem("shift_formed"), 1)
                        tell(V.tensor_scalar(rows(shift), pair(2), 1.0 / (4 * P), None, ALU.mult), "shift_read")
                        for n in range(4):
                            tell(V.tensor_tensor(z[:, n, :], z[:, n, :], shift, ALU.subtract), "centred")
                        link(stt(acc, shift, -4.0, acc, ALU.mult, ALU.add))
                        for n in range(4):
                            add_square(n)
                else:
                    link(V.tensor_tensor(z[:, c, :], x_c[0], x_c[1], ALU.add))
                    link(stt(z[:, c, :], z[:, c, :], ALPHA, shift, ALU.mult, ALU.subtract))
                    dve.wait_ge(panel_done, p + 1)
                    tell(V.tensor_tensor(rows(z[:, c, :]), rows(z[:, c, :]), pair(b), ALU.add), "centred")
                    if c < KD - 1:
                        link(V.tensor_tensor(acc, acc, z[:, c, :], ALU.add))
                        add_square(c)
            mean, rstd, off = (lnr[:, n, :] for n in (L_MEAN, L_RSTD, L_OFF))
            dve.wait_ge(sem("sum_done"), 1)
            V.tensor_scalar(rows(mean), pair(2), 1.0 / D, None, ALU.mult).then_inc(drained[2], 1)
            dve.wait_ge(drained[2], 1)
            link(V.tensor_tensor(off, mean, mean, ALU.mult))
            dve.wait_ge(sem("square_summed"), 1)
            stt(rows(rstd), pair(3), 1.0 / D, rows(off), ALU.mult, ALU.subtract).then_inc(drained[3], 1)
            dve.wait_ge(sem("std_done"), 1)
            link(V.reciprocal(rstd, lnr[:, L_SQ, :]))
            tell(stt(off, mean, -1.0, rstd, ALU.mult, ALU.mult), "offset_done")
            for c in range(KD):
                link(stt(z[:, c, :], z[:, c, :], ln1g[:, c:c + 1], rstd, ALU.mult, ALU.mult))
                dve.wait_ge(sem("offset_row"), c + 1)
                tell(V.tensor_tensor(z[:, c, :], z[:, c, :], lnr[:, L_SQ + c % 2, :], ALU.add), "x1_full")

            with dve.Fori(0, KF // 2) as i:
                for j in range(2):
                    c = bass.ds(i * 2 + j, 1)
                    dve.wait_ge(sem("f_tanh"), i * 2 + (j + 1))
                    V.scalar_tensor_tensor(rows(tw[:, j, :]), rows(tg[:, j, :]), 1.0, pair(2 * j), ALU.add, ALU.mult
                                           ).then_inc(drained[2 * j], 1)
                    dve.wait_ge(drained[2 * j], i * 1 + ((READ_FF if j == 0 else FF_READS) + 1))
                    dve.wait_ge(panel_done, i * 4 + (PAN_FF + 2 * j + 2))
                    V.tensor_tensor(rows(tw[:, j, :]), rows(tw[:, j, :]), pair(2 * j + 1), ALU.mult).then_inc(drained[2 * j + 1], 1)
                    dve.wait_ge(sem("f_high"), i * 2 + (j + 1))
                    V.scalar_tensor_tensor(f_lo[:, c, :], tw[:, j:j + 1, :], 0.5, f_hi[:, c, :].bitcast(F32), ALU.mult,
                                           ALU.subtract).then_inc(sem("f_split"), 1)

            def statistics(o, output, read):
                dve.wait_ge(drained[2 + o], read)
                for t in range(NT + 1):
                    row, n = (ztok[:, t, :], P) if t < NT else (zdec[:, :], DEC)
                    ins = V.bn_stats(stats[0:n, t, bass.ds(output - 1, 1), :], row[:, bass.ds(output * P - P, P)])
                return ins

            def down_turn(i, first):
                for o in range(2):
                    if o == 1:
                        statistics(0, i * 2 + 1, i * 1 + (FF_READS + KF // 2 + 1))
                    elif not first:
                        statistics(1, i * 2, i * 1 + (FF_READS + KF // 2))
                    dve.wait_ge(panel_done, i * 8 + (PAN_DOWN + 4 * o + 4))
                    V.scalar_tensor_tensor(rows(tw[:, o, :]), z[:, bass.ds(i * 2 + o, 1), :].rearrange("p o (h t) -> p (o h) t", h=2),
                                           ALPHA, pair(o), ALU.mult, ALU.add).then_inc(drained[o], 1)
                    dve.wait_ge(drained[o], i * 1 + (READ_FF + KF // 2 + 1))

            V.memset(mv[:, :, :], 0.0)
            down_turn(0, True)
            with dve.Fori(1, KD // 2) as i:
                down_turn(i, False)
            link(statistics(1, KD, FF_READS + KF // 2 + KD // 2))
            for t in range(NT + 1):
                n = P if t < NT else DEC
                ins = V.bn_aggr(mv[0:n, t, :], stats[0:n, t, :, :])
            tell(ins, "var2_done")
            dve.wait_ge(sem("std2_done"), 1)
            link(V.reciprocal(rn[:, 0, :], rn[:, 0, :]))
            tell(V.scalar_tensor_tensor(rn[:, 1, :], mv[:, :, 0], -1.0, rn[:, 0, :], ALU.mult, ALU.mult), "rstd2_done")
            dve.wait_ge(sem("gb_in"), 32)
            for t in range(NT + 1):
                row, n = (ztok[:, t, :], P) if t < NT else (zdec[:, :], DEC)
                dve.wait_ge(sem("y_normed"), t + 1)
                tell(V.tensor_tensor(row, row, gb[0:n, 0, :], ALU.mult), "y_scaled")
                if t not in POOL_ADDS:
                    tell(V.tensor_tensor(row, row, gb[0:n, 1, :], ALU.add), "y_added")


FF_READS = 1
N_PAR, N_VEC = 11, 8
_INS = ['x_prompt', 'x_sample', 'cache_k_w128', 'cache_v_w128', 'cache_k_w512', 'cache_v_w512', 'cache_k_w2048',
        'cache_v_w2048', 'state_pool', 'state_ssm_re', 'state_ssm_im', 'w_in', 'pool_w', 'pool_scale',
        'ssm_lambda_re', 'ssm_lambda_im', 'ssm_b_re', 'ssm_b_im', 'ssm_c_re', 'ssm_c_im', 'ssm_d', 'ssm_log_step',
        'ssm_w_glu', 'w_br_att', 'w_br_pool', 'w_br_ssm', 'w_out', 'ln1_g', 'ln1_b', 'ffn_w_gate', 'ffn_w_up',
        'ffn_w_down', 'ln2_g', 'ln2_b']
_OUTS = ([(1, SEQ, D), (DEC, 1, D)] + [(1, 1, min(w, SEQ), HEADS, E) for w in WINDOWS for _ in range(2)]
         + [(1, 1, PBUF, 512), (1, 1, 32, 64), (1, 1, 32, 64)] + [(1, DEC, 1, HEADS, E)] * 6
         + [(1, DEC, 1, 512), (1, DEC, 32, 64), (1, DEC, 32, 64)])


def kernel(**inputs):
    import numpy as _np
    import concourse.bacc as _bacc
    from concourse.bass_utils import run_bass_kernel_spmd as _run

    nc = _bacc.Bacc("TRN2", target_bir_lowering=False, num_devices=1, dynamic_dma_scratch_size=2048)
    arrays, ins, outs = {}, [], []
    for name in _INS:
        a = _np.ascontiguousarray(inputs[name])
        arrays[f"in_{name}"] = a
        ins.append(nc.dram_tensor(f"in_{name}", a.shape, F32, kind="ExternalInput").ap())
    for n, shape in enumerate(_OUTS):
        outs.append(nc.dram_tensor(f"out_{n}", shape, F32, kind="ExternalOutput").ap())
    build(nc, ins, outs)
    r = _run(nc, [arrays], core_ids=[0])
    return tuple(r.results[0][f"out_{n}"] for n in range(len(_OUTS)))
```
